# Optimizing a Trainium2 kernel written in Bass

```python
import math
import jax, jax.numpy as jnp
from jax import lax
import numpy as np

D_MODEL = 1024
BATCH = 1
SEQ = 256
DEPTH = 4

N_MIXERS = 4
N_LAYERS_CONV = (DEPTH + 3) // N_MIXERS
N_LAYERS_RWKV = (DEPTH + 2) // N_MIXERS
N_LAYERS_SGU = (DEPTH + 1) // N_MIXERS
N_LAYERS_RET = DEPTH // N_MIXERS

N_MEM = 256
XA_HEADS = 4
XA_HEAD_DIM = D_MODEL // XA_HEADS

CONV_WIDTH = 31

RWKV_HEAD_DIM = 64
RWKV_HEADS = D_MODEL // RWKV_HEAD_DIM
RWKV_DECAY_LORA = 64
RWKV_AAA_LORA = 64
RWKV_GATE_LORA = 160
RWKV_GN_EPS = RWKV_HEAD_DIM * 1e-5

SGU_CHUNK = 128
SGU_WIDTH = 2 * D_MODEL
SGU_GROUPS = 8
SGU_GROUP_DIM = SGU_WIDTH // SGU_GROUPS

RET_HEADS = 4
RET_QK_DIM = D_MODEL // RET_HEADS
RET_V_DIM = 2 * RET_QK_DIM
RET_CHUNK = 128

D_FF = 256 * math.ceil(8 * D_MODEL / 3 / 256)
NORM_EPS = 1e-6
LN_EPS = 1e-5

kernel_name = 'hybrid_conv_rwkv7_sgu_retention_trunk'

def rmsnorm(x, g, eps=NORM_EPS):
    x32 = x.astype(jnp.float32)
    y = x32 * lax.rsqrt(jnp.mean(x32 * x32, axis=-1, keepdims=True) + eps)
    return (y * g.astype(jnp.float32)).astype(x.dtype)

def layernorm(x, g, b, eps=LN_EPS):
    x32 = x.astype(jnp.float32)
    mu = jnp.mean(x32, axis=-1, keepdims=True)
    var = jnp.mean(jnp.square(x32 - mu), axis=-1, keepdims=True)
    y = (x32 - mu) * lax.rsqrt(var + eps)
    return (y * g.astype(jnp.float32) + b.astype(jnp.float32)).astype(x.dtype)

def conv_module(h, w_in, b_in, dw, dw_b, ln_g, ln_b, w_out, b_out):
    z = h @ w_in + b_in
    a, gate = jnp.split(z, 2, axis=-1)
    z = a * jax.nn.sigmoid(gate)
    z = lax.conv_general_dilated(
        z, dw[:, None, :].astype(z.dtype), window_strides=(1,),
        padding=[(CONV_WIDTH - 1, 0)],
        dimension_numbers=('NWC', 'WIO', 'NWC'),
        feature_group_count=D_MODEL) + dw_b
    z = jax.nn.silu(layernorm(z, ln_g, ln_b))
    return z @ w_out + b_out

def rwkv7_time_mix(h, mix, w_rkv, w0, w1, w2, a0, a1, a2, g1, g2, k_k, k_a, r_k, gn_g, gn_b, w_o):
    B, T, D = h.shape
    H, N = RWKV_HEADS, RWKV_HEAD_DIM
    h_prev = jnp.pad(h, ((0, 0), (1, 0), (0, 0)))[:, :T]
    xs = h[None] + (h_prev - h)[None] * mix[:, None, None, :]
    r = xs[0] @ w_rkv[0]
    k = xs[2] @ w_rkv[1]
    v = xs[3] @ w_rkv[2]
    w = -jax.nn.softplus(-(w0 + jnp.tanh(xs[1] @ w1) @ w2)) - 0.5
    decay = jnp.exp(-jnp.exp(w.astype(jnp.float32)))
    a = jax.nn.sigmoid(a0 + (xs[4] @ a1) @ a2)
    g = jax.nn.sigmoid(xs[5] @ g1) @ g2

    def heads(t):
        return t.astype(jnp.float32).reshape(B, T, H, N)

    kk = heads(k * k_k)
    kk = kk / jnp.maximum(jnp.sqrt(jnp.sum(kk * kk, axis=-1, keepdims=True)), 1e-12)
    k = k * (1.0 + (a - 1.0) * k_a)
    r_h, k_h, v_h, a_h, w_h = heads(r), heads(k), heads(v), heads(a), heads(decay)

    def step(S, inp):
        r_t, w_t, k_t, v_t, a_t, b_t = inp
        sa = jnp.einsum('bhij,bhj->bhi', S, a_t)
        S = S * w_t[:, :, None, :] + sa[..., None] * b_t[:, :, None, :] + v_t[..., None] * k_t[:, :, None, :]
        return S, jnp.einsum('bhij,bhj->bhi', S, r_t)

    def tmajor(t):
        return jnp.swapaxes(t, 0, 1)

    S0 = jnp.zeros((B, H, N, N), jnp.float32)
    _, y = lax.scan(step, S0, (tmajor(r_h), tmajor(w_h), tmajor(k_h), tmajor(v_h),
                               tmajor(-kk), tmajor(kk * a_h)))
    y = tmajor(y)
    y = layernorm(y, gn_g.reshape(H, N), gn_b.reshape(H, N), RWKV_GN_EPS)
    y = y + jnp.sum(r_h * k_h * r_k, axis=-1, keepdims=True) * v_h
    return (y.reshape(B, T, D) * g) @ w_o

def spatial_gating_mixer(h, w_in, b_in, ln_g, ln_b, ws, bs, w_out):
    B, T, _ = h.shape
    z = jax.nn.gelu(h @ w_in + b_in, approximate=False)
    u, v = jnp.split(z, 2, axis=-1)
    v = layernorm(v, ln_g, ln_b)
    n_chunks = T // SGU_CHUNK
    v = v.reshape(B, n_chunks, SGU_CHUNK, SGU_GROUPS, SGU_GROUP_DIM)
    causal = jnp.tril(jnp.ones((SGU_CHUNK, SGU_CHUNK), dtype=bool))
    ws_c = jnp.where(causal[None], ws, jnp.zeros((), ws.dtype))
    v = jnp.einsum('gts,bcsge->bctge', ws_c, v) + jnp.transpose(bs)[None, None, :, :, None]
    return (u * v.reshape(B, T, SGU_WIDTH)) @ w_out

def rotate_every_two(x):
    x1 = x[..., ::2]
    x2 = x[..., 1::2]
    return jnp.stack((-x2, x1), axis=-1).reshape(x.shape)

def retention_mixer(h, w_in, w_out):
    B, T, D = h.shape
    H, dk, dv, C = RET_HEADS, RET_QK_DIM, RET_V_DIM, RET_CHUNK
    q, k, v, g = jnp.split(h @ w_in, [D, 2 * D, 4 * D], axis=-1)
    q = q.reshape(B, T, H, dk)
    k = k.reshape(B, T, H, dk) * (dk ** -0.5)
    v = v.reshape(B, T, H, dv).astype(jnp.float32)
    angle = jnp.repeat(1.0 / (10000.0 ** jnp.linspace(0.0, 1.0, dk // 2, dtype=jnp.float32)), 2)
    theta = jnp.arange(T, dtype=jnp.float32)[:, None] * angle[None]
    sin, cos = jnp.sin(theta)[:, None, :], jnp.cos(theta)[:, None, :]
    q = q * cos + rotate_every_two(q) * sin
    k = k * cos + rotate_every_two(k) * sin

    log_gamma = jnp.log(1.0 - 2.0 ** (-5.0 - jnp.arange(H, dtype=jnp.float32)))
    n_chunks = T // C

    def chunked(t):
        return t.reshape(B, n_chunks, C, H, t.shape[-1]).transpose(0, 3, 1, 2, 4)

    q, k, v = chunked(q), chunked(k), chunked(v)
    idx = jnp.arange(C, dtype=jnp.float32)
    diff = idx[:, None] - idx[None, :]
    decay_mask = jnp.where(diff[None] >= 0,
                           jnp.exp(log_gamma[:, None, None] * jnp.maximum(diff, 0.0)[None]), 0.0)
    scores = jnp.einsum('bhncd,bhnsd->bhncs', q, k) * decay_mask[:, None]
    inner = jnp.einsum('bhncs,bhnse->bhnce', scores, v)

    q_decay = jnp.exp(log_gamma[:, None] * (idx + 1.0))
    k_decay = jnp.exp(log_gamma[:, None] * (C - 1.0 - idx))
    chunk_decay = jnp.exp(log_gamma * C)
    qs = q * q_decay[:, None, :, None]
    ks = k * k_decay[:, None, :, None]

    def step(R, inp):
        qc, kc, vc = inp
        cross = jnp.einsum('bhcd,bhde->bhce', qc, R)
        R = R * chunk_decay[None, :, None, None] + jnp.einsum('bhcd,bhce->bhde', kc, vc)
        return R, cross

    def nmajor(t):
        return jnp.moveaxis(t, 2, 0)

    R0 = jnp.zeros((B, H, dk, dv), jnp.float32)
    _, cross = lax.scan(step, R0, (nmajor(qs), nmajor(ks), nmajor(v)))
    o = inner + jnp.moveaxis(cross, 0, 2)
    o = o.transpose(0, 2, 3, 1, 4).reshape(B, T, H, dv)
    o = o * lax.rsqrt(jnp.mean(o * o, axis=-1, keepdims=True) + NORM_EPS)
    return (jax.nn.silu(g) * o.reshape(B, T, H * dv)) @ w_out

def memory_cross_attention(h, mem_n, wq, wkv, wo):
    B, T, D = h.shape
    M = mem_n.shape[1]
    q = (h @ wq).reshape(B, T, XA_HEADS, XA_HEAD_DIM)
    k, v = jnp.split(mem_n @ wkv, 2, axis=-1)
    k = k.reshape(B, M, XA_HEADS, XA_HEAD_DIM)
    v = v.reshape(B, M, XA_HEADS, XA_HEAD_DIM)
    s = jnp.einsum('bthd,bmhd->bhtm', q, k).astype(jnp.float32) * (XA_HEAD_DIM ** -0.5)
    p = jax.nn.softmax(s, axis=-1).astype(v.dtype)
    o = jnp.einsum('bhtm,bmhd->bthd', p, v).reshape(B, T, D)
    return o @ wo

def swiglu(h, w_gate_up, w_down):
    gt, up = jnp.split(h @ w_gate_up, 2, axis=-1)
    return (jax.nn.silu(gt) * up) @ w_down

def setup_inputs(seed: int = 0) -> dict:
    key = jax.random.key(seed)
    ks = iter(jax.random.split(key, 64))
    D, F, E = D_MODEL, D_FF, SGU_WIDTH
    nA, nB, nC, nD = N_LAYERS_CONV, N_LAYERS_RWKV, N_LAYERS_SGU, N_LAYERS_RET

    def normal(shape, scale):
        return scale * jax.random.normal(next(ks), shape, jnp.float32)

    def gain(shape):
        return 1.0 + normal(shape, 0.02)

    def uniform(shape, lo, hi):
        return jax.random.uniform(next(ks), shape, jnp.float32, lo, hi)

    return {
        'x': normal((BATCH, SEQ, D), 1.0),
        'mem': normal((BATCH, N_MEM, D), 1.0),
        'mix_norm_g': gain((DEPTH, D)),
        'xattn_norm_g': gain((DEPTH, D)),
        'mem_norm_g': gain((DEPTH, D)),
        'xattn_wq': normal((DEPTH, D, D), D ** -0.5),
        'xattn_wkv': normal((DEPTH, D, 2 * D), D ** -0.5),
        'xattn_wo': normal((DEPTH, D, D), D ** -0.5),
        'ffn_norm_g': gain((DEPTH, D)),
        'ffn_w_gate_up': normal((DEPTH, D, 2 * F), D ** -0.5),
        'ffn_w_down': normal((DEPTH, F, D), F ** -0.5),
        'conv_w_in': normal((nA, D, 2 * D), D ** -0.5),
        'conv_b_in': normal((nA, 2 * D), 0.02),
        'conv_dw': normal((nA, CONV_WIDTH, D), CONV_WIDTH ** -0.5),
        'conv_dw_b': normal((nA, D), 0.02),
        'conv_ln_g': gain((nA, D)),
        'conv_ln_b': normal((nA, D), 0.02),
        'conv_w_out': normal((nA, D, D), D ** -0.5),
        'conv_b_out': normal((nA, D), 0.02),
        'rwkv_mix': uniform((nB, 6, D), 0.0, 1.0),
        'rwkv_w_rkv': normal((nB, 3, D, D), D ** -0.5),
        'rwkv_w0': uniform((nB, D), -6.0, 1.0),
        'rwkv_w1': normal((nB, D, RWKV_DECAY_LORA), D ** -0.5),
        'rwkv_w2': normal((nB, RWKV_DECAY_LORA, D), 0.1 * RWKV_DECAY_LORA ** -0.5),
        'rwkv_a0': normal((nB, D), 0.5),
        'rwkv_a1': normal((nB, D, RWKV_AAA_LORA), D ** -0.5),
        'rwkv_a2': normal((nB, RWKV_AAA_LORA, D), 0.1 * RWKV_AAA_LORA ** -0.5),
        'rwkv_g1': normal((nB, D, RWKV_GATE_LORA), D ** -0.5),
        'rwkv_g2': normal((nB, RWKV_GATE_LORA, D), RWKV_GATE_LORA ** -0.5),
        'rwkv_k_k': 0.85 + normal((nB, D), 0.02),
        'rwkv_k_a': gain((nB, D)),
        'rwkv_r_k': normal((nB, RWKV_HEADS, RWKV_HEAD_DIM), 0.1),
        'rwkv_gn_g': gain((nB, D)),
        'rwkv_gn_b': normal((nB, D), 0.02),
        'rwkv_w_o': normal((nB, D, D), D ** -0.5),
        'sgu_w_in': normal((nC, D, 2 * E), D ** -0.5),
        'sgu_b_in': normal((nC, 2 * E), 0.02),
        'sgu_ln_g': gain((nC, E)),
        'sgu_ln_b': normal((nC, E), 0.02),
        'sgu_ws': normal((nC, SGU_GROUPS, SGU_CHUNK, SGU_CHUNK), 0.5 * SGU_CHUNK ** -0.5),
        'sgu_bs': gain((nC, SGU_GROUPS, SGU_CHUNK)),
        'sgu_w_out': normal((nC, E, D), E ** -0.5),
        'ret_w_in': normal((nD, D, 6 * D), D ** -0.5),
        'ret_w_out': normal((nD, 2 * D, D), (2 * D) ** -0.5),
        'final_norm_g': gain((D,)),
    }

def reference(x, mem, mix_norm_g, xattn_norm_g, mem_norm_g, xattn_wq, xattn_wkv, xattn_wo,
              ffn_norm_g, ffn_w_gate_up, ffn_w_down,
              conv_w_in, conv_b_in, conv_dw, conv_dw_b, conv_ln_g, conv_ln_b, conv_w_out, conv_b_out,
              rwkv_mix, rwkv_w_rkv, rwkv_w0, rwkv_w1, rwkv_w2, rwkv_a0, rwkv_a1, rwkv_a2,
              rwkv_g1, rwkv_g2, rwkv_k_k, rwkv_k_a, rwkv_r_k, rwkv_gn_g, rwkv_gn_b, rwkv_w_o,
              sgu_w_in, sgu_b_in, sgu_ln_g, sgu_ln_b, sgu_ws, sgu_bs, sgu_w_out,
              ret_w_in, ret_w_out, final_norm_g):
    for i in range(DEPTH):
        m, j = i % N_MIXERS, i // N_MIXERS
        hn = rmsnorm(x, mix_norm_g[i])
        if m == 0:
            y = conv_module(hn, conv_w_in[j], conv_b_in[j], conv_dw[j], conv_dw_b[j],
                            conv_ln_g[j], conv_ln_b[j], conv_w_out[j], conv_b_out[j])
        elif m == 1:
            y = rwkv7_time_mix(hn, rwkv_mix[j], rwkv_w_rkv[j], rwkv_w0[j], rwkv_w1[j], rwkv_w2[j],
                               rwkv_a0[j], rwkv_a1[j], rwkv_a2[j], rwkv_g1[j], rwkv_g2[j],
                               rwkv_k_k[j], rwkv_k_a[j], rwkv_r_k[j], rwkv_gn_g[j], rwkv_gn_b[j],
                               rwkv_w_o[j])
        elif m == 2:
            y = spatial_gating_mixer(hn, sgu_w_in[j], sgu_b_in[j], sgu_ln_g[j], sgu_ln_b[j],
                                     sgu_ws[j], sgu_bs[j], sgu_w_out[j])
        else:
            y = retention_mixer(hn, ret_w_in[j], ret_w_out[j])
        x = x + y
        x = x + memory_cross_attention(rmsnorm(x, xattn_norm_g[i]), rmsnorm(mem, mem_norm_g[i]),
                                       xattn_wq[i], xattn_wkv[i], xattn_wo[i])
        x = x + swiglu(rmsnorm(x, ffn_norm_g[i]), ffn_w_gate_up[i], ffn_w_down[i])
    return rmsnorm(x, final_norm_g)


_drawn_inputs = setup_inputs


def setup_inputs(seed=0):
    import zlib

    import numpy as np

    out = dict(_drawn_inputs(seed))
    spreads = {}
    factors = {'xattn_norm_g': 8.0,
     'mem_norm_g': 8.0,
     'conv_ln_b': 2.83,
     'rwkv_w1': 8.0,
     'rwkv_w2': 8.0,
     'rwkv_a1': 2.774,
     'rwkv_a2': 2.884,
     'rwkv_k_k': 7.149,
     'rwkv_k_a': 4.465,
     'rwkv_gn_g': 5.588,
     'rwkv_gn_b': 5.283,
     'sgu_b_in': 4.798,
     'sgu_ln_g': 8.0,
     'sgu_ln_b': 8.0,
     'sgu_bs': 5.31,
     'final_norm_g': 3.026}
    for name, (base, spread) in spreads.items():
        noise = np.random.default_rng([zlib.crc32(name.encode()), seed]).standard_normal(out[name].shape)
        drawn = base * np.exp(spread * noise) if base else spread * noise
        out[name] = __import__('jax').numpy.asarray(drawn.astype(out[name].dtype))
    for name, factor in factors.items():
        out[name] = (out[name] * factor).astype(out[name].dtype)
    return out
```

```python
import numpy as np
import concourse.bass as bass
from concourse import mybir

P = 128
D = 1024
T = 256
HALVES = T // P
KC = D // P
COLS = 512
F = 2816
FC = F // P
E2 = 2 * D
TAPS = 31
HD = 64
NH = D // HD
CH = 64
XH = 4
HW = D // XH
RAW, SPLIT, LOOK = 4, 8, 4
MIXER_LOADS = [2, 10, 12, 15]

M_IDENT, M_CUM, M_STRICT, M_INCL, M_PAIR_T, M_LEVEL = 0, 1, 2, 3, 4, 5
LEVELS = 6
M_CHUNK = M_LEVEL + LEVELS
M_TRI_ALL = M_CHUNK + 1
N_MASKS = M_TRI_ALL + 1


def constant_masks():
    r = np.arange(P)[:, None]
    c = np.arange(P)[None, :]
    same = (r // CH) == (c // CH)
    m = np.zeros((N_MASKS, P, P), np.float32)
    m[M_IDENT] = r == c
    m[M_CUM] = same & (r <= c)
    m[M_STRICT] = same & (r < c)
    m[M_INCL] = same & (r <= c)
    for n in range(LEVELS):
        b = 1 << n
        m[M_LEVEL + n] = ((r // (2 * b)) == (c // (2 * b))) & ((r // b) % 2 == 1) & ((c // b) % 2 == 0)
    m[M_PAIR_T] = m[M_LEVEL].T
    m[M_CHUNK][:, 0] = (np.arange(P) < CH)
    m[M_CHUNK][:, 1] = (np.arange(P) >= CH)
    m[M_TRI_ALL] = r <= c
    return np.ascontiguousarray(m.transpose(1, 0, 2).reshape(P, N_MASKS * P))


def rotary_tables():
    angle = np.repeat(np.float32(1.0) / (np.float32(10000.0) ** np.linspace(0.0, 1.0, HW // 2, dtype=np.float32)), 2)
    theta = np.arange(T, dtype=np.float32)[:, None] * angle.astype(np.float32)[None]
    sin = np.sin(theta).astype(np.float32)
    sin[:, 0::2] *= -1.0
    return np.stack([np.cos(theta).astype(np.float32), sin])


def decay_masks():
    lg = np.log(1.0 - 2.0 ** (-5.0 - np.arange(XH, dtype=np.float64)))
    s = np.arange(P)[:, None]
    t = np.arange(P)[None, :]
    out = np.zeros((P, XH, 3, P), np.float64)
    for h in range(XH):
        out[:, h, 0] = np.where(t >= s, np.exp(lg[h] * np.maximum(t - s, 0)), 0.0)
        out[:, h, 1] = np.exp(lg[h] * (t + P - s))
        out[:, h, 2] = out[:, h, 0]
    return (out * HW ** -0.5).astype(np.float32).reshape(P, XH * 3 * P)


def weight_plan(w, layers):
    plan = []

    def product(name, src, rows, cols, paired=False):
        plan.append(dict(name=name, src=src, tiles=rows // 256, groups=cols // COLS, paired=paired))

    for i in range(layers):
        if i == 0:
            product("conv_in", w["conv_w_in"][0], D, 2 * D, True)
            product("conv_out", w["conv_w_out"][0], D, D)
        if i == 1:
            for m in range(3):
                product("rkv", w["rwkv_w_rkv"][0, m], D, D)
            product("rwkv_out", w["rwkv_w_o"][0], D, D)
        if i == 2:
            product("sgu_in", w["sgu_w_in"][0], D, 2 * E2)
            product("sgu_out", w["sgu_w_out"][0], E2, D)
        if i == 3:
            product("ret_in", w["ret_w_in"][0], D, 6 * D)
            product("ret_out", w["ret_w_out"][0], E2, D)
        product("kv", w["xattn_wkv"][i], D, 2 * D)
        product("q", w["xattn_wq"][i], D, D)
        product("wo", w["xattn_wo"][i], D, D)
        product("gate_up", w["ffn_w_gate_up"][i], D, 2 * F, True)
        product("down", w["ffn_w_down"][i], F, D)
    tile = group = 0
    for p in plan:
        p["tile0"], p["group0"] = tile, group
        tile += p["tiles"] * p["groups"]
        group += p["groups"]
    return plan


def row_plan(w, layers):
    rows = []
    for i in range(layers):
        rows.append((f"mix{i}", w["mix_norm_g"][i:i + 1, :], True))
        if i == 0:
            b = w["conv_b_in"]
            rows += [("b_a", b[:, 0:D], False), ("b_gate", b[:, D:2 * D], False),
                     ("conv_g", w["conv_ln_g"], True), ("conv_b", w["conv_ln_b"], True)]
        if i == 1:
            rows += [("w0", w["rwkv_w0"], False), ("a0", w["rwkv_a0"], False)]
            rows += [(n, w["rwkv_" + n] if n != "r_k" else w["rwkv_r_k"].rearrange("a h n -> a (h n)"), True)
                     for n in ("k_k", "k_a", "r_k", "gn_g", "gn_b")]
        if i == 2:
            rows += [(f"sgu_bias{j}", w["sgu_b_in"][:, j * D:(j + 1) * D], False) for j in range(4)]
            rows += [(f"sgu_g{j}", w["sgu_ln_g"][:, j * D:(j + 1) * D], True) for j in range(2)]
            rows += [(f"sgu_b{j}", w["sgu_ln_b"][:, j * D:(j + 1) * D], True) for j in range(2)]
        rows.append((f"mem{i}", w["mem_norm_g"][i:i + 1, :], True))
        if i == 0:
            rows.append(("conv_bo", w["conv_b_out"], False))
        rows.append((f"xattn{i}", w["xattn_norm_g"][i:i + 1, :], True))
        rows.append((f"ffn{i}", w["ffn_norm_g"][i:i + 1, :], True))
    rows.append(("final", w["final_norm_g"].rearrange("(a n) -> a n", a=1), True))
    return rows


def trunk_program(nc, w, out, layers):
    f32, f32r = mybir.dt.float32, mybir.dt.float32r
    ALU, ACT, AX = mybir.AluOpType, mybir.ActivationFunctionType, mybir.AxisListType
    plan = weight_plan(w, layers)
    rows = row_plan(w, layers)
    row_at = {name: n for n, (name, _, _) in enumerate(rows)}

    KB = 1024
    cursor = [(nc.sbuf_base + 63) // 64 * 64]

    def place(name, shape, dtype, at=None):
        size = 4 * int(np.prod(shape[1:]))
        if at is None:
            at = cursor[0]
            cursor[0] += (size + 63) // 64 * 64
        assert at + size <= nc.sbuf_usable_end, (name, at, size)
        return nc.alloc_sbuf_tensor_at(name, shape, dtype, offset=at)

    raw = place("raw_weights", [P, RAW, 2, COLS], f32)
    w_high = place("weights_high", [P, SPLIT, 2, COLS], f32r)
    w_low = place("weights_low", [P, SPLIT, 2, COLS], f32r)
    x = place("x", [P, HALVES, D], f32)
    mem = place("mem_normed", [P, HALVES, D], f32)
    row = place("rows", [P, 2, D], f32)
    masks = place("masks", [P, N_MASKS, P], f32)
    ones = place("ones", [1, P], f32)
    stat = place("stat", [P, 16], f32)
    pc = place("chunk_decay", [HD, HALVES, NH, 2], f32)
    bn = place("bn", [P, HALVES, 4, 6], f32)
    mv = place("mean_var", [P, HALVES, 2], f32)
    den = place("softmax_den", [P, 3, HALVES * XH], f32)
    small = place("head_stats", [P, 6, NH], f32)
    taps = place("taps", [P, KC, 32], f32)
    XT0 = cursor[0]
    xT_high = place("xT_high", [P, KC, T], f32r)
    xT_low = place("xT_low", [P, KC, T], f32r)
    ARENA = cursor[0]
    memT_high = place("memT_high", [P, KC, T], f32r, ARENA)
    memT_low = place("memT_low", [P, KC, T], f32r, ARENA + 8 * KB)
    kT = place("kT", [P, KC, T], f32, ARENA + 16 * KB)
    v_tok = place("v_tok", [P, HALVES, D], f32, ARENA + 24 * KB)
    BIG = ARENA + 32 * KB
    hT_high = place("hT_high", [P, FC, T], f32r, BIG)
    hT_low = place("hT_low", [P, FC, T], f32r, BIG + 22 * KB)
    sgate = place("silu_gate", [P, HALVES, 2, 256], f32, ARENA + 16 * KB)
    htok = place("h_tok", [P, HALVES, 2, 256], f32, ARENA + 20 * KB)
    k_tok = place("k_tok", [P, 2, HALVES, COLS], f32, BIG)
    xn = place("x_normed", [P, HALVES, D], f32, BIG + 36 * KB)
    q_tok = place("q_tok", [P, HALVES, D], f32, BIG)
    qT = place("qT", [P, KC, T], f32, BIG + 8 * KB)
    prob = place("prob", [P, HALVES, XH, T], f32, BIG + 16 * KB)
    probT = place("probT", [P, XH, HALVES, T], f32, BIG + 24 * KB)
    junk = place("junk", [P, D], f32, BIG + 32 * KB)
    yT_high = place("yT_high", [P, 2 * KC, T], f32r, XT0)

    psum = nc.alloc_psum_tensor("psum", [P, 8, COLS], f32)
    TR = 4

    def sem(name):
        return nc.alloc_semaphore(name)

    raw_loaded = [sem(f"raw_loaded{s}") for s in range(RAW)]
    w_high_ready = sem("w_high_ready")
    w_low_ready = sem("w_low_ready")
    tile_used = sem("tile_used")
    group_drained = sem("group_drained")
    cols_filled = sem("cols_filled")
    cols_high = sem("cols_high")
    cols_drained = sem("cols_drained")
    x_loaded = sem("x_loaded")
    const_loaded = sem("const_loaded")
    row_loaded = [sem(f"row_loaded{s}") for s in range(2)]
    row_used = sem("row_used")
    vec_step = sem("vec_step")
    act_step = sem("act_step")
    squares_summed = sem("squares_summed")
    stat_ready = sem("stat_ready")
    root_ready = sem("root_ready")
    tok_ready = sem("tok_ready")
    scores_filled = sem("scores_filled")
    scores_used = sem("scores_used")
    neg_max = sem("neg_max")
    exp_done = sem("exp_done")
    act_out = sem("act_out")
    vec_out = sem("vec_out")
    result_ready = sem("result_ready")
    stored = sem("stored")
    mixer_in = sem("mixer_in")
    mixer_free = sem("mixer_free")
    mixer_zero = sem("mixer_zero")
    square_summed = sem("square_summed")
    lane_filled = [sem(f"lane_filled{j}") for j in range(2)]
    lane_used = [sem(f"lane_used{j}") for j in range(2)]

    ident = masks[:, M_IDENT, :]

    z_tok = place("z_tok", [P, HALVES, D], f32, BIG)
    zT = place("zT", [P, KC, T + TAPS - 1], f32, BIG + 8 * KB)
    conv = place("conv", [P, KC, T], f32, BIG + 18 * KB)
    sig = place("sig", [P, 2, HALVES, 256], f32, BIG + 26 * KB)
    dw_tok = place("dw_tok", [32, D], f32, BIG + 30 * KB)
    u_tok = place("u_tok", [P, HALVES, E2], f32, BIG)
    g_tok = place("g_tok", [P, HALVES, E2], f32, BIG + 16 * KB)
    gate_low = place("gate_low", [P, 2 * KC, T], f32r, BIG + 16 * KB)
    ws_in = place("ws_in", [P, 8, P], f32, ARENA + 16 * KB)
    wsT = place("wsT", [P, 8, P], f32, ARENA + 20 * KB)
    bs_in = place("bs_in", [8, P], f32, ARENA + 24 * KB)
    bsT = place("bsT", [P, 8], f32, ARENA + 25 * KB)
    sgu_low = place("sgu_low", [P, 2 * KC, T], f32r, BIG + 16 * KB)

    qk = [place(f"ret_{n}", [P, HALVES, D], f32, ARENA + 8 * KB * j) for j, n in enumerate("qk")]
    o_tok = place("o_tok", [P, HALVES, E2], f32, ARENA)
    rv = place("ret_v", [P, HALVES, E2], f32, ARENA + 16 * KB)
    ret_low = place("ret_low", [P, 2 * KC, T], f32r, ARENA + 16 * KB)
    rg = place("ret_gate", [P, HALVES, E2], f32, ARENA + 32 * KB)
    rotary = place("rotary_cs", [P, 2, HALVES, HW], f32, ARENA + 48 * KB)
    decay = place("decay", [P, XH, 3 * P], f32, ARENA + 52 * KB)
    sc = place("ret_scores", [P, XH, 3 * P], f32, ARENA + 58 * KB)
    rtmp = place("rot_tmp", [P, XH, HW // 2, 2], f32, ARENA + 64 * KB)
    qkT = [place(f"ret_{n}T", [P, KC, T], f32, XT0 + 8 * KB * j) for j, n in enumerate("qk")]
    hT = place("hT", [P, KC, T + 1], f32, ARENA)
    diff = place("shift_diff", [P, KC, T], f32, ARENA + 8 * KB + 256)
    xs = place("xs", [P, KC, T], f32, ARENA + 16 * KB + 256)
    W0 = ARENA + 24 * KB + 256
    rr, rk, rvv, lw, ra, rgate = [place("rwkv_" + n, [P, HALVES, D], f32, W0 + 8 * KB * j)
                                  for j, n in enumerate(["r", "k", "v", "lw", "a", "gate"])]
    xs_b = place("xs_b", [P, KC, T], f32, W0 + 16 * KB)
    mix_in = place("mix_in", [6, D], f32, W0 + 32 * KB)
    lora = [place(f"lora_hidden{j}", [P, T], f32, W0 + (48 + j) * KB) for j in range(3)]
    lora1 = [place("lora1_" + n, [P, KC, k], f32, XT0 + o) for n, k, o in (("w", 64, 0), ("a", 64, 2 * KB), ("g", 160, 4 * KB))]
    lora2 = [place("lora2_" + n, [k, D], f32, W0 + 4 * KB * j)
             for j, (n, k) in enumerate((("w", 64), ("a", 64), ("g", P), ("g_rest", 32)))]
    kk = place("kk", [P, HALVES, D], f32, ARENA + 16 * KB + 256)
    tmp = [place(f"tmp{j}", [P, D], f32, XT0 + 4 * KB * j) for j in range(4)]
    aT, bT, kkT, rT = [place("chunk_" + n, [HD, 8, P], f32, XT0 + 4 * KB * j) for j, n in enumerate(["aT", "bT", "kT", "rT"])]
    inv, invT, lvl = [place("chunk_" + n, [P, 8, P], f32, XT0 + 4 * KB * j) for j, n in enumerate(["inv", "invT", "level"])]
    wT = place("chunk_wT", [HD, 8, P], f32, XT0)
    abT, akT, rbT, rkT = [place("chunk_" + n, [P, 8, P], f32, ARENA + 4 * KB * j) for j, n in enumerate(["abT", "akT", "rbT", "rkT"])]
    hh = place("chunk_h", [P, 8, HD], f32, W0 + 24 * KB)
    uu = place("chunk_u", [P, 8, HD], f32, W0 + 24 * KB)
    zz = place("chunk_z", [P, 8, HD], f32, W0 + 26 * KB)
    state = place("state", [HD, NH, HD], f32, W0 + 28 * KB)

    def bank(b):
        return psum[:, b, :]

    def source(p, g, kt):
        if p["paired"]:
            half = p["groups"] * 256
            v = p["src"].rearrange("(k p) n -> p k n", p=P)
            return [v[:, 2 * kt:2 * kt + 2, a * half + 256 * g:a * half + 256 * g + 256] for a in range(2)]
        return p["src"].rearrange("(k p) n -> p k n", p=P)[:, 2 * kt:2 * kt + 2, COLS * g:COLS * g + COLS]

    n_tiles = sum(p["tiles"] * p["groups"] for p in plan)

    with nc.Block() as block:

        @block.sync
        def _(sp):
            sp.dma_start(x[:, :, :], w["x"][0].rearrange("(h p) n -> p h n", p=P)).then_inc(x_loaded, 16)
            sp.dma_start(mem[:, :, :], w["mem"][0].rearrange("(h p) n -> p h n", p=P)).then_inc(x_loaded, 16)
            sp.dma_start(masks[:, :, :], w["masks"].rearrange("p (m n) -> p m n", n=P)).then_inc(const_loaded, 16)
            n = 0
            for p in plan:
                for g in range(p["groups"]):
                    for kt in range(p["tiles"]):
                        if n >= RAW:
                            sp.wait_ge(w_low_ready, n - RAW + 1)
                        if p["paired"]:
                            for a, src in enumerate(source(p, g, kt)):
                                sp.dma_start(raw[:, n % RAW, :, 256 * a:256 * a + 256], src).then_inc(raw_loaded[n % RAW], 16)
                        else:
                            sp.dma_start(raw[:, n % RAW, :, :], source(p, g, kt)).then_inc(raw_loaded[n % RAW], 32)
                        n += 1
            sp.wait_ge(result_ready, 1)
            sp.dma_start(out[0].rearrange("(h p) n -> p h n", p=P), xn[:, :, :]).then_inc(stored, 16)
            sp.wait_ge(stored, 16)

        @block.gpsimd
        def _(pool):
            pool.memset(ones[:, :], 1.0).then_inc(mixer_zero, 1)
            mixer_count = [0]
            for n, (name, src, wide) in enumerate(rows):
                if n >= 2:
                    pool.wait_ge(row_used, n - 1)
                dst, s = (row[:, n % 2, :], src.to_broadcast([P, D])) if wide else (row[0:1, n % 2, :], src)
                pool.dma_start(dst, s).then_inc(row_loaded[n % 2], 16)
                if name == "mix0":
                    pool.memset(zT[:, :, 0:TAPS - 1], 0.0).then_inc(mixer_zero, 1)
                    pool.dma_start(dw_tok[0:TAPS, :], w["conv_dw"][0]).then_inc(mixer_in, 16)
                    pool.dma_start(dw_tok[TAPS:TAPS + 1, :], w["conv_dw_b"]).then_inc(mixer_in, 16)
                if name == "mix1":
                    pool.wait_ge(mixer_free, 1)
                    for j, n1 in enumerate(("rwkv_w1", "rwkv_a1", "rwkv_g1")):
                        pool.dma_start(lora1[j][:, :, :], w[n1][0].rearrange("(k p) n -> p k n", p=P)).then_inc(mixer_in, 16)
                    pool.dma_start(lora2[0][:, :], w["rwkv_w2"][0]).then_inc(mixer_in, 16)
                    pool.dma_start(lora2[1][:, :], w["rwkv_a2"][0]).then_inc(mixer_in, 16)
                    pool.dma_start(lora2[2][:, :], w["rwkv_g2"][0, 0:P, :]).then_inc(mixer_in, 16)
                    pool.dma_start(lora2[3][:, :], w["rwkv_g2"][0, P:P + 32, :]).then_inc(mixer_in, 16)
                    pool.dma_start(mix_in[:, :], w["rwkv_mix"][0]).then_inc(mixer_in, 16)
                if name == "mix3":
                    pool.wait_ge(mixer_free, 3)
                    pool.dma_start(rotary[:, 0, :, :], w["rotary"][0].rearrange("(h p) n -> p h n", p=P)).then_inc(mixer_in, 16)
                    pool.dma_start(rotary[:, 1, :, :], w["rotary"][1].rearrange("(h p) n -> p h n", p=P)).then_inc(mixer_in, 16)
                    pool.dma_start(decay[:, :, :], w["decay"].rearrange("p (h n) -> p h n", h=XH)).then_inc(mixer_in, 16)
                if name == "mix2":
                    pool.wait_ge(mixer_free, 2)
                    pool.dma_start(ws_in[:, :, :], w["sgu_ws"][0].rearrange("g t s -> t g s")).then_inc(mixer_in, 16)
                    pool.dma_start(bs_in[:, :], w["sgu_bs"][0]).then_inc(mixer_in, 16)

        @block.scalar
        def _(act):
            at = dict(prod=0, split=0, col=0, high=0, score=0, sumsq=0, stat=0, exp=0, step=0, vec=0, neg=0, tile=0, lane=0, lane1=0)

            def split_to(n):
                while at["split"] < min(n, n_tiles):
                    t = at["split"]
                    act.wait_ge(raw_loaded[t % RAW], 32 * (t // RAW + 1))
                    if t >= SPLIT:
                        act.wait_ge(tile_used, t - SPLIT + 1)
                    act.activation(w_high[:, t % SPLIT, :, :], raw[:, t % RAW, :, :], ACT.Copy).then_inc(w_high_ready, 1)
                    at["split"] += 1

            def group_done(tiles):
                at["tile"] += tiles
                split_to(at["tile"] + LOOK)
                act.wait_ge(tile_used, at["tile"])

            def columns(high, chunks, c0=0):
                for c in range(0, chunks, 2):
                    act.wait_ge(cols_filled, at["col"] + 1)
                    act.activation(high[:, c0 + c:c0 + c + 2, :], bank(TR + at["col"] % 2), ACT.Copy).then_inc(cols_high, 1)
                    at["col"] += 1

            def skip_columns(banks):
                at["col"] += banks

            def root(view):
                at["stat"] += 1
                act.wait_ge(stat_ready, at["stat"])
                act.activation(view, view, ACT.Sqrt).then_inc(root_ready, 1)

            def rms(src, wait):
                wait()
                for h in range(HALVES):
                    act.activation(xn[:, h, :], src[:, h, :], ACT.Square, accum_out=stat[:, h:h + 1]).then_inc(squares_summed, 1)
                root(stat[:, 2:4])

            def x_complete():
                act.wait_ge(group_drained, at["prod"])

            def product_groups(groups, tiles, evac=None):
                for g in range(groups):
                    group_done(tiles)
                    if evac:
                        evac(g, at["prod"] % 2)
                    at["prod"] += 1

            def gelu_evac(g, par):
                dst = u_tok if g < 4 else g_tok
                for h in range(HALVES):
                    act.activation(dst[:, h, (g % 4) * COLS:(g % 4 + 1) * COLS], bank(2 * par + h), ACT.Gelu).then_inc(act_out, 1)

            def sigmoid_evac(g, par):
                for h in range(HALVES):
                    if g >= 2:
                        act.wait_ge(group_drained, at["prod"] - 1)
                    act.activation(sig[:, g % 2, h, :], psum[:, 2 * par + h, 256:512], ACT.Sigmoid).then_inc(act_out, 1)

            def silu_evac(g, par):
                for h in range(HALVES):
                    if g >= 2:
                        act.wait_ge(group_drained, at["prod"] - 1)
                    act.activation(sgate[:, g % 2, h, :], psum[:, 2 * par + h, 0:256], ACT.Silu).then_inc(act_out, 1)

            def conv_mixer():
                skip_columns(2)
                product_groups(4, 4, sigmoid_evac)
                skip_columns(4 + 4)
                for h in range(HALVES):
                    root(mv[:, h, 1:2])
                at["vec"] += 1
                act.wait_ge(vec_out, at["vec"])
                act.activation(z_tok[:, :, :], z_tok[:, :, :], ACT.Silu).then_inc(act_out, 1)
                columns(xT_high, KC)
                return 2, 4

            def sgu_mixer():
                skip_columns(3)
                product_groups(8, 4, gelu_evac)
                for h in range(HALVES):
                    root(mv[:, h, 1:2])
                at["score"] += 8
                columns(yT_high, 2 * KC)
                return 2, 8

            def ret_mixer():
                product_groups(4, 4)
                for g in range(8):
                    group_done(4)
                    par = at["prod"] % 2
                    dst, fn = (rv, ACT.Copy) if g < 4 else (rg, ACT.Silu)
                    for h in range(HALVES):
                        act.activation(dst[:, h, (g % 4) * COLS:(g % 4 + 1) * COLS], bank(2 * par + h), fn).then_inc(act_out, 1)
                    at["prod"] += 1
                skip_columns(8)
                at["score"] += XH
                for n in range(HALVES * XH):
                    act.wait_ge(scores_filled, at["score"] + 1)
                    if n:
                        act.wait_ge(square_summed, n)
                    act.activation(rtmp[:, 0:2, :, :].rearrange("p a n e -> p (a n e)"), bank(6 + at["score"] % 2), ACT.Square,
                                   accum_out=small[:, 0, n:n + 1]).then_inc(square_summed, 1)
                    at["score"] += 1
                root(small[:, 1, 0:8])
                columns(yT_high, 2 * KC)
                return 2, 8

            def lane_take():
                n = at["lane"]
                act.wait_ge(lane_filled[0], n + 1)
                at["lane"] += 1
                return n % 4

            def lane_copy(dst, view, fn=ACT.Copy):
                b = lane_take()
                act.activation(dst, view(psum[:, b, :]), fn).then_inc(lane_used[0], 1)

            def rwkv_mixer():
                skip_columns(4 + 1)
                for j, fn in enumerate((ACT.Tanh, ACT.Copy, ACT.Sigmoid)):
                    lane_copy(lora[j][0:(P if j == 2 else 64), :], lambda v: v[0:(P if j == 2 else 64), 0:T], fn)
                    if j == 2:
                        lane_copy(lora[0][0:32, :], lambda v: v[0:32, 0:T], fn)
                    for h in range(HALVES):
                        for n in range(2):
                            dst = (lw, ra, rgate)[j][:, h, COLS * n:COLS * n + COLS]
                            lane_copy(dst, lambda v: v, ACT.Copy if j == 2 else ACT.Sigmoid)
                for m in range(3):
                    at["vec"] += 1
                    act.wait_ge(vec_out, at["vec"])
                    act.activation(xT_high[:, :, :], (xs, xs_b, xs)[m][:, :, :], ACT.Copy).then_inc(act_out, 1)
                    product_groups(2, 4)
                for h in range(HALVES):
                    root(small[:, 1, :])
                for h in range(HALVES):
                    for n in range(2):
                        lane1 = at["lane1"]
                        act.wait_ge(lane_filled[1], lane1 + 1)
                        at["lane1"] += 1
                        cols = slice(COLS * n, COLS * n + COLS)
                        if 2 * h + n >= 1:
                            act.wait_ge(lane_used[1], lane1)
                            at["vec"] += 1
                            act.wait_ge(vec_out, at["vec"])
                        act.activation(tmp[0][:, 0:COLS], bank(4 + lane1 % 4), ACT.Exp).then_inc(act_out, 1)
                        act.activation(tmp[1][:, 0:COLS], bank(4 + lane1 % 4), ACT.Exp, scale=-1.0).then_inc(act_out, 1)
                        act.wait_ge(lane_used[1], lane1 + 1)
                        act.activation(tmp[2][:, 0:COLS], tmp[2][:, 0:COLS], ACT.Exp).then_inc(act_out, 1)
                lane_copy(pc[:, :, :, :], lambda v: v[0:HD, 0:64].rearrange("p (h n c) -> p h n c", h=HALVES, c=2), ACT.Exp)
                heads4 = lambda v: v[0:HD, :].rearrange("p (h t) -> p h t", h=4)
                heads8 = lambda v: v.rearrange("p (h t) -> p h t", h=8)
                for h in range(HALVES):
                    for hg in range(2):
                        for dst in (aT, bT, kkT, rT):
                            for sb in range(2):
                                lane_copy(dst[:, 4 * sb:4 * sb + 4, :], heads4)
                        for sb in range(2):
                            lane_copy(wT[:, 4 * sb:4 * sb + 4, :], heads4)
                        lane_copy(hh[:, :, :], heads8)
                        lane_copy(zz[:, :, :], heads8)
                        lane_copy(rr[:, h, 512 * hg:512 * hg + 512], lambda v: v)
                for h in range(HALVES):
                    root(small[:, 3, :])
                columns(xT_high, KC)
                return 2, 4

            act.wait_ge(x_loaded, 32)
            rms(mem, lambda: None)
            for i in range(layers):
                split_to(at["tile"] + LOOK)
                rms(x, x_complete)
                if i != 1:
                    columns(xT_high, KC)
                groups, tiles = [conv_mixer, rwkv_mixer, sgu_mixer, ret_mixer][i]()
                columns(memT_high, KC)
                product_groups(groups, tiles)
                rms(x, x_complete)
                product_groups(4, 4)
                skip_columns(4)
                columns(xT_high, KC)
                product_groups(2, 4)
                skip_columns(4)
                for h in range(HALVES):
                    for hp in range(XH // 2):
                        at["neg"] += 1
                        act.wait_ge(neg_max, at["neg"])
                        for e in range(2):
                            hd = 2 * hp + e
                            j = h * XH + hd
                            act.activation(prob[:, h, hd, :], psum[:, 6 + at["score"] % 2, e * T:(e + 1) * T], ACT.Exp,
                                           bias=den[:, 0, j:j + 1], scale=float(HW) ** -0.5,
                                           accum_out=den[:, 1, j:j + 1]).then_inc(exp_done, 1)
                        at["score"] += 1
                skip_columns(4)
                for c in range(XH):
                    act.wait_ge(scores_filled, at["score"] + 1)
                    act.activation(xT_high[:, 2 * c:2 * c + 2, :], bank(6 + at["score"] % 2), ACT.Copy).then_inc(cols_high, 1)
                    at["score"] += 1
                product_groups(2, 4)
                rms(x, x_complete)
                columns(xT_high, KC)
                for g in range(11):
                    group_done(4)
                    silu_evac(g, at["prod"] % 2)
                    at["prod"] += 1
                    if g:
                        columns(hT_high, 2, 2 * (g - 1))
                columns(hT_high, 2, 20)
                product_groups(2, 11)
            rms(x, x_complete)

        @block.vector
        def _(dve):
            at = dict(prod=0, split=0, col=0, high=0, score=0, sumsq=0, stat=0, exp=0, step=0, act=0, tile=0, lane=0)

            def link(ins):
                at["step"] += 1
                ins.then_inc(vec_step, 1)
                dve.wait_ge(vec_step, at["step"])

            def split_to(n):
                while at["split"] < min(n, n_tiles):
                    t = at["split"]
                    dve.wait_ge(w_high_ready, t + 1)
                    dve.tensor_tensor(w_low[:, t % SPLIT, :, :], raw[:, t % RAW, :, :],
                                      w_high[:, t % SPLIT, :, :].bitcast(f32), ALU.subtract).then_inc(w_low_ready, 1)
                    at["split"] += 1

            def group_done(tiles):
                at["tile"] += tiles
                split_to(at["tile"] + LOOK)
                dve.wait_ge(tile_used, at["tile"])

            def columns(high, low, chunks, c0=0):
                for c in range(0, chunks, 2):
                    at["high"] += 1
                    dve.wait_ge(cols_high, at["high"])
                    dve.tensor_tensor(low[:, c0 + c:c0 + c + 2, :], psum[:, TR + at["col"] % 2, :].rearrange("p (c t) -> p c t", c=2),
                                      high[:, c0 + c:c0 + c + 2, :].bitcast(f32), ALU.subtract).then_inc(cols_drained, 1)
                    at["col"] += 1

            def plain_columns(dst_of, banks):
                for b in range(banks):
                    dve.wait_ge(cols_filled, at["col"] + 1)
                    dst, src = dst_of(b, TR + at["col"] % 2)
                    dve.tensor_copy(dst, src).then_inc(cols_drained, 1)
                    at["col"] += 1

            def pair_of(dst):
                return lambda b, bk: (dst[:, 2 * b:2 * b + 2, :], psum[:, bk, :].rearrange("p (c t) -> p c t", c=2))

            def use_row(name):
                n = row_at[name]
                dve.wait_ge(row_loaded[n % 2], 16 * (n // 2 + 1))
                return row[:, n % 2, :]

            def drop_row(ins):
                ins.then_inc(row_used, 1)

            def rms(src, name, scale_src=None):
                at["sumsq"] += HALVES
                dve.wait_ge(squares_summed, at["sumsq"])
                dve.tensor_scalar(stat[:, 2:4], stat[:, 0:2], 1.0 / D, 1e-6, ALU.mult, ALU.add).then_inc(stat_ready, 1)
                at["stat"] += 1
                dve.wait_ge(root_ready, at["stat"])
                link(dve.reciprocal(stat[:, 4:6], stat[:, 2:4]))
                if name is None:
                    for h in range(HALVES):
                        link(dve.tensor_scalar(src[:, h, :], src[:, h, :], stat[:, 4 + h:5 + h], None, ALU.mult))
                    return
                r = use_row(name)
                for h in range(HALVES):
                    dve.scalar_tensor_tensor(xn[:, h, :], src[:, h, :], stat[:, 4 + h:5 + h], r, ALU.mult, ALU.mult).then_inc(tok_ready, 1)
                    at["tok"] = at.get("tok", 0) + 1
                dve.wait_ge(tok_ready, at["tok"])
                dve.sem_inc(row_used, 1)

            def tok_done(ins):
                at["tok"] = at.get("tok", 0) + 1
                ins.then_inc(tok_ready, 1)

            def tok_signal():
                at["tok"] = at.get("tok", 0) + 1
                dve.sem_inc(tok_ready, 1)

            def mem_rows(i):
                r = use_row(f"mem{i}")
                for h in range(HALVES):
                    tok_done(dve.tensor_tensor(xn[:, h, :], mem[:, h, :], r, ALU.mult))
                dve.wait_ge(tok_ready, at["tok"])
                dve.sem_inc(row_used, 1)

            def drained(ins):
                ins.then_inc(group_drained, 1)
                at["prod"] += 1

            def residual(groups, tiles):
                for g in range(groups):
                    group_done(tiles)
                    par = at["prod"] % 2
                    for h in range(HALVES):
                        cols = x[:, h, g * COLS:(g + 1) * COLS]
                        ins = dve.tensor_tensor(cols, cols, bank(2 * par + h), ALU.add)
                        if h:
                            drained(ins)
                        else:
                            link(ins)
                dve.wait_ge(group_drained, at["prod"])

            def copies(dst, groups, tiles, g0=0):
                for g in range(groups):
                    group_done(tiles)
                    par = at["prod"] % 2
                    for h in range(HALVES):
                        ins = dve.tensor_copy(dst[:, h, (g + g0) * COLS:(g + g0 + 1) * COLS], bank(2 * par + h))
                        drained(ins) if h else link(ins)

            def gated(g, mul_cols, gate_of, dst_of):
                par = at["prod"] % 2
                for h in range(HALVES):
                    at["act"] += 1
                    dve.wait_ge(act_out, at["act"])
                    ins = dve.tensor_tensor(dst_of(h), gate_of(h), psum[:, 2 * par + h, mul_cols:mul_cols + 256], ALU.mult)
                    drained(ins) if h else link(ins)
                dve.wait_ge(group_drained, at["prod"])

            def layer_norm(buf, width, gains, biases):
                for h in range(HALVES):
                    for s in range(width // 512):
                        link(dve.bn_stats(bn[:, h, s, :], buf[:, h, 512 * s:512 * s + 512]))
                    link(dve.bn_aggr(mv[:, h, :], bn[:, h, 0:width // 512, :].rearrange("p s c -> p (s c)")))
                for h in range(HALVES):
                    dve.tensor_scalar(mv[:, h, 1:2], mv[:, h, 1:2], 1e-5, None, ALU.add).then_inc(stat_ready, 1)
                    at["stat"] += 1
                    dve.wait_ge(root_ready, at["stat"])
                    link(dve.reciprocal(stat[:, 6 + h:7 + h], mv[:, h, 1:2]))
                    link(dve.tensor_scalar(buf[:, h, :], buf[:, h, :], mv[:, h, 0:1], stat[:, 6 + h:7 + h], ALU.subtract, ALU.mult))
                for names, op in ((gains, ALU.mult), (biases, ALU.add)):
                    for j, name in enumerate(names):
                        r = use_row(name)
                        for h in range(HALVES):
                            v = buf[:, h, j * D:(j + 1) * D]
                            link(dve.tensor_tensor(v, v, r, op))
                        dve.sem_inc(row_used, 1)

            def conv_mixer():
                plain_columns(lambda b, bk: (taps[:, 4 * b:4 * b + 4, :], psum[:, bk, 0:128].rearrange("p (c t) -> p c t", c=4)), 2)
                for g in range(4):
                    group_done(4)
                    gated(g, 0, lambda h: sig[:, g % 2, h, :], lambda h: z_tok[:, h, 256 * g:256 * g + 256])
                dve.sem_inc(row_used, 2)
                tok_signal()
                plain_columns(lambda b, bk: (zT[:, 2 * b:2 * b + 2, TAPS - 1:TAPS - 1 + T],
                                             psum[:, bk, :].rearrange("p (c t) -> p c t", c=2)), 4)
                dve.wait_ge(cols_drained, at["col"])
                dve.wait_ge(mixer_zero, 2)
                base = at["step"]
                for t in range(TAPS):
                    for c in range(KC):
                        src = zT[:, c, t:t + T]
                        if t:
                            dve.wait_ge(vec_step, base + KC * (t - 1) + c + 1)
                            ins = dve.scalar_tensor_tensor(conv[:, c, :], src, taps[:, c, t:t + 1], conv[:, c, :], ALU.mult, ALU.add)
                        else:
                            ins = dve.tensor_scalar(conv[:, c, :], src, taps[:, c, 0:1], taps[:, c, TAPS:TAPS + 1], ALU.mult, ALU.add)
                        ins.then_inc(vec_step, 1)
                        at["step"] += 1
                dve.wait_ge(vec_step, at["step"])
                tok_signal()
                plain_columns(lambda b, bk: (z_tok[:, b // 2, (b % 2) * 512:(b % 2) * 512 + 512], psum[:, bk, :]), 4)
                dve.wait_ge(cols_drained, at["col"])
                layer_norm(z_tok, D, ["conv_g"], ["conv_b"])
                dve.sem_inc(vec_out, 1)
                at["act"] += 1
                columns(xT_high, xT_low, KC)
                return 2, 4

            def sgu_mixer():
                plain_columns(lambda b, bk: (wsT[:, 4 * b:4 * b + 4, :], psum[:, bk, :].rearrange("p (c t) -> p c t", c=4)) if b < 2
                              else (bsT[:, :], psum[:, bk, 0:8]), 3)
                dve.wait_ge(cols_drained, at["col"])
                for g in range(8):
                    link(dve.tensor_tensor(wsT[:, g, :], wsT[:, g, :], masks[:, M_TRI_ALL, :], ALU.mult))
                for g in range(8):
                    group_done(4)
                    at["act"] += HALVES
                    dve.wait_ge(act_out, at["act"])
                    dve.sem_inc(group_drained, 1)
                    at["prod"] += 1
                    if g % 2:
                        dve.sem_inc(row_used, 1)
                layer_norm(g_tok, E2, ["sgu_g0", "sgu_g1"], ["sgu_b0", "sgu_b1"])
                tok_signal()
                for h in range(HALVES):
                    for gp in range(4):
                        dve.wait_ge(scores_filled, at["score"] + 1)
                        for e in range(2):
                            g = 2 * gp + e
                            u = u_tok[:, h, 256 * g:256 * g + 256]
                            ins = dve.scalar_tensor_tensor(u, psum[:, 6 + at["score"] % 2, 256 * e:256 * e + 256], bsT[:, g:g + 1], u,
                                                           ALU.add, ALU.mult)
                            ins.then_inc(scores_used, 1) if e else link(ins)
                        at["score"] += 1
                columns(yT_high, sgu_low, 2 * KC)
                return 2, 8

            def ret_mixer():
                for j in range(2):
                    copies(qk[j], 2, 4)
                dve.wait_ge(group_drained, at["prod"])
                for g in range(8):
                    group_done(4)
                    at["act"] += HALVES
                    dve.wait_ge(act_out, at["act"])
                    dve.sem_inc(group_drained, 1)
                    at["prod"] += 1
                    if g == 0:
                        dve.wait_ge(mixer_in, 16 * MIXER_LOADS[3])
                    if g < 4:
                        v = qk[g // 2][:, g % 2, :].rearrange("p (a n e) -> p a n e", a=XH, e=2)
                        cos = rotary[:, 0, g % 2, :].unsqueeze(1).to_broadcast([P, XH, HW])
                        sin = rotary[:, 1, g % 2, :].rearrange("p (n e) -> p n e", e=2)
                        for e in range(2):
                            link(dve.tensor_tensor(rtmp[:, :, :, e], v[:, :, :, 1 - e],
                                                   sin[:, :, e].unsqueeze(1).to_broadcast([P, XH, HW // 2]), ALU.mult))
                        flat = qk[g // 2][:, g % 2, :].rearrange("p (a n) -> p a n", a=XH)
                        link(dve.tensor_tensor(flat, flat, cos, ALU.mult))
                        link(dve.tensor_tensor(flat, flat, rtmp[:, :, :, :].rearrange("p a n e -> p a (n e)"), ALU.add))
                tok_signal()
                for j in range(2):
                    plain_columns(pair_of(qkT[j]), 4)
                for hd in range(XH):
                    dve.wait_ge(scores_filled, at["score"] + 1)
                    dve.tensor_tensor(sc[:, hd, :], psum[:, 6 + at["score"] % 2, 0:3 * P], decay[:, hd, :], ALU.mult).then_inc(scores_used, 1)
                    at["score"] += 1
                for h in range(HALVES):
                    for hd in range(XH):
                        dve.wait_ge(square_summed, XH * h + hd + 1)
                        dve.tensor_tensor(o_tok[:, h, 512 * hd:512 * hd + 512], bank(6 + at["score"] % 2),
                                          rg[:, h, 512 * hd:512 * hd + 512], ALU.mult).then_inc(scores_used, 1)
                        at["score"] += 1
                dve.wait_ge(scores_used, at["score"])
                dve.tensor_scalar(small[:, 1, 0:8], small[:, 0, 0:8], 1.0 / 512, 1e-6, ALU.mult, ALU.add).then_inc(stat_ready, 1)
                at["stat"] += 1
                dve.wait_ge(root_ready, at["stat"])
                link(dve.reciprocal(small[:, 2, 0:8], small[:, 1, 0:8]))
                for n in range(HALVES * XH):
                    v = o_tok[:, n // XH, 512 * (n % XH):512 * (n % XH) + 512]
                    link(dve.tensor_scalar(v, v, small[:, 2, n:n + 1], None, ALU.mult))
                tok_signal()
                columns(yT_high, ret_low, 2 * KC)
                return 2, 8

            def lane_take():
                n = at["lane"]
                dve.wait_ge(lane_filled[1], n + 1)
                at["lane"] += 1
                return 4 + n % 4

            def over_heads(m):
                return masks[:, m, :].unsqueeze(1).to_broadcast([P, 4, P])

            def per_head(v):
                return v.unsqueeze(2).to_broadcast([P, NH, HD])

            def by_head(v):
                return v.rearrange("p (h n) -> p h n", h=NH)

            def mixed(m, dst):
                for c in range(KC):
                    last = dve.scalar_tensor_tensor(dst[:, c, :], diff[:, c, :], taps[:, c, m:m + 1], hT[:, c, 1:T + 1], ALU.mult, ALU.add)
                link(last)

            def rwkv_mixer():
                link(dve.memset(hT[:, :, 0:1], 0.0))
                plain_columns(lambda b, bk: (hT[:, 2 * b:2 * b + 2, 1:T + 1], psum[:, bk, :].rearrange("p (c t) -> p c t", c=2)), 4)
                plain_columns(lambda b, bk: (taps[:, :, 0:6], psum[:, bk, 0:48].rearrange("p (c t) -> p c t", c=KC)), 1)
                dve.wait_ge(cols_drained, at["col"])
                link(dve.tensor_tensor(diff[:, :, :], hT[:, :, 0:T], hT[:, :, 1:T + 1], ALU.subtract))
                lora_acts = 0
                for j, m in enumerate((1, 4, 5)):
                    if j == 2:
                        dve.wait_ge(lane_used[0], 1)
                    mixed(m, (xs, xs_b, xs)[j])
                    tok_signal()
                dve.wait_ge(lane_used[0], 16)
                dve.sem_inc(row_used, 2)
                for m, src in enumerate((0, 2, 3)):
                    buf = (xs, xs_b, xs)[m]
                    mixed(src, buf)
                    if m:
                        dve.wait_ge(tile_used, at["tile"])
                    dve.sem_inc(vec_out, 1)
                    at["act"] += 1
                    dve.wait_ge(act_out, at["act"])
                    link(dve.tensor_tensor(xT_low[:, :, :], buf[:, :, :], xT_high[:, :, :].bitcast(f32), ALU.subtract))
                    tok_signal()
                    copies((rr, rk, rvv)[m], 2, 4)
                dve.wait_ge(group_drained, at["prod"])
                r = use_row("k_k")
                for h in range(HALVES):
                    link(dve.tensor_tensor(kk[:, h, :], rk[:, h, :], r, ALU.mult))
                    link(dve.tensor_tensor(tmp[0][:, :], kk[:, h, :], kk[:, h, :], ALU.mult))
                    dve.tensor_reduce(small[:, 1, :], by_head(tmp[0][:, :]), AX.X, ALU.add).then_inc(stat_ready, 1)
                    at["stat"] += 1
                    dve.wait_ge(root_ready, at["stat"])
                    link(dve.tensor_scalar(small[:, 1, :], small[:, 1, :], 1e-12, None, ALU.max))
                    link(dve.reciprocal(small[:, 2, :], small[:, 1, :]))
                    link(dve.tensor_tensor(by_head(kk[:, h, :]), by_head(kk[:, h, :]), per_head(small[:, 2, :]), ALU.mult))
                dve.sem_inc(row_used, 1)
                r = use_row("k_a")
                for h in range(HALVES):
                    link(dve.scalar_tensor_tensor(tmp[0][:, :], ra[:, h, :], -1.0, r, ALU.add, ALU.mult))
                    link(dve.scalar_tensor_tensor(rk[:, h, :], tmp[0][:, :], 1.0, rk[:, h, :], ALU.add, ALU.mult))
                dve.sem_inc(row_used, 1)
                r = use_row("r_k")
                for h in range(HALVES):
                    link(dve.tensor_tensor(tmp[0][:, :], rr[:, h, :], rk[:, h, :], ALU.mult))
                    link(dve.tensor_tensor(tmp[0][:, :], tmp[0][:, :], r, ALU.mult))
                    link(dve.tensor_reduce(small[:, 4 + h, :], by_head(tmp[0][:, :]), AX.X, ALU.add))
                    link(dve.tensor_tensor(ra[:, h, :], ra[:, h, :], kk[:, h, :], ALU.mult))
                    link(dve.tensor_scalar(lw[:, h, :], lw[:, h, :], -float(np.exp(-0.5)), None, ALU.mult))
                dve.sem_inc(row_used, 1)
                tok_signal()
                for h in range(HALVES):
                    for n in range(2):
                        b = lane_take()
                        cols = slice(COLS * n, COLS * n + COLS)
                        at["act"] += 2
                        dve.wait_ge(act_out, at["act"])
                        dve.tensor_tensor(tmp[2][:, 0:COLS], bank(b), lw[:, h, cols], ALU.subtract).then_inc(lane_used[1], 1)
                        link(dve.tensor_tensor(rr[:, h, cols], rr[:, h, cols], tmp[0][:, 0:COLS], ALU.mult))
                        link(dve.tensor_tensor(rk[:, h, cols], rk[:, h, cols], tmp[1][:, 0:COLS], ALU.mult))
                        link(dve.tensor_tensor(ra[:, h, cols], ra[:, h, cols], tmp[1][:, 0:COLS], ALU.mult))
                        at["act"] += 1
                        dve.wait_ge(act_out, at["act"])
                        link(dve.scalar_tensor_tensor(kk[:, h, cols], kk[:, h, cols], -1.0, tmp[2][:, 0:COLS], ALU.mult, ALU.mult))
                        if 2 * h + n < 3:
                            dve.sem_inc(vec_out, 1)
                dve.wait_ge(lane_used[0], 17)
                link(dve.memset(state[:, :, :], 0.0))
                tok_signal()
                heads = lambda b: psum[:, b, :].rearrange("p (h t) -> p h t", h=4)
                for h in range(HALVES):
                    for hg in range(2):
                        if h or hg:
                            dve.wait_ge(lane_used[0], 17 + 13 * (2 * h + hg))
                        for sb in range(2):
                            hs = slice(4 * sb, 4 * sb + 4)
                            for dst, m in ((abT, M_STRICT), (akT, M_STRICT), (rbT, M_INCL), (rkT, M_INCL)):
                                b = lane_take()
                                dve.tensor_tensor(dst[:, hs, :], heads(b), over_heads(m), ALU.mult).then_inc(lane_used[1], 1)
                            b = lane_take()
                            dve.tensor_tensor(inv[:, hs, :], heads(b), over_heads(M_LEVEL), ALU.mult).then_inc(lane_used[1], 1)
                            dve.wait_ge(lane_used[1], at["lane"])
                            link(dve.tensor_tensor(inv[:, hs, :], inv[:, hs, :], over_heads(M_IDENT), ALU.add))
                            link(dve.tensor_tensor(invT[:, hs, :], abT[:, hs, :], over_heads(M_PAIR_T), ALU.mult))
                            link(dve.tensor_tensor(invT[:, hs, :], invT[:, hs, :], over_heads(M_IDENT), ALU.add))
                            tok_signal()
                        for level in range(1, LEVELS):
                            for sb in range(2):
                                b = lane_take()
                                dve.tensor_tensor(lvl[:, 4 * sb:4 * sb + 4, :], heads(b), over_heads(M_LEVEL + level), ALU.mult).then_inc(lane_used[1], 1)
                            for sb in range(2):
                                for dst in ((inv, invT) if level < LEVELS - 1 else (invT,)):
                                    b = lane_take()
                                    d = dst[:, 4 * sb:4 * sb + 4, :]
                                    dve.tensor_tensor(d, heads(b), d, ALU.add).then_inc(lane_used[1], 1)
                        for c in range(2):
                            rs = slice(CH * c, CH * c + CH)
                            b = lane_take()
                            dve.wait_ge(lane_used[0], 17 + 13 * (2 * h + hg) + 12)
                            dve.tensor_tensor(uu[rs, :, :], psum[rs, b, :].rearrange("p (h n) -> p h n", h=8), zz[rs, :, :], ALU.add).then_inc(lane_used[1], 1)
                            b = lane_take()
                            st = state[:, 8 * hg:8 * hg + 8, :]
                            link(dve.tensor_tensor(st, psum[0:HD, b, :].rearrange("p (h n) -> p h n", h=8), st, ALU.add))
                            dve.tensor_tensor(st, st, pc[:, h, 8 * hg:8 * hg + 8, c:c + 1].to_broadcast([HD, 8, HD]), ALU.mult).then_inc(lane_used[1], 1)
                dve.wait_ge(lane_used[0], 17 + 13 * 4)
                for h in range(HALVES):
                    y = by_head(rr[:, h, :])
                    t = by_head(tmp[3][:, :])
                    link(dve.tensor_reduce(small[:, 1, :], y, AX.X, ALU.add))
                    link(dve.tensor_scalar(small[:, 1, :], small[:, 1, :], 1.0 / HD, None, ALU.mult))
                    link(dve.tensor_tensor(y, y, per_head(small[:, 1, :]), ALU.subtract))
                    link(dve.tensor_tensor(t, y, y, ALU.mult))
                    link(dve.tensor_reduce(small[:, 2, :], t, AX.X, ALU.add))
                    dve.tensor_scalar(small[:, 3, :], small[:, 2, :], 1.0 / HD, HD * 1e-5, ALU.mult, ALU.add).then_inc(stat_ready, 1)
                    at["stat"] += 1
                    dve.wait_ge(root_ready, at["stat"])
                    link(dve.reciprocal(small[:, 3, :], small[:, 3, :]))
                    link(dve.tensor_tensor(y, y, per_head(small[:, 3, :]), ALU.mult))
                for name, op in (("gn_g", ALU.mult), ("gn_b", ALU.add)):
                    r = use_row(name)
                    for h in range(HALVES):
                        link(dve.tensor_tensor(rr[:, h, :], rr[:, h, :], r, op))
                    dve.sem_inc(row_used, 1)
                for h in range(HALVES):
                    link(dve.tensor_tensor(by_head(tmp[3][:, :]), by_head(rvv[:, h, :]), per_head(small[:, 4 + h, :]), ALU.mult))
                    link(dve.tensor_tensor(rr[:, h, :], rr[:, h, :], tmp[3][:, :], ALU.add))
                    link(dve.tensor_tensor(rr[:, h, :], rr[:, h, :], rgate[:, h, :], ALU.mult))
                tok_signal()
                columns(xT_high, xT_low, KC)
                return 2, 4

            dve.wait_ge(x_loaded, 32)
            rms(mem, None)
            for i in range(layers):
                split_to(at["tile"] + LOOK)
                rms(x, f"mix{i}")
                if i != 1:
                    columns(xT_high, xT_low, KC)
                groups, tiles = [conv_mixer, rwkv_mixer, sgu_mixer, ret_mixer][i]()
                mem_rows(i)
                columns(memT_high, memT_low, KC)
                if i == 0:
                    use_row("conv_bo")
                residual(groups, tiles)
                if i == 0:
                    dve.sem_inc(row_used, 1)
                rms(x, f"xattn{i}")
                for g in range(4):
                    if g < 2:
                        group_done(4)
                        par = at["prod"] % 2
                        for h in range(HALVES):
                            ins = dve.tensor_copy(k_tok[:, g, h, :], bank(2 * par + h))
                            drained(ins) if h else link(ins)
                    else:
                        copies(v_tok, 1, 4, g - 2)
                plain_columns(pair_of(kT), 4)
                columns(xT_high, xT_low, KC)
                copies(q_tok, 2, 4)
                plain_columns(pair_of(qT), 4)
                for h in range(HALVES):
                    for hp in range(XH // 2):
                        dve.wait_ge(scores_filled, at["score"] + 1)
                        j = h * XH + 2 * hp
                        link(dve.tensor_reduce(den[:, 2, j:j + 2], psum[:, 6 + at["score"] % 2, :].rearrange("p (e t) -> p e t", e=2), AX.X, ALU.max))
                        dve.tensor_scalar(den[:, 0, j:j + 2], den[:, 2, j:j + 2], -float(HW) ** -0.5, None, ALU.mult).then_inc(neg_max, 1)
                        at["score"] += 1
                        at["exp"] += 2
                        dve.wait_ge(exp_done, at["exp"])
                        dve.sem_inc(scores_used, 1)
                        link(dve.reciprocal(den[:, 2, j:j + 2], den[:, 1, j:j + 2]))
                        for e in range(2):
                            v = prob[:, h, 2 * hp + e, :]
                            tok_done(dve.tensor_scalar(v, v, den[:, 2, j + e:j + e + 1], None, ALU.mult))
                plain_columns(lambda b, bk: (probT[:, b, :, :], psum[:, bk, :].rearrange("p (c t) -> p c t", c=2)), 4)
                for c in range(XH):
                    at["high"] += 1
                    dve.wait_ge(cols_high, at["high"])
                    dve.tensor_tensor(xT_low[:, 2 * c:2 * c + 2, :], psum[:, 6 + at["score"] % 2, :].rearrange("p (c t) -> p c t", c=2),
                                      xT_high[:, 2 * c:2 * c + 2, :].bitcast(f32), ALU.subtract).then_inc(scores_used, 1)
                    at["score"] += 1
                residual(2, 4)
                rms(x, f"ffn{i}")
                columns(xT_high, xT_low, KC)
                for g in range(11):
                    group_done(4)
                    gated(g, 256, lambda h: sgate[:, g % 2, h, :], lambda h: htok[:, g % 2, h, :])
                    if g:
                        columns(hT_high, hT_low, 2, 2 * (g - 1))
                columns(hT_high, hT_low, 2, 20)
                residual(2, 11)
                dve.sem_inc(mixer_free, 1)
            rms(x, "final")
            dve.sem_inc(result_ready, 1)

        @block.tensor
        def _(pe):
            at = dict(plan=0, prod=0, tile=0, col=0, score=0, tok=0)

            def product(name, high, low, groups, bias=None):
                p = plan[at["plan"]]
                if groups[-1] == p["groups"] - 1:
                    at["plan"] += 1
                assert p["name"] == name, (p["name"], name)
                pe.wait_ge(cols_drained, at["col"])
                for g in groups:
                    par = at["prod"] % 2
                    if at["prod"] >= 2:
                        pe.wait_ge(group_drained, at["prod"] - 1)
                    if bias:
                        for h in range(HALVES):
                            for b, (rhs, c0, c1) in enumerate(bias(g)):
                                pe.matmul(psum[:, 2 * par + h, c0:c1], ones[0:1, :], rhs, start=(b == 0), stop=False, skip_group_check=True)
                    for kt in range(p["tiles"]):
                        t = at["tile"]
                        pe.wait_ge(w_low_ready, t + 1)
                        for k in range(2):
                            for h in range(HALVES):
                                c = 2 * kt + k
                                first = c == 0 and not bias
                                last = c == 2 * p["tiles"] - 1
                                xh, xl = high[:, c, h * P:(h + 1) * P], low[:, c, h * P:(h + 1) * P]
                                wh, wl = w_high[:, t % SPLIT, k, :], w_low[:, t % SPLIT, k, :]
                                o = bank(2 * par + h)
                                skip = bool(bias)
                                pe.matmul(o, xh, wh, start=first, stop=False, skip_group_check=skip)
                                pe.matmul(o, xh, wl, start=False, stop=False, skip_group_check=skip)
                                mm = pe.matmul(o, xl, wh, start=False, stop=last, skip_group_check=skip)
                        mm.then_inc(tile_used, 1)
                        at["tile"] += 1
                    at["prod"] += 1

            def transposes(src, banks, tok=0):
                at["tok"] += tok
                if at["tok"]:
                    pe.wait_ge(tok_ready, at["tok"])
                for b in range(banks):
                    n = at["col"]
                    if n >= 2:
                        pe.wait_ge(cols_drained, n - 1)
                    for off, v in src(b):
                        rows_, cols_ = v.shape
                        mm = pe.transpose(psum[0:cols_, TR + n % 2, off:off + rows_], v, ident[0:rows_, 0:rows_])
                    mm.then_inc(cols_filled, 1)
                    at["col"] += 1

            def two_chunks(buf, c0=0):
                return lambda b: [(256 * e + P * h, buf[:, h, (c0 + 2 * b + e) * P:(c0 + 2 * b + e + 1) * P])
                                  for e in range(2) for h in range(HALVES)]

            def row_ready(name):
                n = row_at[name]
                pe.wait_ge(row_loaded[n % 2], 16 * (n // 2 + 1))

            def brow(name, lo, n):
                return row[0:1, row_at[name] % 2, lo:lo + n]

            def conv_mixer():
                pe.wait_ge(mixer_in, 32)
                transposes(lambda b: [(32 * e, dw_tok[:, (4 * b + e) * P:(4 * b + e + 1) * P]) for e in range(4)], 2)
                row_ready("b_a")
                row_ready("b_gate")
                product("conv_in", xT_high, xT_low, range(4),
                        lambda g: [(brow("b_a", 256 * g, 256), 0, 256), (brow("b_gate", 256 * g, 256), 256, 512)])
                transposes(two_chunks(z_tok), 4, 1)
                transposes(lambda b: [(P * e, conv[:, 4 * (b % 2) + e, (b // 2) * P:(b // 2 + 1) * P]) for e in range(4)], 4, 1)
                pe.wait_ge(act_out, 9)
                transposes(two_chunks(z_tok), 4)

            def sgu_mixer():
                pe.wait_ge(mixer_in, 16 * MIXER_LOADS[2])
                transposes(lambda b: [(P * e, ws_in[:, 4 * b + e, :]) for e in range(4)] if b < 2 else [(0, bs_in[:, :])], 3)
                for g in range(8):
                    name = f"sgu_bias{g // 2}"
                    row_ready(name)
                    product("sgu_in", xT_high, xT_low, [g], lambda g: [(brow(f"sgu_bias{g // 2}", COLS * (g % 2), COLS), 0, COLS)])
                at["tok"] += 1
                pe.wait_ge(tok_ready, at["tok"])
                for h in range(HALVES):
                    for gp in range(4):
                        n = at["score"]
                        pe.wait_ge(scores_used, n - 1)
                        for e in range(2):
                            g = 2 * gp + e
                            mm = pe.matmul(psum[:, 6 + n % 2, 256 * e:256 * e + 256], wsT[:, g, :], g_tok[:, h, 256 * g:256 * g + 256],
                                           start=True, stop=True)
                        mm.then_inc(scores_filled, 1)
                        at["score"] += 1
                pe.wait_ge(scores_used, at["score"])
                transposes(two_chunks(u_tok), 8)

            def ret_mixer():
                product("ret_in", xT_high, xT_low, range(12))
                for j in range(2):
                    transposes(two_chunks(qk[j]), 4, 1 - j)
                pe.wait_ge(cols_drained, at["col"])
                for hd in range(XH):
                    n = at["score"]
                    pe.wait_ge(scores_used, n - 1)
                    for s_, t0, c0 in ((0, 0, 0), (1, P, 2 * P)):
                        for c in range(2):
                            mm = pe.matmul(psum[:, 6 + n % 2, c0:c0 + T - t0], qkT[1][:, 2 * hd + c, s_ * P:(s_ + 1) * P],
                                           qkT[0][:, 2 * hd + c, t0:T], start=(c == 0), stop=(c == 1))
                    mm.then_inc(scores_filled, 1)
                    at["score"] += 1
                decayed = at["score"]
                for h in range(HALVES):
                    for hd in range(XH):
                        n = at["score"]
                        pe.wait_ge(scores_used, n - 1 if h or hd > 1 else decayed)
                        v = [rv[:, s_, 512 * hd:512 * hd + 512] for s_ in range(2)]
                        if h == 0:
                            mm = pe.matmul(bank(6 + n % 2), sc[:, hd, 0:P], v[0], start=True, stop=True)
                        else:
                            pe.matmul(bank(6 + n % 2), sc[:, hd, P:2 * P], v[0], start=True, stop=False)
                            mm = pe.matmul(bank(6 + n % 2), sc[:, hd, 2 * P:3 * P], v[1], start=False, stop=True)
                        mm.then_inc(scores_filled, 1)
                        at["score"] += 1
                transposes(two_chunks(o_tok), 8, 1)

            lanes = [0, 0]

            def lane_bank(j):
                n = lanes[j]
                if n >= 4:
                    pe.wait_ge(lane_used[j], n - 3)
                return 4 * j + n % 4

            def lane_done(j, mm):
                mm.then_inc(lane_filled[j], 1)
                lanes[j] += 1
                return lanes[j]

            def lane_ready(j, n):
                pe.wait_ge(lane_used[j], n)

            def rwkv_mixer():
                transposes(lambda b: two_chunks(xn)(b), 4, HALVES)
                pe.wait_ge(mixer_in, 16 * MIXER_LOADS[1])
                transposes(lambda b: [(6 * e, mix_in[:, e * P:(e + 1) * P]) for e in range(KC)], 1)
                pe.wait_ge(group_drained, at["prod"])
                pe.wait_ge(cols_drained, at["col"])
                pe.wait_ge(scores_used, at["score"])
                for j, (m, width) in enumerate(((1, 64), (4, 64), (5, P))):
                    at["tok"] += 1
                    pe.wait_ge(tok_ready, at["tok"])
                    src = (xs, xs_b, xs)[j]
                    hid = [(lora[j], 0, width)] + ([(lora[0], P, 32)] if j == 2 else [])
                    for buf, o, k in hid:
                        b = lane_bank(0)
                        for c in range(KC):
                            mm = pe.matmul(psum[0:k, b, 0:T], lora1[j][:, c, o:o + k], src[:, c, :], start=(c == 0), stop=(c == KC - 1))
                        ready = lane_done(0, mm)
                    lane_ready(0, ready)
                    if j < 2:
                        row_ready(("w0", "a0")[j])
                    for h in range(HALVES):
                        for n in range(2):
                            b = lane_bank(0)
                            cols = slice(COLS * n, COLS * n + COLS)
                            if j < 2:
                                pe.matmul(bank(b), ones[0:1, :], brow(("w0", "a0")[j], COLS * n, COLS), start=True, stop=False)
                                mm = pe.matmul(bank(b), lora[j][0:64, h * P:(h + 1) * P], lora2[j][:, cols], start=False, stop=True)
                            else:
                                pe.matmul(bank(b), lora[2][:, h * P:(h + 1) * P], lora2[2][:, cols], start=True, stop=False)
                                mm = pe.matmul(bank(b), lora[0][0:32, h * P:(h + 1) * P], lora2[3][:, cols], start=False, stop=True)
                            lane_done(0, mm)
                lane_ready(0, lanes[0])
                for m in range(3):
                    at["tok"] += 1
                    pe.wait_ge(tok_ready, at["tok"])
                    product("rkv", xT_high, xT_low, range(2))
                at["tok"] += 1
                pe.wait_ge(tok_ready, at["tok"])
                pe.wait_ge(group_drained, at["prod"])
                for h in range(HALVES):
                    for n in range(2):
                        b = lane_bank(1)
                        mm = pe.matmul(bank(b), masks[:, M_CUM, :], lw[:, h, COLS * n:COLS * n + COLS], start=True, stop=True)
                        lane_done(1, mm)
                b = lane_bank(0)
                for h in range(HALVES):
                    for n in range(NH):
                        o = (h * NH + n) * 2
                        mm = pe.matmul(psum[0:HD, b, o:o + 2], lw[:, h, HD * n:HD * n + HD], masks[:, M_CHUNK, 0:2], start=True, stop=True)
                lane_done(0, mm)
                at["tok"] += 1
                pe.wait_ge(tok_ready, at["tok"])
                for h in range(HALVES):
                    for hg in range(2):
                        def head(buf, n):
                            return buf[:, h, 512 * hg + HD * n:512 * hg + HD * n + HD]

                        for src in (kk, ra, rk, rr):
                            for sb in range(2):
                                b = lane_bank(0)
                                for e in range(4):
                                    mm = pe.transpose(psum[0:HD, b, P * e:P * e + P], head(src, 4 * sb + e), ident)
                                ready = lane_done(0, mm)
                        lane_ready(0, ready)
                        for sb in range(2):
                            for l, r in ((bT, aT), (kkT, aT), (bT, rT), (kkT, rT), (aT, bT)):
                                b = lane_bank(1)
                                for e in range(4):
                                    n = 4 * sb + e
                                    mm = pe.matmul(psum[:, b, P * e:P * e + P], l[:, n, :], r[:, n, :], start=True, stop=True)
                                lane_done(1, mm)
                        at["tok"] += 2
                        pe.wait_ge(tok_ready, at["tok"])
                        inv_at = [[lanes[1]] * 2, [lanes[1]] * 2]
                        for level in range(1, LEVELS):
                            q_at = []
                            for sb in range(2):
                                lane_ready(1, inv_at[sb][0])
                                b = lane_bank(1)
                                for e in range(4):
                                    n = 4 * sb + e
                                    mm = pe.matmul(psum[:, b, P * e:P * e + P], abT[:, n, :], inv[:, n, :], start=True, stop=True)
                                q_at.append(lane_done(1, mm))
                            for sb in range(2):
                                lane_ready(1, q_at[sb])
                                for which in ((0, 1) if level < LEVELS - 1 else (1,)):
                                    b = lane_bank(1)
                                    for e in range(4):
                                        n = 4 * sb + e
                                        l, r = (invT, lvl) if which == 0 else (lvl, invT)
                                        mm = pe.matmul(psum[:, b, P * e:P * e + P], l[:, n, :], r[:, n, :], start=True, stop=True)
                                    inv_at[sb][which] = lane_done(1, mm)
                        lane_ready(1, lanes[1])
                        for sb in range(2):
                            b = lane_bank(0)
                            for e in range(4):
                                n = 4 * sb + e
                                mm = pe.matmul(psum[0:HD, b, P * e:P * e + P], head(kk, n), invT[:, n, :], start=True, stop=True)
                            lane_done(0, mm)
                        for l, r in ((akT, lambda n: head(rvv, n)), (invT, lambda n: hh[:, n, :])):
                            b = lane_bank(0)
                            for n in range(8):
                                mm = pe.matmul(psum[:, b, HD * n:HD * n + HD], l[:, n, :], r(n), start=True, stop=True)
                            ready = lane_done(0, mm)
                            lane_ready(0, ready)
                        yb = lane_bank(0)
                        for n in range(8):
                            pe.matmul(psum[:, yb, HD * n:HD * n + HD], rkT[:, n, :], head(rvv, n), start=(n == 0), stop=False, skip_group_check=True)
                        for c in range(2):
                            rs = slice(CH * c, CH * c + CH)
                            b = lane_bank(1)
                            for n in range(8):
                                mm = pe.matmul(psum[rs, b, HD * n:HD * n + HD], wT[:, n, rs], state[:, 8 * hg + n, :], start=True, stop=True)
                            u_at = lane_done(1, mm)
                            for n in range(8):
                                pe.matmul(psum[rs, yb, HD * n:HD * n + HD], rT[:, n, rs], state[:, 8 * hg + n, :], start=False, stop=False,
                                          skip_group_check=True)
                            lane_ready(1, u_at)
                            b = lane_bank(1)
                            for n in range(8):
                                pe.matmul(psum[0:HD, b, HD * n:HD * n + HD], head(ra, n)[rs, :], uu[rs, n, :], start=True, stop=False)
                                mm = pe.matmul(psum[0:HD, b, HD * n:HD * n + HD], head(rk, n)[rs, :], head(rvv, n)[rs, :], start=False, stop=True)
                            s_at = lane_done(1, mm)
                            lane_ready(1, s_at)
                        for n in range(8):
                            mm = pe.matmul(psum[:, yb, HD * n:HD * n + HD], rbT[:, n, :], uu[:, n, :], start=False, stop=(n == 7), skip_group_check=True)
                        ready = lane_done(0, mm)
                        lane_ready(0, ready)
                lane_ready(1, lanes[1])
                transposes(two_chunks(rr), 4, 1)

            pe.wait_ge(const_loaded, 16)
            pe.wait_ge(mixer_zero, 1)
            for i in range(layers):
                if i != 1:
                    transposes(two_chunks(xn), 4, HALVES)
                [conv_mixer, rwkv_mixer, sgu_mixer, ret_mixer][i]()
                transposes(two_chunks(xn), 4, HALVES)
                if i == 0:
                    row_ready("conv_bo")
                    product("conv_out", xT_high, xT_low, range(2), lambda g: [(brow("conv_bo", COLS * g, COLS), 0, COLS)])
                if i == 1:
                    product("rwkv_out", xT_high, xT_low, range(2))
                if i == 2:
                    product("sgu_out", yT_high, sgu_low, range(2))
                if i == 3:
                    product("ret_out", yT_high, ret_low, range(2))
                product("kv", memT_high, memT_low, range(4))
                pe.wait_ge(group_drained, at["prod"] - 2)
                transposes(lambda b: [(256 * e + P * h, k_tok[:, b // 2, h, (2 * (b % 2) + e) * P:(2 * (b % 2) + e + 1) * P])
                                      for e in range(2) for h in range(HALVES)], 4)
                transposes(two_chunks(xn), 4, HALVES)
                product("q", xT_high, xT_low, range(2))
                pe.wait_ge(group_drained, at["prod"])
                transposes(two_chunks(q_tok), 4)
                pe.wait_ge(cols_drained, at["col"])
                for h in range(HALVES):
                    for hp in range(XH // 2):
                        n = at["score"]
                        if n >= 2:
                            pe.wait_ge(scores_used, n - 1)
                        for e in range(2):
                            hd = 2 * hp + e
                            for c in range(2):
                                mm = pe.matmul(psum[:, 6 + n % 2, e * T:(e + 1) * T], qT[:, 2 * hd + c, h * P:(h + 1) * P],
                                               kT[:, 2 * hd + c, :], start=(c == 0), stop=(c == 1))
                        mm.then_inc(scores_filled, 1)
                        at["score"] += 1
                transposes(lambda b: [(256 * m + P * h, prob[:, h, b, m * P:(m + 1) * P]) for m in range(2) for h in range(HALVES)],
                           4, HALVES * XH)
                pe.wait_ge(cols_drained, at["col"])
                for hd in range(XH):
                    n = at["score"]
                    pe.wait_ge(scores_used, n - 1)
                    for e in range(2):
                        c = 2 * hd + e
                        for m in range(2):
                            mm = pe.matmul(psum[:, 6 + n % 2, e * T:(e + 1) * T], v_tok[:, m, c * P:(c + 1) * P],
                                           probT[:, hd, m, :], start=(m == 0), stop=(m == 1))
                    mm.then_inc(scores_filled, 1)
                    at["score"] += 1
                pe.wait_ge(scores_used, at["score"])
                product("wo", xT_high, xT_low, range(2))
                transposes(two_chunks(xn), 4, HALVES)
                for g in range(11):
                    product("gate_up", xT_high, xT_low, [g])
                    if g:
                        pe.wait_ge(group_drained, at["prod"] - 1)
                        transposes(lambda b: [(256 * e + P * h, htok[:, (g - 1) % 2, h, e * P:(e + 1) * P])
                                              for e in range(2) for h in range(HALVES)], 1)
                pe.wait_ge(group_drained, at["prod"])
                transposes(lambda b: [(256 * e + P * h, htok[:, 0, h, e * P:(e + 1) * P])
                                      for e in range(2) for h in range(HALVES)], 1)
                product("down", hT_high, hT_low, range(2))


def kernel(**inputs):
    import concourse.bacc as _bacc
    from concourse import mybir as _mybir
    from concourse.bass_utils import run_bass_kernel_spmd as _run

    arrays = {f"in_{name}": np.ascontiguousarray(a) for name, a in inputs.items()}
    arrays["in_masks"] = constant_masks()
    arrays["in_rotary"] = rotary_tables()
    arrays["in_decay"] = decay_masks()
    nc = _bacc.Bacc("TRN2", target_bir_lowering=False, num_devices=1)
    w = {name[3:]: nc.dram_tensor(name, a.shape, _mybir.dt.from_np(a.dtype), kind="ExternalInput").ap()
         for name, a in arrays.items()}
    out = nc.dram_tensor("out", (1, T, D), _mybir.dt.float32, kind="ExternalOutput").ap()
    trunk_program(nc, w, out, 4)
    return _run(nc, [arrays], core_ids=[0]).results[0]["out"]
```

```python
import numpy as np
import concourse.bass as bass
from concourse import mybir

P = 128
D = 1024
T = 256
HALVES = T // P
KC = D // P
COLS = 512
F = 2816
FC = F // P
E2 = 2 * D
TAPS = 31
HD = 64
NH = D // HD
CH = 64
XH = 4
HW = D // XH
RAW, SPLIT, LOOK = 4, 8, 4
CONV_DVE = 5
MIXER_LOADS = [2, 10, 12, 15]

M_IDENT, M_CUM, M_STRICT, M_INCL, M_PAIR_T, M_LEVEL = 0, 1, 2, 3, 4, 5
LEVELS = 6
M_CHUNK = M_LEVEL + LEVELS
M_TRI_ALL = M_CHUNK + 1
N_MASKS = M_TRI_ALL + 1


def constant_masks():
    r = np.arange(P)[:, None]
    c = np.arange(P)[None, :]
    same = (r // CH) == (c // CH)
    m = np.zeros((N_MASKS, P, P), np.float32)
    m[M_IDENT] = r == c
    m[M_CUM] = same & (r <= c)
    m[M_STRICT] = same & (r < c)
    m[M_INCL] = same & (r <= c)
    for n in range(LEVELS):
        b = 1 << n
        m[M_LEVEL + n] = ((r // (2 * b)) == (c // (2 * b))) & ((r // b) % 2 == 1) & ((c // b) % 2 == 0)
    m[M_PAIR_T] = m[M_LEVEL].T
    m[M_CHUNK][:, 0] = (np.arange(P) < CH)
    m[M_CHUNK][:, 1] = (np.arange(P) >= CH)
    m[M_TRI_ALL] = r <= c
    return np.ascontiguousarray(m.transpose(1, 0, 2).reshape(P, N_MASKS * P))


def rotary_tables():
    angle = np.repeat(np.float32(1.0) / (np.float32(10000.0) ** np.linspace(0.0, 1.0, HW // 2, dtype=np.float32)), 2)
    theta = np.arange(T, dtype=np.float32)[:, None] * angle.astype(np.float32)[None]
    sin = np.sin(theta).astype(np.float32)
    sin[:, 0::2] *= -1.0
    return np.stack([np.cos(theta).astype(np.float32), sin])


def decay_masks():
    lg = np.log(1.0 - 2.0 ** (-5.0 - np.arange(XH, dtype=np.float64)))
    s = np.arange(P)[:, None]
    t = np.arange(P)[None, :]
    out = np.zeros((P, XH, 3, P), np.float64)
    for h in range(XH):
        out[:, h, 0] = np.where(t >= s, np.exp(lg[h] * np.maximum(t - s, 0)), 0.0)
        out[:, h, 1] = np.exp(lg[h] * (t + P - s))
        out[:, h, 2] = out[:, h, 0]
    return (out * HW ** -0.5).astype(np.float32).reshape(P, XH * 3 * P)


def weight_plan(w, layers):
    plan = []

    def product(name, src, rows, cols, paired=False):
        plan.append(dict(name=name, src=src, tiles=rows // 256, groups=cols // COLS, paired=paired))

    for i in range(layers):
        if i == 0:
            product("conv_in", w["conv_w_in"][0], D, 2 * D, True)
            product("k", w["xattn_wkv"][i, :, 0:D], D, D)
            product("conv_out", w["conv_w_out"][0], D, D)
        if i == 1:
            for m in range(3):
                product("rkv", w["rwkv_w_rkv"][0, m], D, D)
            product("rwkv_out", w["rwkv_w_o"][0], D, D)
        if i == 2:
            product("sgu_in", w["sgu_w_in"][0], D, 2 * E2)
            product("sgu_out", w["sgu_w_out"][0], E2, D)
        if i == 3:
            product("ret_in", w["ret_w_in"][0], D, 6 * D)
            product("ret_out", w["ret_w_out"][0], E2, D)
        if i:
            product("k", w["xattn_wkv"][i, :, 0:D], D, D)
        product("q", w["xattn_wq"][i], D, D)
        product("v", w["xattn_wkv"][i, :, D:2 * D], D, D)
        product("wo", w["xattn_wo"][i], D, D)
        product("gate_up", w["ffn_w_gate_up"][i], D, 2 * F, True)
        product("down", w["ffn_w_down"][i], F, D)
    tile = group = 0
    for p in plan:
        p["tile0"], p["group0"] = tile, group
        tile += p["tiles"] * p["groups"]
        group += p["groups"]
    return plan


def row_plan(w, layers):
    rows = []
    for i in range(layers):
        rows.append((f"mix{i}", w["mix_norm_g"][i:i + 1, :], True))
        if i in (0, 2):
            rows.append((f"mem{i}", w["mem_norm_g"][i:i + 1, :], True))
        if i == 0:
            b = w["conv_b_in"]
            rows += [("b_a", b[:, 0:D], False), ("b_gate", b[:, D:2 * D], False),
                     ("conv_g", w["conv_ln_g"], True), ("conv_b", w["conv_ln_b"], True)]
        if i == 1:
            rows += [("w0", w["rwkv_w0"], False), ("a0", w["rwkv_a0"], False)]
            rows += [(n, w["rwkv_" + n] if n != "r_k" else w["rwkv_r_k"].rearrange("a h n -> a (h n)"), True)
                     for n in ("k_k", "k_a", "r_k", "gn_g", "gn_b")]
        if i == 2:
            rows += [(f"sgu_bias{j}", w["sgu_b_in"][:, j * D:(j + 1) * D], False) for j in range(4)]
            rows += [(f"sgu_g{j}", w["sgu_ln_g"][:, j * D:(j + 1) * D], True) for j in range(2)]
            rows += [(f"sgu_b{j}", w["sgu_ln_b"][:, j * D:(j + 1) * D], True) for j in range(2)]
        if i in (1, 3):
            rows.append((f"mem{i}", w["mem_norm_g"][i:i + 1, :], True))
        if i == 0:
            rows.append(("conv_bo", w["conv_b_out"], False))
        rows.append((f"xattn{i}", w["xattn_norm_g"][i:i + 1, :], True))
        rows.append((f"ffn{i}", w["ffn_norm_g"][i:i + 1, :], True))
    rows.append(("final", w["final_norm_g"].rearrange("(a n) -> a n", a=1), True))
    return rows


def small_plan(layers):
    events = [("rms", None)]
    for i in range(layers):
        if i == 1:
            events += [("rms", None), ("drop", "mix1"), ("drop", "w0"), ("drop", "a0"),
                       ("pow", "kk"), ("drop", "k_k"), ("drop", "k_a"), ("drop", "r_k"),
                       ("pow", "gn"), ("drop", "gn_g"), ("drop", "gn_b"), ("drop", "mem1")]
        else:
            events += [("drop", f"mix{i}"), ("rms", None)]
        if i == 0:
            events += [("drop", "mem0"), ("drop", "b_a"), ("drop", "b_gate"), ("pow", "ln"), ("drop", "conv_g"),
                       ("drop", "conv_b")]
        if i == 2:
            events += [("drop", "mem2")] + [("drop", f"sgu_bias{j}") for j in range(4)] + [("pow", "ln")]
            events += [("drop", f"sgu_{n}{j}") for n in "gb" for j in range(2)]
        if i == 3:
            events += [("pow", "ret"), ("drop", "mem3")]
        events += [("drop", "conv_bo")] * (i == 0) + [("drop", f"xattn{i}"), ("rms", None), ("drop", f"ffn{i}"), ("rms", None)]
    return events + [("rms", None), ("drop", "final")]


def trunk_program(nc, w, out, layers):
    f32, f32r = mybir.dt.float32, mybir.dt.float32r
    ALU, ACT, AX = mybir.AluOpType, mybir.ActivationFunctionType, mybir.AxisListType
    plan = weight_plan(w, layers)
    rows = row_plan(w, layers)
    row_at = {name: n for n, (name, _, _) in enumerate(rows)}

    KB = 1024
    cursor = [(nc.sbuf_base + 63) // 64 * 64]

    def place(name, shape, dtype, at=None):
        size = 4 * int(np.prod(shape[1:]))
        if at is None:
            at = cursor[0]
            cursor[0] += (size + 63) // 64 * 64
        assert at + size <= nc.sbuf_usable_end, (name, at, size, nc.sbuf_usable_end)
        return nc.alloc_sbuf_tensor_at(name, shape, dtype, offset=at)

    raw = place("raw_weights", [P, RAW, 2, COLS], f32)
    w_high = place("weights_high", [P, SPLIT, 2, COLS], f32r)
    w_low = place("weights_low", [P, SPLIT, 2, COLS], f32r)
    x = place("x", [P, HALVES, D], f32)
    mem = place("mem", [P, HALVES, D], f32)
    row = place("rows", [P, 2, D], f32)
    masks = place("masks", [P, N_MASKS, P], f32)
    ones = place("ones", [1, P], f32)
    sums = place("square_sums", [P, HALVES, 2], f32)
    mean_sq = place("mean_square", [P, HALVES], f32)
    rstd = place("rstd", [P, HALVES], f32)
    rms_col = place("rms_col", [P, HALVES], f32)
    rms_row = place("rms_row", [1, T], f32)
    neg_half = place("neg_half", [P, NH], f32)
    stat = place("stat", [P, HALVES], f32)
    scratch_at = cursor[0]
    scratch = place("scratch", [P, COLS], f32)
    bn = place("bn", [P, HALVES, 4, 6], f32)
    mv = place("mean_var", [P, HALVES, 2], f32)
    den = place("softmax_den", [P, 3, HALVES * XH], f32)
    taps = place("taps", [P, KC, 32], f32)
    small = place("head_stats", [P, 6, NH], f32, cursor[0] - KB)
    pc = place("chunk_decay", [HD, HALVES, NH, 2], f32, cursor[0] - KB + 384)
    mix_cols = place("mix_columns", [P, KC, 6], f32, cursor[0] - KB + 640)
    XT0 = cursor[0]
    xT_high = place("xT_high", [P, KC, T], f32r)
    xT_low = place("xT_low", [P, KC, T], f32r)
    ARENA = cursor[0]
    memT_high = place("memT_high", [P, KC, T], f32r, ARENA)
    memT_low = place("memT_low", [P, KC, T], f32r, ARENA + 8 * KB)
    kT = place("kT", [P, KC, T], f32, ARENA + 16 * KB)
    v_tok = place("v_tok", [P, HALVES, D], f32, ARENA + 24 * KB)
    BIG = ARENA + 32 * KB
    hT_high = place("hT_high", [P, FC, T], f32r, BIG)
    hT_low = place("hT_low", [P, FC, T], f32r, BIG + 22 * KB)
    sgate = place("silu_gate", [P, HALVES, 2, 256], f32, ARENA + 24 * KB)
    htok = place("h_tok", [P, HALVES, 2, 256], f32, ARENA + 28 * KB)
    k_tok = place("k_tok", [P, 2, HALVES, COLS], f32, BIG + 36 * KB)
    xn = place("x_normed", [P, HALVES, D], f32, BIG + 36 * KB)
    xg = place("x_gained", [P, HALVES, D], f32, ARENA + 16 * KB)
    q_tok = place("q_tok", [P, HALVES, D], f32, BIG)
    qT = place("qT", [P, KC, T], f32, BIG + 8 * KB)
    prob = place("prob", [P, HALVES, XH, T], f32, BIG + 16 * KB)
    probT = place("probT", [P, XH, HALVES, T], f32, BIG + 24 * KB)
    yT_high = place("yT_high", [P, 2 * KC, T], f32r, XT0)

    psum = nc.alloc_psum_tensor("psum", [P, 8, COLS], f32)
    TR = 4

    def sem(name):
        return nc.alloc_semaphore(name)

    raw_loaded = [sem(f"raw_loaded{s}") for s in range(RAW)]
    w_high_ready = sem("w_high_ready")
    w_low_ready = sem("w_low_ready")
    tile_used = sem("tile_used")
    group_drained = sem("group_drained")
    cols_filled = sem("cols_filled")
    cols_high = sem("cols_high")
    cols_drained = sem("cols_drained")
    x_loaded = sem("x_loaded")
    const_loaded = sem("const_loaded")
    row_loaded = [sem(f"row_loaded{s}") for s in range(2)]
    row_used = sem("row_used")
    vec_step = sem("vec_step")
    act_step = sem("act_step")
    squares_summed = sem("squares_summed")
    rstd_ready = sem("rstd_ready")
    stat_ready = sem("stat_ready")
    root_ready = sem("root_ready")
    pool_step = sem("pool_step")
    rms_copied = sem("rms_copied")
    tok_ready = sem("tok_ready")
    scores_filled = sem("scores_filled")
    scores_used = sem("scores_used")
    neg_max = sem("neg_max")
    exp_done = sem("exp_done")
    act_out = sem("act_out")
    vec_out = sem("vec_out")
    result_ready = sem("result_ready")
    stored = sem("stored")
    mixer_in = sem("mixer_in")
    mixer_free = sem("mixer_free")
    mixer_zero = sem("mixer_zero")
    tap_ready = sem("tap_ready")
    tap_used = sem("tap_used")
    conv_filled = sem("conv_filled")
    square_summed = sem("square_summed")
    lane_filled = [sem(f"lane_filled{j}") for j in range(2)]
    lane_used = [sem(f"lane_used{j}") for j in range(2)]

    ident = masks[:, M_IDENT, :]

    z_tok = place("z_tok", [P, HALVES, D], f32, BIG)
    zT = place("zT", [P, KC, T + TAPS - 1], f32, BIG + 8 * KB)
    conv = place("conv", [P, KC, T], f32, BIG + 18 * KB)
    sig = place("sig", [P, 2, HALVES, 256], f32, BIG + 26 * KB)
    dw_tok = place("dw_tok", [32, D], f32, BIG + 30 * KB)
    tap_diag = place("tap_diagonals", [P, 4, P], f32, scratch_at)
    u_tok = place("u_tok", [P, HALVES, E2], f32, BIG)
    g_tok = place("g_tok", [P, HALVES, E2], f32, BIG + 16 * KB)
    gate_low = place("gate_low", [P, 2 * KC, T], f32r, BIG + 16 * KB)
    ws_in = place("ws_in", [P, 8, P], f32, ARENA + 24 * KB)
    wsT = place("wsT", [P, 8, P], f32, ARENA + 28 * KB)
    bs_in = place("bs_in", [8, P], f32, BIG + 32 * KB)
    bsT = place("bsT", [P, 8], f32, BIG + 33 * KB)
    sgu_low = place("sgu_low", [P, 2 * KC, T], f32r, BIG + 16 * KB)

    qk = [place(f"ret_{n}", [P, HALVES, D], f32, ARENA + 8 * KB * j) for j, n in enumerate("qk")]
    o_tok = place("o_tok", [P, HALVES, E2], f32, ARENA)
    rv = place("ret_v", [P, HALVES, E2], f32, ARENA + 16 * KB)
    ret_low = place("ret_low", [P, 2 * KC, T], f32r, ARENA + 16 * KB)
    rg = place("ret_gate", [P, HALVES, E2], f32, ARENA + 32 * KB)
    rotary = place("rotary_cs", [P, 2, HALVES, HW], f32, ARENA + 48 * KB)
    decay = place("decay", [P, XH, 3 * P], f32, ARENA + 52 * KB)
    sc = place("ret_scores", [P, XH, 3 * P], f32, ARENA + 58 * KB)
    rtmp = place("rot_tmp", [P, XH, HW // 2, 2], f32, ARENA + 64 * KB)
    qkT = [place(f"ret_{n}T", [P, KC, T], f32, XT0 + 8 * KB * j) for j, n in enumerate("qk")]
    hT = place("hT", [P, KC, T + 1], f32, ARENA)
    diff = place("shift_diff", [P, KC, T], f32, ARENA + 8 * KB + 256)
    xs = place("xs", [P, KC, T], f32, ARENA + 16 * KB + 256)
    W0 = ARENA + 24 * KB + 256
    rr, rk, rvv, lw, ra, rgate = [place("rwkv_" + n, [P, HALVES, D], f32, W0 + 8 * KB * j)
                                  for j, n in enumerate(["r", "k", "v", "lw", "a", "gate"])]
    xs_b = place("xs_b", [P, KC, T], f32, W0 + 16 * KB)
    mix_in = place("mix_in", [6, D], f32, W0 + 32 * KB)
    lora = [place(f"lora_hidden{j}", [P, T], f32, W0 + (48 + j) * KB) for j in range(3)]
    lora1 = [place("lora1_" + n, [P, KC, k], f32, XT0 + o) for n, k, o in (("w", 64, 0), ("a", 64, 2 * KB), ("g", 160, 4 * KB))]
    lora2 = [place("lora2_" + n, [k, D], f32, W0 + 4 * KB * j)
             for j, (n, k) in enumerate((("w", 64), ("a", 64), ("g", P), ("g_rest", 32)))]
    kk = place("kk", [P, HALVES, D], f32, ARENA + 16 * KB + 256)
    tmp = [place(f"tmp{j}", [P, D], f32, XT0 + 4 * KB * j) for j in range(4)]
    aT, bT, kkT, rT = [place("chunk_" + n, [HD, 8, P], f32, XT0 + 4 * KB * j) for j, n in enumerate(["aT", "bT", "kT", "rT"])]
    inv, invT, lvl = [place("chunk_" + n, [P, 8, P], f32, XT0 + 4 * KB * j) for j, n in enumerate(["inv", "invT", "level"])]
    wT = place("chunk_wT", [HD, 8, P], f32, XT0)
    abT, akT, rbT, rkT = [place("chunk_" + n, [P, 8, P], f32, ARENA + 4 * KB * j) for j, n in enumerate(["abT", "akT", "rbT", "rkT"])]
    hh = place("chunk_h", [P, 8, HD], f32, W0 + 24 * KB)
    uu = place("chunk_u", [P, 8, HD], f32, W0 + 24 * KB)
    zz = place("chunk_z", [P, 8, HD], f32, W0 + 26 * KB)
    state = place("state", [HD, NH, HD], f32, W0 + 28 * KB)

    def bank(b):
        return psum[:, b, :]

    def source(p, g, kt):
        if p["paired"]:
            half = p["groups"] * 256
            v = p["src"].rearrange("(k p) n -> p k n", p=P)
            return [v[:, 2 * kt:2 * kt + 2, a * half + 256 * g:a * half + 256 * g + 256] for a in range(2)]
        return p["src"].rearrange("(k p) n -> p k n", p=P)[:, 2 * kt:2 * kt + 2, COLS * g:COLS * g + COLS]

    n_tiles = sum(p["tiles"] * p["groups"] for p in plan)

    with nc.Block() as block:

        @block.sync
        def _(sp):
            sp.dma_start(x[:, :, :], w["x"][0].rearrange("(h p) n -> p h n", p=P)).then_inc(x_loaded, 16)
            sp.dma_start(mem[:, :, :], w["mem"][0].rearrange("(h p) n -> p h n", p=P)).then_inc(x_loaded, 16)
            sp.dma_start(masks[:, :, :], w["masks"].rearrange("p (m n) -> p m n", n=P)).then_inc(const_loaded, 16)
            n = 0
            for p in plan:
                for g in range(p["groups"]):
                    for kt in range(p["tiles"]):
                        if n >= RAW:
                            sp.wait_ge(w_low_ready, n - RAW + 1)
                        if p["paired"]:
                            for a, src in enumerate(source(p, g, kt)):
                                sp.dma_start(raw[:, n % RAW, :, 256 * a:256 * a + 256], src).then_inc(raw_loaded[n % RAW], 16)
                        else:
                            sp.dma_start(raw[:, n % RAW, :, :], source(p, g, kt)).then_inc(raw_loaded[n % RAW], 32)
                        n += 1
            sp.wait_ge(result_ready, 1)
            sp.dma_start(out[0].rearrange("(h p) n -> p h n", p=P), xn[:, :, :]).then_inc(stored, 16)
            sp.wait_ge(stored, 16)

        @block.gpsimd
        def _(pool):
            pool.memset(ones[:, :], 1.0).then_inc(mixer_zero, 1)
            pool.memset(neg_half[:, :], -0.5).then_inc(pool_step, 1)
            at = dict(row=0, norm=0, stat=0, step=1)

            def link(ins):
                at["step"] += 1
                ins.then_inc(pool_step, 1)
                pool.wait_ge(pool_step, at["step"])

            def load_row():
                n = at["row"]
                at["row"] += 1
                if n >= len(rows):
                    return
                name, src, wide = rows[n]
                if n >= 2:
                    pool.wait_ge(row_used, n - 1)
                dst, v = (row[:, n % 2, :], src.to_broadcast([P, D])) if wide else (row[0:1, n % 2, :], src)
                pool.dma_start(dst, v).then_inc(row_loaded[n % 2], 16)
                if name == "mix0":
                    pool.memset(zT[:, :, 0:TAPS - 1], 0.0).then_inc(mixer_zero, 1)
                    pool.dma_start(dw_tok[0:TAPS, :], w["conv_dw"][0]).then_inc(mixer_in, 16)
                    pool.dma_start(dw_tok[TAPS:TAPS + 1, :], w["conv_dw_b"]).then_inc(mixer_in, 16)

            def load_mixer(i):
                pool.wait_ge(mixer_free, i)
                if i == 1:
                    for j, n1 in enumerate(("rwkv_w1", "rwkv_a1", "rwkv_g1")):
                        pool.dma_start(lora1[j][:, :, :], w[n1][0].rearrange("(k p) n -> p k n", p=P)).then_inc(mixer_in, 16)
                    pool.dma_start(lora2[0][:, :], w["rwkv_w2"][0]).then_inc(mixer_in, 16)
                    pool.dma_start(lora2[1][:, :], w["rwkv_a2"][0]).then_inc(mixer_in, 16)
                    pool.dma_start(lora2[2][:, :], w["rwkv_g2"][0, 0:P, :]).then_inc(mixer_in, 16)
                    pool.dma_start(lora2[3][:, :], w["rwkv_g2"][0, P:P + 32, :]).then_inc(mixer_in, 16)
                    pool.dma_start(mix_in[:, :], w["rwkv_mix"][0]).then_inc(mixer_in, 16)
                if i == 2:
                    pool.dma_start(ws_in[:, :, :], w["sgu_ws"][0].rearrange("g t s -> t g s")).then_inc(mixer_in, 16)
                    pool.dma_start(bs_in[:, :], w["sgu_bs"][0]).then_inc(mixer_in, 16)
                if i == 3:
                    pool.dma_start(rotary[:, 0, :, :], w["rotary"][0].rearrange("(h p) n -> p h n", p=P)).then_inc(mixer_in, 16)
                    pool.dma_start(rotary[:, 1, :, :], w["rotary"][1].rearrange("(h p) n -> p h n", p=P)).then_inc(mixer_in, 16)
                    pool.dma_start(decay[:, :, :], w["decay"].rearrange("p (h n) -> p h n", h=XH)).then_inc(mixer_in, 16)

            load_row()
            load_row()
            pool.wait_ge(pool_step, 1)
            roots = {"ln": (mv[:, :, 1], stat[:, :]), "kk": (small[:, 1:3, :], small[:, 2:4, :]),
                     "gn": (small[:, 0:2, :], small[:, 2:4, :]), "ret": (small[:, 1, 0:8], small[:, 2, 0:8])}
            for kind, name in small_plan(layers):
                if kind == "drop":
                    load_row()
                elif kind == "rms":
                    at["norm"] += 1
                    pool.wait_ge(squares_summed, 4 * at["norm"])
                    link(pool.tensor_tensor(mean_sq[:, :], sums[:, :, 0], sums[:, :, 1], ALU.add))
                    link(pool.tensor_scalar(mean_sq[:, :], mean_sq[:, :], 1.0 / D, 1e-6, ALU.mult, ALU.add))
                    link(pool.tensor_tensor(rstd[:, :], mean_sq[:, :], neg_half[:, 0:HALVES], ALU.pow))
                    pool.tensor_tensor(rms_col[:, :], mean_sq[:, :], rstd[:, :], ALU.mult).then_inc(rstd_ready, 1)
                    if at["norm"] in (2 + 3 * i for i in range(1, layers)):
                        load_mixer((at["norm"] - 2) // 3)
                else:
                    at["stat"] += 1
                    pool.wait_ge(stat_ready, at["stat"])
                    src, dst = roots[name]
                    for j in (range(HALVES - 1, -1, -1) if len(src.shape) == 3 else range(1)):
                        v, o = (src[:, j, :], dst[:, j, :]) if len(src.shape) == 3 else (src, dst)
                        link(pool.tensor_tensor(o, v, neg_half[:, 0:v.shape[-1]], ALU.pow))
                    pool.sem_inc(root_ready, 1)

        @block.scalar
        def _(act):
            at = dict(prod=0, split=0, col=0, high=0, score=0, sumsq=0, stat=0, exp=0, step=0, vec=0, neg=0, tile=0, lane=0, lane1=0)

            def split_to(n):
                while at["split"] < min(n, n_tiles):
                    t = at["split"]
                    act.wait_ge(raw_loaded[t % RAW], 32 * (t // RAW + 1))
                    if t >= SPLIT:
                        act.wait_ge(tile_used, t - SPLIT + 1)
                    act.activation(w_high[:, t % SPLIT, :, :], raw[:, t % RAW, :, :], ACT.Copy).then_inc(w_high_ready, 1)
                    at["split"] += 1

            def group_done(tiles):
                at["tile"] += tiles
                split_to(at["tile"] + LOOK)
                act.wait_ge(tile_used, at["tile"])

            def columns(high, chunks, c0=0):
                for c in range(0, chunks, 2):
                    act.wait_ge(cols_filled, at["col"] + 1)
                    act.activation(high[:, c0 + c:c0 + c + 2, :], bank(TR + at["col"] % 2), ACT.Copy).then_inc(cols_high, 1)
                    at["col"] += 1

            def skip_columns(banks):
                at["col"] += banks

            def squares(src, g):
                for h in range(HALVES):
                    if at["sumsq"]:
                        act.wait_ge(squares_summed, at["sumsq"])
                    act.activation(scratch[:, :], src[:, h, g * COLS:(g + 1) * COLS], ACT.Square,
                                   accum_out=sums[:, h, g:g + 1]).then_inc(squares_summed, 1)
                    at["sumsq"] += 1

            def scale_ready():
                act.wait_ge(rstd_ready, at["sumsq"] // 4)

            def residual(groups, tiles, deferred=True):
                for g in range(groups):
                    group_done(tiles)
                    at["prod"] += 1
                    if deferred and g == 0:
                        act.wait_ge(group_drained, at["prod"])
                        squares(x, g)
                        split_to(at["tile"] + 2 * LOOK)
                    if deferred:
                        columns(xT_high, KC // 2, g * KC // 2)
                    if not (deferred and g == 0):
                        act.wait_ge(group_drained, at["prod"])
                        squares(x, g)

            def product_groups(groups, tiles, evac=None):
                for g in range(groups):
                    group_done(tiles)
                    if evac:
                        evac(g, at["prod"] % 2)
                    at["prod"] += 1

            def gelu_evac(g, par):
                dst = u_tok if g < 4 else g_tok
                for h in range(HALVES):
                    act.activation(dst[:, h, (g % 4) * COLS:(g % 4 + 1) * COLS], bank(2 * par + h), ACT.Gelu,
                                   scale=rstd[:, h:h + 1]).then_inc(act_out, 1)

            def sigmoid_evac(g, par):
                for h in range(HALVES):
                    if g >= 2:
                        act.wait_ge(group_drained, at["prod"] - 1)
                    act.activation(sig[:, g % 2, h, :], psum[:, 2 * par + h, 256:512], ACT.Sigmoid, scale=rstd[:, h:h + 1]).then_inc(act_out, 1)

            def silu_evac(g, par):
                for h in range(HALVES):
                    if g >= 2:
                        act.wait_ge(group_drained, at["prod"] - 1)
                    act.activation(sgate[:, g % 2, h, :], psum[:, 2 * par + h, 0:256], ACT.Silu, scale=rstd[:, h:h + 1]).then_inc(act_out, 1)

            def conv_mixer():
                columns(memT_high, KC)
                skip_columns(2 + 1)
                scale_ready()
                product_groups(4, 4, sigmoid_evac)
                split_to(at["tile"] + SPLIT)
                act.wait_ge(cols_drained, 4 + 4 + 2)
                n = 0
                for c in range(CONV_DVE, KC):
                    for t in range(TAPS):
                        if n >= 4:
                            act.wait_ge(tap_used, n - 3)
                        act.activation(tap_diag[:, n % 4, :], ident, ACT.Copy, scale=taps[:, c, t:t + 1]).then_inc(tap_ready, 1)
                        n += 1
                skip_columns(4)
                product_groups(1, 4)
                skip_columns(4)
                product_groups(1, 4)
                at["vec"] += 1
                act.wait_ge(vec_out, at["vec"])
                act.activation(z_tok[:, :, :], z_tok[:, :, :], ACT.Silu).then_inc(act_out, 1)
                columns(xT_high, KC)
                skip_columns(4)
                return 2, 4

            def sgu_mixer():
                columns(memT_high, KC)
                skip_columns(3 + 1)
                scale_ready()
                product_groups(8, 4, gelu_evac)
                at["score"] += 8
                columns(yT_high, 2 * KC)
                return 2, 8

            def ret_mixer():
                scale_ready()
                product_groups(4, 4)
                for g in range(8):
                    group_done(4)
                    par = at["prod"] % 2
                    dst, fn = (rv, ACT.Copy) if g < 4 else (rg, ACT.Silu)
                    for h in range(HALVES):
                        act.activation(dst[:, h, (g % 4) * COLS:(g % 4 + 1) * COLS], bank(2 * par + h), fn, scale=rstd[:, h:h + 1]).then_inc(act_out, 1)
                    at["prod"] += 1
                skip_columns(8)
                at["score"] += XH
                for n in range(HALVES * XH):
                    act.wait_ge(scores_filled, at["score"] + 1)
                    if n:
                        act.wait_ge(square_summed, n)
                    act.activation(rtmp[:, 0:2, :, :].rearrange("p a n e -> p (a n e)"), bank(6 + at["score"] % 2), ACT.Square,
                                   accum_out=small[:, 0, n:n + 1]).then_inc(square_summed, 1)
                    at["score"] += 1
                columns(yT_high, 2 * KC)
                return 2, 8

            def lane_take():
                n = at["lane"]
                act.wait_ge(lane_filled[0], n + 1)
                at["lane"] += 1
                return n % 4

            def lane_copy(dst, view, fn=ACT.Copy):
                b = lane_take()
                act.activation(dst, view(psum[:, b, :]), fn).then_inc(lane_used[0], 1)

            def rwkv_mixer():
                skip_columns(4 + 1)
                for j, fn in enumerate((ACT.Tanh, ACT.Copy, ACT.Sigmoid)):
                    lane_copy(lora[j][0:(P if j == 2 else 64), :], lambda v: v[0:(P if j == 2 else 64), 0:T], fn)
                    if j == 2:
                        lane_copy(lora[0][0:32, :], lambda v: v[0:32, 0:T], fn)
                    for h in range(HALVES):
                        for n in range(2):
                            dst = (lw, ra, rgate)[j][:, h, COLS * n:COLS * n + COLS]
                            lane_copy(dst, lambda v: v, ACT.Copy if j == 2 else ACT.Sigmoid)
                for m in range(3):
                    at["vec"] += 1
                    act.wait_ge(vec_out, at["vec"])
                    act.activation(xT_high[:, :, :], (xs, xs_b, xs)[m][:, :, :], ACT.Copy).then_inc(act_out, 1)
                    product_groups(2, 4)
                for h in range(HALVES):
                    for n in range(2):
                        lane1 = at["lane1"]
                        act.wait_ge(lane_filled[1], lane1 + 1)
                        at["lane1"] += 1
                        cols = slice(COLS * n, COLS * n + COLS)
                        if 2 * h + n >= 1:
                            act.wait_ge(lane_used[1], lane1)
                            at["vec"] += 1
                            act.wait_ge(vec_out, at["vec"])
                        act.activation(tmp[0][:, 0:COLS], bank(4 + lane1 % 4), ACT.Exp).then_inc(act_out, 1)
                        act.activation(tmp[1][:, 0:COLS], bank(4 + lane1 % 4), ACT.Exp, scale=-1.0).then_inc(act_out, 1)
                        act.wait_ge(lane_used[1], lane1 + 1)
                        act.activation(tmp[2][:, 0:COLS], tmp[2][:, 0:COLS], ACT.Exp).then_inc(act_out, 1)
                lane_copy(pc[:, :, :, :], lambda v: v[0:HD, 0:64].rearrange("p (h n c) -> p h n c", h=HALVES, c=2), ACT.Exp)
                heads4 = lambda v: v[0:HD, :].rearrange("p (h t) -> p h t", h=4)
                heads8 = lambda v: v.rearrange("p (h t) -> p h t", h=8)
                for h in range(HALVES):
                    for hg in range(2):
                        for dst in (aT, bT, kkT, rT):
                            for sb in range(2):
                                lane_copy(dst[:, 4 * sb:4 * sb + 4, :], heads4)
                        for sb in range(2):
                            lane_copy(wT[:, 4 * sb:4 * sb + 4, :], heads4)
                        lane_copy(hh[:, :, :], heads8)
                        lane_copy(zz[:, :, :], heads8)
                        lane_copy(rr[:, h, 512 * hg:512 * hg + 512], lambda v: v)
                columns(xT_high, KC)
                return 2, 4

            act.wait_ge(x_loaded, 32)
            squares(mem, 0)
            squares(mem, 1)
            act.wait_ge(rstd_ready, 1)
            squares(x, 0)
            squares(x, 1)
            split_to(LOOK)
            columns(xT_high, KC)
            for i in range(layers):
                groups, tiles = [conv_mixer, rwkv_mixer, sgu_mixer, ret_mixer][i]()
                if i in (1, 3):
                    columns(memT_high, KC)
                residual(groups, tiles)
                if i:
                    product_groups(2, 4)
                    skip_columns(4)
                product_groups(2, 4)
                skip_columns(4)
                product_groups(1, 4)
                for h in range(HALVES):
                    for hp in range(XH // 2):
                        at["neg"] += 1
                        act.wait_ge(neg_max, at["neg"])
                        for e in range(2):
                            hd = 2 * hp + e
                            j = h * XH + hd
                            act.activation(prob[:, h, hd, :], psum[:, 6 + at["score"] % 2, e * T:(e + 1) * T], ACT.Exp,
                                           bias=den[:, 0, j:j + 1], scale=float(HW) ** -0.5,
                                           accum_out=den[:, 1, j:j + 1]).then_inc(exp_done, 1)
                        at["score"] += 1
                product_groups(1, 4)
                skip_columns(4)
                for c in range(XH):
                    act.wait_ge(scores_filled, at["score"] + 1)
                    act.activation(xT_high[:, 2 * c:2 * c + 2, :], bank(6 + at["score"] % 2), ACT.Copy).then_inc(cols_high, 1)
                    at["score"] += 1
                residual(2, 4)
                scale_ready()
                for g in range(11):
                    group_done(4)
                    silu_evac(g, at["prod"] % 2)
                    at["prod"] += 1
                    if g:
                        columns(hT_high, 2, 2 * (g - 1))
                columns(hT_high, 2, 20)
                residual(2, 11, i + 1 < layers and i != 0)

        @block.vector
        def _(dve):
            at = dict(prod=0, split=0, col=0, high=0, score=0, sumsq=0, stat=0, exp=0, step=0, act=0, tile=0, lane=0)

            def link(ins):
                at["step"] += 1
                ins.then_inc(vec_step, 1)
                dve.wait_ge(vec_step, at["step"])

            def split_to(n):
                while at["split"] < min(n, n_tiles):
                    t = at["split"]
                    dve.wait_ge(w_high_ready, t + 1)
                    dve.tensor_tensor(w_low[:, t % SPLIT, :, :], raw[:, t % RAW, :, :],
                                      w_high[:, t % SPLIT, :, :].bitcast(f32), ALU.subtract).then_inc(w_low_ready, 1)
                    at["split"] += 1

            def group_done(tiles):
                at["tile"] += tiles
                split_to(at["tile"] + LOOK)
                dve.wait_ge(tile_used, at["tile"])

            def columns(high, low, chunks, c0=0):
                for c in range(0, chunks, 2):
                    at["high"] += 1
                    dve.wait_ge(cols_high, at["high"])
                    dve.tensor_tensor(low[:, c0 + c:c0 + c + 2, :], psum[:, TR + at["col"] % 2, :].rearrange("p (c t) -> p c t", c=2),
                                      high[:, c0 + c:c0 + c + 2, :].bitcast(f32), ALU.subtract).then_inc(cols_drained, 1)
                    at["col"] += 1

            def plain_columns(dst_of, banks):
                for b in range(banks):
                    dve.wait_ge(cols_filled, at["col"] + 1)
                    dst, src = dst_of(b, TR + at["col"] % 2)
                    dve.tensor_copy(dst, src).then_inc(cols_drained, 1)
                    at["col"] += 1

            def pair_of(dst):
                return lambda b, bk: (dst[:, 2 * b:2 * b + 2, :], psum[:, bk, :].rearrange("p (c t) -> p c t", c=2))

            def use_row(name):
                n = row_at[name]
                dve.wait_ge(row_loaded[n % 2], 16 * (n // 2 + 1))
                return row[:, n % 2, :]

            def drop_row(ins):
                ins.then_inc(row_used, 1)

            def scale_ready():
                at["norm"] = at.get("norm", 0) + 1
                dve.wait_ge(rstd_ready, at["norm"])

            def tok_done(ins):
                at["tok"] = at.get("tok", 0) + 1
                ins.then_inc(tok_ready, 1)

            def tok_signal():
                at["tok"] = at.get("tok", 0) + 1
                dve.sem_inc(tok_ready, 1)

            def gain(dst, src, name, g0, g1):
                r = use_row(name)
                c = slice(g0 * COLS, g1 * COLS)
                for h in range(HALVES):
                    tok_done(dve.tensor_tensor(dst[:, h, c], src[:, h, c], r[:, c], ALU.mult))
                if g1 == 2:
                    dve.wait_ge(tok_ready, at["tok"])
                    dve.sem_inc(row_used, 1)

            def normed(name):
                scale_ready()
                r = use_row(name)
                for h in range(HALVES):
                    tok_done(dve.scalar_tensor_tensor(xn[:, h, :], x[:, h, :], rstd[:, h:h + 1], r, ALU.mult, ALU.mult))
                dve.wait_ge(tok_ready, at["tok"])
                dve.sem_inc(row_used, 1)

            def rms_rows():
                dve.wait_ge(cols_filled, at["col"] + 1)
                dve.tensor_copy(rms_row[:, :], psum[0:1, TR + at["col"] % 2, 0:T]).then_inc(cols_drained, 1)
                at["col"] += 1

            def drained(ins):
                ins.then_inc(group_drained, 1)
                at["prod"] += 1

            def residual(groups, tiles, buf, name=None, bias_row=False):
                for g in range(groups):
                    group_done(tiles)
                    par = at["prod"] % 2
                    for h in range(HALVES):
                        cols = x[:, h, g * COLS:(g + 1) * COLS]
                        ins = dve.tensor_tensor(cols, cols, bank(2 * par + h), ALU.add)
                        drained(ins) if h else link(ins)
                    dve.wait_ge(group_drained, at["prod"])
                    if bias_row and g:
                        dve.sem_inc(row_used, 1)
                    if name:
                        gain(buf, x, name, g, g + 1)
                        if g == 0:
                            split_to(at["tile"] + 2 * LOOK)
                        columns(xT_high, xT_low, KC // 2, g * KC // 2)

            def scaled(dst, groups, tiles):
                for g in range(groups):
                    group_done(tiles)
                    par = at["prod"] % 2
                    for h in range(HALVES):
                        ins = dve.tensor_scalar(dst[:, h, g * COLS:(g + 1) * COLS], bank(2 * par + h), rstd[:, h:h + 1], None, ALU.mult)
                        drained(ins) if h else link(ins)

            def copies(dst, groups, tiles, g0=0):
                for g in range(groups):
                    group_done(tiles)
                    par = at["prod"] % 2
                    for h in range(HALVES):
                        ins = dve.tensor_copy(dst[:, h, (g + g0) * COLS:(g + g0 + 1) * COLS], bank(2 * par + h))
                        drained(ins) if h else link(ins)

            def gated(g, mul_cols, gate_of, dst_of):
                par = at["prod"] % 2
                for h in range(HALVES):
                    at["act"] += 1
                    dve.wait_ge(act_out, at["act"])
                    ins = dve.scalar_tensor_tensor(dst_of(h), psum[:, 2 * par + h, mul_cols:mul_cols + 256], rstd[:, h:h + 1],
                                                   gate_of(h), ALU.mult, ALU.mult)
                    drained(ins) if h else link(ins)
                dve.wait_ge(group_drained, at["prod"])

            def layer_norm(buf, width, gains, biases):
                for h in range(HALVES):
                    for s in range(width // 512):
                        link(dve.bn_stats(bn[:, h, s, :], buf[:, h, 512 * s:512 * s + 512]))
                    link(dve.bn_aggr(mv[:, h, :], bn[:, h, 0:width // 512, :].rearrange("p s c -> p (s c)")))
                dve.tensor_scalar(mv[:, :, 1], mv[:, :, 1], 1e-5, None, ALU.add).then_inc(stat_ready, 1)
                at["stat"] += 1
                dve.wait_ge(root_ready, at["stat"])
                for h in range(HALVES):
                    link(dve.tensor_scalar(buf[:, h, :], buf[:, h, :], mv[:, h, 0:1], stat[:, h:h + 1], ALU.subtract, ALU.mult))
                for names, op in ((gains, ALU.mult), (biases, ALU.add)):
                    for j, name in enumerate(names):
                        r = use_row(name)
                        for h in range(HALVES):
                            v = buf[:, h, j * D:(j + 1) * D]
                            link(dve.tensor_tensor(v, v, r, op))
                        dve.sem_inc(row_used, 1)

            def key_group(g):
                par = at["prod"] % 2
                for h in range(HALVES):
                    ins = dve.tensor_copy(k_tok[:, g, h, :], bank(2 * par + h))
                    drained(ins) if h else link(ins)

            def conv_mixer():
                gain(xn, mem, "mem0", 0, 2)
                columns(memT_high, memT_low, KC)
                plain_columns(lambda b, bk: (taps[:, 4 * b:4 * b + 4, :], psum[:, bk, 0:128].rearrange("p (c t) -> p c t", c=4)), 2)
                scale_ready()
                rms_rows()
                for g in range(4):
                    group_done(4)
                    gated(g, 0, lambda h: sig[:, g % 2, h, :], lambda h: z_tok[:, h, 256 * g:256 * g + 256])
                dve.sem_inc(row_used, 2)
                tok_signal()
                plain_columns(lambda b, bk: (zT[:, 2 * b:2 * b + 2, TAPS - 1:TAPS - 1 + T],
                                             psum[:, bk, :].rearrange("p (c t) -> p c t", c=2)), 4)
                dve.wait_ge(cols_drained, at["col"])
                dve.wait_ge(mixer_zero, 2)
                split_to(at["tile"] + SPLIT)
                base = at["step"]
                for t in range(TAPS):
                    for c in range(CONV_DVE):
                        src = zT[:, c, t:t + T]
                        if t:
                            dve.wait_ge(vec_step, base + CONV_DVE * (t - 1) + c + 1)
                            ins = dve.scalar_tensor_tensor(conv[:, c, :], src, taps[:, c, t:t + 1], conv[:, c, :], ALU.mult, ALU.add)
                        else:
                            ins = dve.tensor_scalar(conv[:, c, :], src, taps[:, c, 0:1], taps[:, c, TAPS:TAPS + 1], ALU.mult, ALU.add)
                        ins.then_inc(vec_step, 1)
                        at["step"] += 1
                dve.wait_ge(conv_filled, 1)
                for c in range(CONV_DVE, KC):
                    j = c - CONV_DVE
                    link(dve.tensor_scalar(conv[:, c, :], psum[:, 6 + j // 2, T * (j % 2):T * (j % 2) + T], taps[:, c, TAPS:TAPS + 1], None, ALU.add))
                tok_signal()
                group_done(4)
                key_group(0)
                plain_columns(lambda b, bk: (z_tok[:, b // 2, (b % 2) * 512:(b % 2) * 512 + 512], psum[:, bk, :]), 4)
                dve.wait_ge(cols_drained, at["col"])
                layer_norm(z_tok, D, ["conv_g"], ["conv_b"])
                dve.sem_inc(vec_out, 1)
                at["act"] += 1
                group_done(4)
                key_group(1)
                columns(xT_high, xT_low, KC)
                plain_columns(pair_of(kT), 4)
                return 2, 4

            def sgu_mixer():
                gain(xn, mem, "mem2", 0, 2)
                columns(memT_high, memT_low, KC)
                plain_columns(lambda b, bk: (wsT[:, 4 * b:4 * b + 4, :], psum[:, bk, :].rearrange("p (c t) -> p c t", c=4)) if b < 2
                              else (bsT[:, :], psum[:, bk, 0:8]), 3)
                dve.wait_ge(cols_drained, at["col"])
                scale_ready()
                rms_rows()
                for g in range(8):
                    link(dve.tensor_tensor(wsT[:, g, :], wsT[:, g, :], masks[:, M_TRI_ALL, :], ALU.mult))
                for g in range(8):
                    group_done(4)
                    at["act"] += HALVES
                    dve.wait_ge(act_out, at["act"])
                    dve.sem_inc(group_drained, 1)
                    at["prod"] += 1
                    if g % 2:
                        dve.sem_inc(row_used, 1)
                layer_norm(g_tok, E2, ["sgu_g0", "sgu_g1"], ["sgu_b0", "sgu_b1"])
                tok_signal()
                for h in range(HALVES):
                    for gp in range(4):
                        dve.wait_ge(scores_filled, at["score"] + 1)
                        for e in range(2):
                            g = 2 * gp + e
                            u = u_tok[:, h, 256 * g:256 * g + 256]
                            ins = dve.scalar_tensor_tensor(u, psum[:, 6 + at["score"] % 2, 256 * e:256 * e + 256], bsT[:, g:g + 1], u,
                                                           ALU.add, ALU.mult)
                            ins.then_inc(scores_used, 1) if e else link(ins)
                        at["score"] += 1
                columns(yT_high, sgu_low, 2 * KC)
                return 2, 8

            def ret_mixer():
                scale_ready()
                for j in range(2):
                    scaled(qk[j], 2, 4)
                dve.wait_ge(group_drained, at["prod"])
                for g in range(8):
                    group_done(4)
                    at["act"] += HALVES
                    dve.wait_ge(act_out, at["act"])
                    dve.sem_inc(group_drained, 1)
                    at["prod"] += 1
                    if g == 0:
                        dve.wait_ge(mixer_in, 16 * MIXER_LOADS[3])
                    if g < 4:
                        v = qk[g // 2][:, g % 2, :].rearrange("p (a n e) -> p a n e", a=XH, e=2)
                        cos = rotary[:, 0, g % 2, :].unsqueeze(1).to_broadcast([P, XH, HW])
                        sin = rotary[:, 1, g % 2, :].rearrange("p (n e) -> p n e", e=2)
                        for e in range(2):
                            link(dve.tensor_tensor(rtmp[:, :, :, e], v[:, :, :, 1 - e],
                                                   sin[:, :, e].unsqueeze(1).to_broadcast([P, XH, HW // 2]), ALU.mult))
                        flat = qk[g // 2][:, g % 2, :].rearrange("p (a n) -> p a n", a=XH)
                        link(dve.tensor_tensor(flat, flat, cos, ALU.mult))
                        link(dve.tensor_tensor(flat, flat, rtmp[:, :, :, :].rearrange("p a n e -> p a (n e)"), ALU.add))
                tok_signal()
                for j in range(2):
                    plain_columns(pair_of(qkT[j]), 4)
                for hd in range(XH):
                    dve.wait_ge(scores_filled, at["score"] + 1)
                    dve.tensor_tensor(sc[:, hd, :], psum[:, 6 + at["score"] % 2, 0:3 * P], decay[:, hd, :], ALU.mult).then_inc(scores_used, 1)
                    at["score"] += 1
                for h in range(HALVES):
                    for hd in range(XH):
                        dve.wait_ge(square_summed, XH * h + hd + 1)
                        dve.tensor_tensor(o_tok[:, h, 512 * hd:512 * hd + 512], bank(6 + at["score"] % 2),
                                          rg[:, h, 512 * hd:512 * hd + 512], ALU.mult).then_inc(scores_used, 1)
                        at["score"] += 1
                dve.wait_ge(scores_used, at["score"])
                dve.tensor_scalar(small[:, 1, 0:8], small[:, 0, 0:8], 1.0 / 512, 1e-6, ALU.mult, ALU.add).then_inc(stat_ready, 1)
                at["stat"] += 1
                dve.wait_ge(root_ready, at["stat"])
                for n in range(HALVES * XH):
                    v = o_tok[:, n // XH, 512 * (n % XH):512 * (n % XH) + 512]
                    link(dve.tensor_scalar(v, v, small[:, 2, n:n + 1], None, ALU.mult))
                tok_signal()
                columns(yT_high, ret_low, 2 * KC)
                return 2, 8

            def lane_take():
                n = at["lane"]
                dve.wait_ge(lane_filled[1], n + 1)
                at["lane"] += 1
                return 4 + n % 4

            def over_heads(m):
                return masks[:, m, :].unsqueeze(1).to_broadcast([P, 4, P])

            def per_head(v):
                return v.unsqueeze(2).to_broadcast([P, NH, HD])

            def by_head(v):
                return v.rearrange("p (h n) -> p h n", h=NH)

            def mixed(m, dst):
                for c in range(KC):
                    last = dve.scalar_tensor_tensor(dst[:, c, :], diff[:, c, :], mix_cols[:, c, m:m + 1], hT[:, c, 1:T + 1], ALU.mult, ALU.add)
                link(last)

            def rwkv_mixer():
                link(dve.memset(hT[:, :, 0:1], 0.0))
                plain_columns(lambda b, bk: (hT[:, 2 * b:2 * b + 2, 1:T + 1], psum[:, bk, :].rearrange("p (c t) -> p c t", c=2)), 4)
                plain_columns(lambda b, bk: (mix_cols[:, :, :], psum[:, bk, 0:48].rearrange("p (c t) -> p c t", c=KC)), 1)
                dve.wait_ge(cols_drained, at["col"])
                link(dve.tensor_tensor(diff[:, :, :], hT[:, :, 0:T], hT[:, :, 1:T + 1], ALU.subtract))
                lora_acts = 0
                for j, m in enumerate((1, 4, 5)):
                    if j == 2:
                        dve.wait_ge(lane_used[0], 1)
                    mixed(m, (xs, xs_b, xs)[j])
                    tok_signal()
                dve.wait_ge(lane_used[0], 16)
                dve.sem_inc(row_used, 2)
                for m, src in enumerate((0, 2, 3)):
                    buf = (xs, xs_b, xs)[m]
                    mixed(src, buf)
                    if m:
                        dve.wait_ge(tile_used, at["tile"])
                    dve.sem_inc(vec_out, 1)
                    at["act"] += 1
                    dve.wait_ge(act_out, at["act"])
                    link(dve.tensor_tensor(xT_low[:, :, :], buf[:, :, :], xT_high[:, :, :].bitcast(f32), ALU.subtract))
                    tok_signal()
                    copies((rr, rk, rvv)[m], 2, 4)
                dve.wait_ge(group_drained, at["prod"])
                r = use_row("k_k")
                for h in range(HALVES):
                    link(dve.tensor_tensor(kk[:, h, :], rk[:, h, :], r, ALU.mult))
                    link(dve.tensor_tensor(tmp[h][:, :], kk[:, h, :], kk[:, h, :], ALU.mult))
                    link(dve.tensor_reduce(small[:, 1 + h, :], by_head(tmp[h][:, :]), AX.X, ALU.add))
                dve.tensor_scalar(small[:, 1:3, :], small[:, 1:3, :], 1e-24, None, ALU.max).then_inc(stat_ready, 1)
                at["stat"] += 1
                dve.wait_ge(root_ready, at["stat"])
                for h in range(HALVES):
                    link(dve.tensor_tensor(by_head(kk[:, h, :]), by_head(kk[:, h, :]), per_head(small[:, 2 + h, :]), ALU.mult))
                dve.sem_inc(row_used, 1)
                r = use_row("k_a")
                for h in range(HALVES):
                    link(dve.scalar_tensor_tensor(tmp[0][:, :], ra[:, h, :], -1.0, r, ALU.add, ALU.mult))
                    link(dve.scalar_tensor_tensor(rk[:, h, :], tmp[0][:, :], 1.0, rk[:, h, :], ALU.add, ALU.mult))
                dve.sem_inc(row_used, 1)
                r = use_row("r_k")
                for h in range(HALVES):
                    link(dve.tensor_tensor(tmp[0][:, :], rr[:, h, :], rk[:, h, :], ALU.mult))
                    link(dve.tensor_tensor(tmp[0][:, :], tmp[0][:, :], r, ALU.mult))
                    link(dve.tensor_reduce(small[:, 4 + h, :], by_head(tmp[0][:, :]), AX.X, ALU.add))
                    link(dve.tensor_tensor(ra[:, h, :], ra[:, h, :], kk[:, h, :], ALU.mult))
                    link(dve.tensor_scalar(lw[:, h, :], lw[:, h, :], -float(np.exp(-0.5)), None, ALU.mult))
                dve.sem_inc(row_used, 1)
                tok_signal()
                for h in range(HALVES):
                    for n in range(2):
                        b = lane_take()
                        cols = slice(COLS * n, COLS * n + COLS)
                        at["act"] += 2
                        dve.wait_ge(act_out, at["act"])
                        dve.tensor_tensor(tmp[2][:, 0:COLS], bank(b), lw[:, h, cols], ALU.subtract).then_inc(lane_used[1], 1)
                        link(dve.tensor_tensor(rr[:, h, cols], rr[:, h, cols], tmp[0][:, 0:COLS], ALU.mult))
                        link(dve.tensor_tensor(rk[:, h, cols], rk[:, h, cols], tmp[1][:, 0:COLS], ALU.mult))
                        link(dve.tensor_tensor(ra[:, h, cols], ra[:, h, cols], tmp[1][:, 0:COLS], ALU.mult))
                        at["act"] += 1
                        dve.wait_ge(act_out, at["act"])
                        link(dve.scalar_tensor_tensor(kk[:, h, cols], kk[:, h, cols], -1.0, tmp[2][:, 0:COLS], ALU.mult, ALU.mult))
                        if 2 * h + n < 3:
                            dve.sem_inc(vec_out, 1)
                dve.wait_ge(lane_used[0], 17)
                link(dve.memset(state[:, :, :], 0.0))
                tok_signal()
                heads = lambda b: psum[:, b, :].rearrange("p (h t) -> p h t", h=4)
                for h in range(HALVES):
                    for hg in range(2):
                        if h or hg:
                            dve.wait_ge(lane_used[0], 17 + 13 * (2 * h + hg))
                        for sb in range(2):
                            hs = slice(4 * sb, 4 * sb + 4)
                            for dst, m in ((abT, M_STRICT), (akT, M_STRICT), (rbT, M_INCL), (rkT, M_INCL)):
                                b = lane_take()
                                dve.tensor_tensor(dst[:, hs, :], heads(b), over_heads(m), ALU.mult).then_inc(lane_used[1], 1)
                            b = lane_take()
                            dve.tensor_tensor(inv[:, hs, :], heads(b), over_heads(M_LEVEL), ALU.mult).then_inc(lane_used[1], 1)
                            dve.wait_ge(lane_used[1], at["lane"])
                            link(dve.tensor_tensor(inv[:, hs, :], inv[:, hs, :], over_heads(M_IDENT), ALU.add))
                            link(dve.tensor_tensor(invT[:, hs, :], abT[:, hs, :], over_heads(M_PAIR_T), ALU.mult))
                            link(dve.tensor_tensor(invT[:, hs, :], invT[:, hs, :], over_heads(M_IDENT), ALU.add))
                            tok_signal()
                        for level in range(1, LEVELS):
                            for sb in range(2):
                                b = lane_take()
                                dve.tensor_tensor(lvl[:, 4 * sb:4 * sb + 4, :], heads(b), over_heads(M_LEVEL + level), ALU.mult).then_inc(lane_used[1], 1)
                            for sb in range(2):
                                for dst in ((inv, invT) if level < LEVELS - 1 else (invT,)):
                                    b = lane_take()
                                    d = dst[:, 4 * sb:4 * sb + 4, :]
                                    dve.tensor_tensor(d, heads(b), d, ALU.add).then_inc(lane_used[1], 1)
                        for c in range(2):
                            rs = slice(CH * c, CH * c + CH)
                            b = lane_take()
                            dve.wait_ge(lane_used[0], 17 + 13 * (2 * h + hg) + 12)
                            dve.tensor_tensor(uu[rs, :, :], psum[rs, b, :].rearrange("p (h n) -> p h n", h=8), zz[rs, :, :], ALU.add).then_inc(lane_used[1], 1)
                            b = lane_take()
                            st = state[:, 8 * hg:8 * hg + 8, :]
                            link(dve.tensor_tensor(st, psum[0:HD, b, :].rearrange("p (h n) -> p h n", h=8), st, ALU.add))
                            dve.tensor_tensor(st, st, pc[:, h, 8 * hg:8 * hg + 8, c:c + 1].to_broadcast([HD, 8, HD]), ALU.mult).then_inc(lane_used[1], 1)
                dve.wait_ge(lane_used[0], 17 + 13 * 4)
                for h in range(HALVES):
                    y = by_head(rr[:, h, :])
                    t = by_head(tmp[3][:, :])
                    link(dve.tensor_reduce(small[:, 2, :], y, AX.X, ALU.add))
                    link(dve.tensor_scalar(small[:, 2, :], small[:, 2, :], 1.0 / HD, None, ALU.mult))
                    link(dve.tensor_tensor(y, y, per_head(small[:, 2, :]), ALU.subtract))
                    link(dve.tensor_tensor(t, y, y, ALU.mult))
                    link(dve.tensor_reduce(small[:, h, :], t, AX.X, ALU.add))
                dve.tensor_scalar(small[:, 0:2, :], small[:, 0:2, :], 1.0 / HD, HD * 1e-5, ALU.mult, ALU.add).then_inc(stat_ready, 1)
                at["stat"] += 1
                dve.wait_ge(root_ready, at["stat"])
                for h in range(HALVES):
                    y = by_head(rr[:, h, :])
                    link(dve.tensor_tensor(y, y, per_head(small[:, 2 + h, :]), ALU.mult))
                for name, op in (("gn_g", ALU.mult), ("gn_b", ALU.add)):
                    r = use_row(name)
                    for h in range(HALVES):
                        link(dve.tensor_tensor(rr[:, h, :], rr[:, h, :], r, op))
                    dve.sem_inc(row_used, 1)
                for h in range(HALVES):
                    link(dve.tensor_tensor(by_head(tmp[3][:, :]), by_head(rvv[:, h, :]), per_head(small[:, 4 + h, :]), ALU.mult))
                    link(dve.tensor_tensor(rr[:, h, :], rr[:, h, :], tmp[3][:, :], ALU.add))
                    link(dve.tensor_tensor(rr[:, h, :], rr[:, h, :], rgate[:, h, :], ALU.mult))
                tok_signal()
                columns(xT_high, xT_low, KC)
                return 2, 4

            dve.wait_ge(x_loaded, 32)
            scale_ready()
            for h in range(HALVES):
                link(dve.tensor_scalar(mem[:, h, :], mem[:, h, :], rstd[:, h:h + 1], None, ALU.mult))
            gain(xg, x, "mix0", 0, 2)
            split_to(LOOK)
            columns(xT_high, xT_low, KC)
            for i in range(layers):
                if i == 1:
                    normed("mix1")
                groups, tiles = [conv_mixer, rwkv_mixer, sgu_mixer, ret_mixer][i]()
                if i in (1, 3):
                    gain(xn, mem, f"mem{i}", 0, 2)
                    columns(memT_high, memT_low, KC)
                if i == 0:
                    use_row("conv_bo")
                residual(groups, tiles, xn, f"xattn{i}", i == 0)
                if i:
                    for g in range(2):
                        group_done(4)
                        key_group(g)
                    plain_columns(pair_of(kT), 4)
                scale_ready()
                scaled(q_tok, 2, 4)
                plain_columns(pair_of(qT), 4)
                copies(v_tok, 1, 4)
                for h in range(HALVES):
                    for hp in range(XH // 2):
                        dve.wait_ge(scores_filled, at["score"] + 1)
                        j = h * XH + 2 * hp
                        link(dve.tensor_reduce(den[:, 2, j:j + 2], psum[:, 6 + at["score"] % 2, :].rearrange("p (e t) -> p e t", e=2), AX.X, ALU.max))
                        dve.tensor_scalar(den[:, 0, j:j + 2], den[:, 2, j:j + 2], -float(HW) ** -0.5, None, ALU.mult).then_inc(neg_max, 1)
                        at["score"] += 1
                        at["exp"] += 2
                        dve.wait_ge(exp_done, at["exp"])
                        dve.sem_inc(scores_used, 1)
                        link(dve.reciprocal(den[:, 2, j:j + 2], den[:, 1, j:j + 2]))
                        for e in range(2):
                            v = prob[:, h, 2 * hp + e, :]
                            tok_done(dve.tensor_scalar(v, v, den[:, 2, j + e:j + e + 1], None, ALU.mult))
                copies(v_tok, 1, 4, 1)
                plain_columns(lambda b, bk: (probT[:, b, :, :], psum[:, bk, :].rearrange("p (c t) -> p c t", c=2)), 4)
                for c in range(XH):
                    at["high"] += 1
                    dve.wait_ge(cols_high, at["high"])
                    dve.tensor_tensor(xT_low[:, 2 * c:2 * c + 2, :], psum[:, 6 + at["score"] % 2, :].rearrange("p (c t) -> p c t", c=2),
                                      xT_high[:, 2 * c:2 * c + 2, :].bitcast(f32), ALU.subtract).then_inc(scores_used, 1)
                    at["score"] += 1
                residual(2, 4, xg, f"ffn{i}")
                scale_ready()
                for g in range(11):
                    group_done(4)
                    gated(g, 256, lambda h: sgate[:, g % 2, h, :], lambda h: htok[:, g % 2, h, :])
                    if g:
                        columns(hT_high, hT_low, 2, 2 * (g - 1))
                columns(hT_high, hT_low, 2, 20)
                defer = i + 1 < layers and i != 0
                residual(2, 11, xg, f"mix{i + 1}" if defer else None)
                dve.sem_inc(mixer_free, 1)
            normed("final")
            dve.sem_inc(result_ready, 1)

        @block.tensor
        def _(pe):
            at = dict(plan=0, prod=0, tile=0, col=0, score=0, tok=0)

            def product(name, high, low, groups, bias=None, ready=None, after=None):
                p = plan[at["plan"]]
                if groups[-1] == p["groups"] - 1:
                    at["plan"] += 1
                assert p["name"] == name, (p["name"], name)
                for g in groups:
                    par = at["prod"] % 2
                    if at["prod"] >= 2:
                        pe.wait_ge(group_drained, at["prod"] - 1)
                    for kt in range(p["tiles"]):
                        t = at["tile"]
                        if g == groups[0] and ready:
                            pe.wait_ge(cols_drained, ready[kt])
                        pe.wait_ge(w_low_ready, t + 1)
                        for k in range(2):
                            for h in range(HALVES):
                                c = 2 * kt + k
                                last = c == 2 * p["tiles"] - 1
                                xh, xl = high[:, c, h * P:(h + 1) * P], low[:, c, h * P:(h + 1) * P]
                                wh, wl = w_high[:, t % SPLIT, k, :], w_low[:, t % SPLIT, k, :]
                                o = bank(2 * par + h)
                                if last and bias:
                                    for lhs, rhs, c0, c1 in bias(g, h):
                                        pe.matmul(psum[:, 2 * par + h, c0:c1], lhs, rhs, start=False, stop=False, skip_group_check=True)
                                skip = bool(bias)
                                pe.matmul(o, xh, wh, start=c == 0, stop=False, skip_group_check=skip)
                                pe.matmul(o, xh, wl, start=False, stop=False, skip_group_check=skip)
                                mm = pe.matmul(o, xl, wh, start=False, stop=last, skip_group_check=skip)
                        mm.then_inc(tile_used, 1)
                        at["tile"] += 1
                        if after and (g, kt) in after:
                            after[g, kt]()
                    at["prod"] += 1
                if name == "k":
                    at["k_done"] = at["prod"]

            def transposes(src, banks, tok=0):
                at["tok"] += tok
                if at["tok"]:
                    pe.wait_ge(tok_ready, at["tok"])
                for b in range(banks):
                    n = at["col"]
                    if n >= 2:
                        pe.wait_ge(cols_drained, n - 1)
                    for off, v in src(b):
                        rows_, cols_ = v.shape
                        mm = pe.transpose(psum[0:cols_, TR + n % 2, off:off + rows_], v, ident[0:rows_, 0:rows_])
                    mm.then_inc(cols_filled, 1)
                    at["col"] += 1

            def two_chunks(buf, c0=0):
                return lambda b: [(256 * e + P * h, buf[:, h, (c0 + 2 * b + e) * P:(c0 + 2 * b + e + 1) * P])
                                  for e in range(2) for h in range(HALVES)]

            def row_ready(name):
                n = row_at[name]
                pe.wait_ge(row_loaded[n % 2], 16 * (n // 2 + 1))

            def brow(name, lo, n):
                return row[0:1, row_at[name] % 2, lo:lo + n]

            def columns_of(buf, banks=4):
                ready = [at["col"] + 1 + b for b in range(banks)]
                transposes(two_chunks(buf), banks, HALVES)
                return ready

            def residual_product(name, high, low, buf, bias=None, ready=None, after=None):
                state_ = {}

                def part(g):
                    def run():
                        state_[g] = [at["col"] + 1, at["col"] + 2]
                        transposes(two_chunks(buf, 4 * g), 2, HALVES)
                    return run

                tile = 6 if plan[at["plan"]]["tiles"] == 8 else 2
                product(name, high, low, range(2), bias, ready, {**(after or {}), (1, tile): part(0)})
                later = [at["col"] + 1, at["col"] + 2]
                return state_[0] + later, {(0, 1): part(1)}

            def root_rows():
                pe.wait_ge(rstd_ready, at["norm"])
                n = at["col"]
                pe.wait_ge(cols_drained, n - 1)
                for h in range(HALVES):
                    mm = pe.transpose(psum[0:1, TR + n % 2, P * h:P * h + P], rms_col[:, h:h + 1], ident)
                mm.then_inc(cols_filled, 1)
                at["col"] += 1
                at["rms_row"] = at["col"]

            def conv_mixer(ready, after):
                transposes(two_chunks(xn), 4, HALVES)
                mem_ready = [at["col"]] * 4
                pe.wait_ge(mixer_in, 32)
                transposes(lambda b: [(32 * e, dw_tok[:, (4 * b + e) * P:(4 * b + e + 1) * P]) for e in range(4)], 2)
                row_ready("b_a")
                row_ready("b_gate")
                at["norm"] = 2
                root_rows()
                pe.wait_ge(cols_drained, at["rms_row"])
                rms = lambda h: rms_row[0:1, h * P:(h + 1) * P]
                product("conv_in", xT_high, xT_low, range(4),
                        lambda g, h: [(rms(h), brow("b_a", 256 * g, 256), 0, 256), (rms(h), brow("b_gate", 256 * g, 256), 256, 512)],
                        ready)
                transposes(two_chunks(z_tok), 4, 1)
                pe.wait_ge(cols_drained, at["col"])
                pe.wait_ge(mixer_zero, 2)
                n = 0
                for c in range(CONV_DVE, KC):
                    j = c - CONV_DVE
                    for t in range(TAPS):
                        pe.wait_ge(tap_ready, n + 1)
                        mm = pe.matmul(psum[:, 6 + j // 2, T * (j % 2):T * (j % 2) + T], tap_diag[:, n % 4, :], zT[:, c, t:t + T],
                                       start=(t == 0), stop=(t == TAPS - 1))
                        mm.then_inc(tap_used, 1)
                        n += 1
                pe.wait_ge(tap_used, n)
                pe.sem_inc(conv_filled, 1)
                product("k", memT_high, memT_low, [0], ready=mem_ready)
                transposes(lambda b: [(P * e, conv[:, 4 * (b % 2) + e, (b // 2) * P:(b // 2 + 1) * P]) for e in range(4)], 4, 1)
                product("k", memT_high, memT_low, [1])
                pe.wait_ge(act_out, 9)
                ready = [at["col"] + 1 + b for b in range(4)]
                transposes(two_chunks(z_tok), 4)
                row_ready("conv_bo")
                return residual_product("conv_out", xT_high, xT_low, xn,
                                        lambda g, h: [(ones[0:1, :], brow("conv_bo", COLS * g, COLS), 0, COLS)], ready,
                                        {(0, 3): key_columns})

            def key_columns():
                pe.wait_ge(group_drained, at["k_done"])
                transposes(lambda b: [(256 * e + P * h, k_tok[:, b // 2, h, (2 * (b % 2) + e) * P:(2 * (b % 2) + e + 1) * P])
                                      for e in range(2) for h in range(HALVES)], 4)

            def sgu_mixer(ready, after):
                after = dict(after)
                part = after.pop((0, 1))
                part()
                transposes(two_chunks(xn), 4, HALVES)
                pe.wait_ge(mixer_in, 16 * MIXER_LOADS[2])
                transposes(lambda b: [(P * e, ws_in[:, 4 * b + e, :]) for e in range(4)] if b < 2 else [(0, bs_in[:, :])], 3)
                at["norm"] = 8
                root_rows()
                pe.wait_ge(cols_drained, at["rms_row"])
                for g in range(8):
                    name = f"sgu_bias{g // 2}"
                    row_ready(name)
                    product("sgu_in", xT_high, xT_low, [g],
                            lambda g, h: [(rms_row[0:1, h * P:(h + 1) * P], brow(f"sgu_bias{g // 2}", COLS * (g % 2), COLS), 0, COLS)],
                            ready if g == 0 else None)
                at["tok"] += 1
                pe.wait_ge(tok_ready, at["tok"])
                for h in range(HALVES):
                    for gp in range(4):
                        n = at["score"]
                        pe.wait_ge(scores_used, n - 1)
                        for e in range(2):
                            g = 2 * gp + e
                            mm = pe.matmul(psum[:, 6 + n % 2, 256 * e:256 * e + 256], wsT[:, g, :], g_tok[:, h, 256 * g:256 * g + 256],
                                           start=True, stop=True)
                        mm.then_inc(scores_filled, 1)
                        at["score"] += 1
                pe.wait_ge(scores_used, at["score"])
                ready = [at["col"] + 1 + b for b in range(8)]
                transposes(two_chunks(u_tok), 8)
                return residual_product("sgu_out", yT_high, sgu_low, xn, None, ready)

            def ret_mixer(ready, after):
                product("ret_in", xT_high, xT_low, range(12), None, ready, after)
                for j in range(2):
                    transposes(two_chunks(qk[j]), 4, 1 - j)
                pe.wait_ge(cols_drained, at["col"])
                for hd in range(XH):
                    n = at["score"]
                    pe.wait_ge(scores_used, n - 1)
                    for s_, t0, c0 in ((0, 0, 0), (1, P, 2 * P)):
                        for c in range(2):
                            mm = pe.matmul(psum[:, 6 + n % 2, c0:c0 + T - t0], qkT[1][:, 2 * hd + c, s_ * P:(s_ + 1) * P],
                                           qkT[0][:, 2 * hd + c, t0:T], start=(c == 0), stop=(c == 1))
                    mm.then_inc(scores_filled, 1)
                    at["score"] += 1
                decayed = at["score"]
                for h in range(HALVES):
                    for hd in range(XH):
                        n = at["score"]
                        pe.wait_ge(scores_used, n - 1 if h or hd > 1 else decayed)
                        v = [rv[:, s_, 512 * hd:512 * hd + 512] for s_ in range(2)]
                        if h == 0:
                            mm = pe.matmul(bank(6 + n % 2), sc[:, hd, 0:P], v[0], start=True, stop=True)
                        else:
                            pe.matmul(bank(6 + n % 2), sc[:, hd, P:2 * P], v[0], start=True, stop=False)
                            mm = pe.matmul(bank(6 + n % 2), sc[:, hd, 2 * P:3 * P], v[1], start=False, stop=True)
                        mm.then_inc(scores_filled, 1)
                        at["score"] += 1
                ready = [at["col"] + 1 + b for b in range(8)]
                transposes(two_chunks(o_tok), 8, 1)
                transposes(two_chunks(xn), 4, HALVES)
                return residual_product("ret_out", yT_high, ret_low, xn, None, ready)

            lanes = [0, 0]

            def lane_bank(j):
                n = lanes[j]
                if n >= 4:
                    pe.wait_ge(lane_used[j], n - 3)
                return 4 * j + n % 4

            def lane_done(j, mm):
                mm.then_inc(lane_filled[j], 1)
                lanes[j] += 1
                return lanes[j]

            def lane_ready(j, n):
                pe.wait_ge(lane_used[j], n)

            def rwkv_mixer(ready, after):
                transposes(two_chunks(xn), 4, HALVES)
                pe.wait_ge(mixer_in, 16 * MIXER_LOADS[1])
                transposes(lambda b: [(6 * e, mix_in[:, e * P:(e + 1) * P]) for e in range(KC)], 1)
                pe.wait_ge(group_drained, at["prod"])
                pe.wait_ge(cols_drained, at["col"])
                pe.wait_ge(scores_used, at["score"])
                for j, (m, width) in enumerate(((1, 64), (4, 64), (5, P))):
                    at["tok"] += 1
                    pe.wait_ge(tok_ready, at["tok"])
                    src = (xs, xs_b, xs)[j]
                    hid = [(lora[j], 0, width)] + ([(lora[0], P, 32)] if j == 2 else [])
                    for buf, o, k in hid:
                        b = lane_bank(0)
                        for c in range(KC):
                            mm = pe.matmul(psum[0:k, b, 0:T], lora1[j][:, c, o:o + k], src[:, c, :], start=(c == 0), stop=(c == KC - 1))
                        ready = lane_done(0, mm)
                    lane_ready(0, ready)
                    if j < 2:
                        row_ready(("w0", "a0")[j])
                    for h in range(HALVES):
                        for n in range(2):
                            b = lane_bank(0)
                            cols = slice(COLS * n, COLS * n + COLS)
                            if j < 2:
                                pe.matmul(bank(b), ones[0:1, :], brow(("w0", "a0")[j], COLS * n, COLS), start=True, stop=False)
                                mm = pe.matmul(bank(b), lora[j][0:64, h * P:(h + 1) * P], lora2[j][:, cols], start=False, stop=True)
                            else:
                                pe.matmul(bank(b), lora[2][:, h * P:(h + 1) * P], lora2[2][:, cols], start=True, stop=False)
                                mm = pe.matmul(bank(b), lora[0][0:32, h * P:(h + 1) * P], lora2[3][:, cols], start=False, stop=True)
                            lane_done(0, mm)
                lane_ready(0, lanes[0])
                for m in range(3):
                    at["tok"] += 1
                    pe.wait_ge(tok_ready, at["tok"])
                    product("rkv", xT_high, xT_low, range(2))
                at["tok"] += 1
                pe.wait_ge(tok_ready, at["tok"])
                pe.wait_ge(group_drained, at["prod"])
                for h in range(HALVES):
                    for n in range(2):
                        b = lane_bank(1)
                        mm = pe.matmul(bank(b), masks[:, M_CUM, :], lw[:, h, COLS * n:COLS * n + COLS], start=True, stop=True)
                        lane_done(1, mm)
                b = lane_bank(0)
                for h in range(HALVES):
                    for n in range(NH):
                        o = (h * NH + n) * 2
                        mm = pe.matmul(psum[0:HD, b, o:o + 2], lw[:, h, HD * n:HD * n + HD], masks[:, M_CHUNK, 0:2], start=True, stop=True)
                lane_done(0, mm)
                at["tok"] += 1
                pe.wait_ge(tok_ready, at["tok"])
                for h in range(HALVES):
                    for hg in range(2):
                        def head(buf, n):
                            return buf[:, h, 512 * hg + HD * n:512 * hg + HD * n + HD]

                        for src in (kk, ra, rk, rr):
                            for sb in range(2):
                                b = lane_bank(0)
                                for e in range(4):
                                    mm = pe.transpose(psum[0:HD, b, P * e:P * e + P], head(src, 4 * sb + e), ident)
                                ready = lane_done(0, mm)
                        lane_ready(0, ready)
                        for sb in range(2):
                            for l, r in ((bT, aT), (kkT, aT), (bT, rT), (kkT, rT), (aT, bT)):
                                b = lane_bank(1)
                                for e in range(4):
                                    n = 4 * sb + e
                                    mm = pe.matmul(psum[:, b, P * e:P * e + P], l[:, n, :], r[:, n, :], start=True, stop=True)
                                lane_done(1, mm)
                        at["tok"] += 2
                        pe.wait_ge(tok_ready, at["tok"])
                        inv_at = [[lanes[1]] * 2, [lanes[1]] * 2]
                        for level in range(1, LEVELS):
                            q_at = []
                            for sb in range(2):
                                lane_ready(1, inv_at[sb][0])
                                b = lane_bank(1)
                                for e in range(4):
                                    n = 4 * sb + e
                                    mm = pe.matmul(psum[:, b, P * e:P * e + P], abT[:, n, :], inv[:, n, :], start=True, stop=True)
                                q_at.append(lane_done(1, mm))
                            for sb in range(2):
                                lane_ready(1, q_at[sb])
                                for which in ((0, 1) if level < LEVELS - 1 else (1,)):
                                    b = lane_bank(1)
                                    for e in range(4):
                                        n = 4 * sb + e
                                        l, r = (invT, lvl) if which == 0 else (lvl, invT)
                                        mm = pe.matmul(psum[:, b, P * e:P * e + P], l[:, n, :], r[:, n, :], start=True, stop=True)
                                    inv_at[sb][which] = lane_done(1, mm)
                        lane_ready(1, lanes[1])
                        for sb in range(2):
                            b = lane_bank(0)
                            for e in range(4):
                                n = 4 * sb + e
                                mm = pe.matmul(psum[0:HD, b, P * e:P * e + P], head(kk, n), invT[:, n, :], start=True, stop=True)
                            lane_done(0, mm)
                        for l, r in ((akT, lambda n: head(rvv, n)), (invT, lambda n: hh[:, n, :])):
                            b = lane_bank(0)
                            for n in range(8):
                                mm = pe.matmul(psum[:, b, HD * n:HD * n + HD], l[:, n, :], r(n), start=True, stop=True)
                            ready = lane_done(0, mm)
                            lane_ready(0, ready)
                        yb = lane_bank(0)
                        for n in range(8):
                            pe.matmul(psum[:, yb, HD * n:HD * n + HD], rkT[:, n, :], head(rvv, n), start=(n == 0), stop=False, skip_group_check=True)
                        for c in range(2):
                            rs = slice(CH * c, CH * c + CH)
                            b = lane_bank(1)
                            for n in range(8):
                                mm = pe.matmul(psum[rs, b, HD * n:HD * n + HD], wT[:, n, rs], state[:, 8 * hg + n, :], start=True, stop=True)
                            u_at = lane_done(1, mm)
                            for n in range(8):
                                pe.matmul(psum[rs, yb, HD * n:HD * n + HD], rT[:, n, rs], state[:, 8 * hg + n, :], start=False, stop=False,
                                          skip_group_check=True)
                            lane_ready(1, u_at)
                            b = lane_bank(1)
                            for n in range(8):
                                pe.matmul(psum[0:HD, b, HD * n:HD * n + HD], head(ra, n)[rs, :], uu[rs, n, :], start=True, stop=False)
                                mm = pe.matmul(psum[0:HD, b, HD * n:HD * n + HD], head(rk, n)[rs, :], head(rvv, n)[rs, :], start=False, stop=True)
                            s_at = lane_done(1, mm)
                            lane_ready(1, s_at)
                        for n in range(8):
                            mm = pe.matmul(psum[:, yb, HD * n:HD * n + HD], rbT[:, n, :], uu[:, n, :], start=False, stop=(n == 7), skip_group_check=True)
                        ready = lane_done(0, mm)
                        lane_ready(0, ready)
                lane_ready(1, lanes[1])
                ready = [at["col"] + 1 + b for b in range(4)]
                transposes(two_chunks(rr), 4, 1)
                transposes(two_chunks(xn), 4, HALVES)
                return residual_product("rwkv_out", xT_high, xT_low, xn, None, ready)

            pe.wait_ge(const_loaded, 16)
            pe.wait_ge(mixer_zero, 1)
            ready, after = columns_of(xg), {}
            for i in range(layers):
                mixer = [conv_mixer, rwkv_mixer, sgu_mixer, ret_mixer][i]
                ready, after = mixer(ready, after)
                if i:
                    after[(0, 1)]()
                    product("k", memT_high, memT_low, range(2))
                    key_columns()
                    after = {}
                product("q", xT_high, xT_low, range(2), None, ready, after)
                pe.wait_ge(group_drained, at["prod"])
                transposes(two_chunks(q_tok), 4)
                product("v", memT_high, memT_low, [0])
                pe.wait_ge(cols_drained, at["col"])
                for h in range(HALVES):
                    for hp in range(XH // 2):
                        n = at["score"]
                        if n >= 2:
                            pe.wait_ge(scores_used, n - 1)
                        for e in range(2):
                            hd = 2 * hp + e
                            for c in range(2):
                                mm = pe.matmul(psum[:, 6 + n % 2, e * T:(e + 1) * T], qT[:, 2 * hd + c, h * P:(h + 1) * P],
                                               kT[:, 2 * hd + c, :], start=(c == 0), stop=(c == 1))
                        mm.then_inc(scores_filled, 1)
                        at["score"] += 1
                product("v", memT_high, memT_low, [1])
                transposes(lambda b: [(256 * m + P * h, prob[:, h, b, m * P:(m + 1) * P]) for m in range(2) for h in range(HALVES)],
                           4, HALVES * XH)
                pe.wait_ge(group_drained, at["prod"])
                prob_at = at["col"] - 3
                ready = []
                for hd in range(XH):
                    n = at["score"]
                    pe.wait_ge(cols_drained, prob_at + hd)
                    pe.wait_ge(scores_used, n - 1)
                    for e in range(2):
                        c = 2 * hd + e
                        for m in range(2):
                            mm = pe.matmul(psum[:, 6 + n % 2, e * T:(e + 1) * T], v_tok[:, m, c * P:(c + 1) * P],
                                           probT[:, hd, m, :], start=(m == 0), stop=(m == 1))
                    mm.then_inc(scores_filled, 1)
                    at["score"] += 1
                pe.wait_ge(scores_used, at["score"])
                ready, after = residual_product("wo", xT_high, xT_low, xg)
                for g in range(11):
                    product("gate_up", xT_high, xT_low, [g], None, ready if g == 0 else None, after if g == 0 else None)
                    if g:
                        pe.wait_ge(group_drained, at["prod"] - 1)
                        transposes(lambda b: [(256 * e + P * h, htok[:, (g - 1) % 2, h, e * P:(e + 1) * P])
                                              for e in range(2) for h in range(HALVES)], 1)
                pe.wait_ge(group_drained, at["prod"])
                transposes(lambda b: [(256 * e + P * h, htok[:, 0, h, e * P:(e + 1) * P])
                                      for e in range(2) for h in range(HALVES)], 1)
                ready = [at["col"]] * 11
                ready[0:10] = [at["col"] - 1] * 10
                if i + 1 < layers and i != 0:
                    ready, after = residual_product("down", hT_high, hT_low, xg, None, ready)
                else:
                    product("down", hT_high, hT_low, range(2), None, ready)


def kernel(**inputs):
    import concourse.bacc as _bacc
    from concourse import mybir as _mybir
    from concourse.bass_utils import run_bass_kernel_spmd as _run

    arrays = {f"in_{name}": np.ascontiguousarray(a) for name, a in inputs.items()}
    arrays["in_masks"] = constant_masks()
    arrays["in_rotary"] = rotary_tables()
    arrays["in_decay"] = decay_masks()
    nc = _bacc.Bacc("TRN2", target_bir_lowering=False, num_devices=1)
    w = {name[3:]: nc.dram_tensor(name, a.shape, _mybir.dt.from_np(a.dtype), kind="ExternalInput").ap()
         for name, a in arrays.items()}
    out = nc.dram_tensor("out", (1, T, D), _mybir.dt.float32, kind="ExternalOutput").ap()
    trunk_program(nc, w, out, 4)
    return _run(nc, [arrays], core_ids=[0]).results[0]["out"]
```

```python
import numpy as np
import concourse.bass as bass
from concourse import mybir

P = 128
D = 1024
T = 256
HALVES = T // P
KC = D // P
COLS = 512
F = 2816
FC = F // P
E2 = 2 * D
TAPS = 31
HD = 64
NH = D // HD
CH = 64
XH = 4
HW = D // XH
RAW, SPLIT, LOOK = 4, 8, 4
CONV_DVE = 4
UNIT_BANKS = 4 + 1 + 2 * 5 + 3
WARM = 7
MIXER_LOADS = [2, 11, 13, 16]

M_IDENT, M_CUM, M_STRICT, M_INCL, M_PAIR_T, M_LEVEL = 0, 1, 2, 3, 4, 5
LEVELS = 6
M_CHUNK = M_LEVEL + LEVELS
M_TRI_ALL = M_CHUNK + 1
N_MASKS = M_TRI_ALL + 1


def constant_masks():
    r = np.arange(P)[:, None]
    c = np.arange(P)[None, :]
    same = (r // CH) == (c // CH)
    m = np.zeros((N_MASKS, P, P), np.float32)
    m[M_IDENT] = r == c
    m[M_CUM] = same & (r <= c)
    m[M_STRICT] = same & (r < c)
    m[M_INCL] = same & (r <= c)
    for n in range(LEVELS):
        b = 1 << n
        m[M_LEVEL + n] = ((r // (2 * b)) == (c // (2 * b))) & ((r // b) % 2 == 1) & ((c // b) % 2 == 0)
    m[M_PAIR_T] = m[M_LEVEL].T
    m[M_CHUNK][:, 0] = (np.arange(P) < CH)
    m[M_CHUNK][:, 1] = (np.arange(P) >= CH)
    m[M_TRI_ALL] = r <= c
    return np.ascontiguousarray(m.transpose(1, 0, 2).reshape(P, N_MASKS * P))


def rotary_tables():
    angle = np.repeat(np.float32(1.0) / (np.float32(10000.0) ** np.linspace(0.0, 1.0, HW // 2, dtype=np.float32)), 2)
    theta = np.arange(T, dtype=np.float32)[:, None] * angle.astype(np.float32)[None]
    sin = np.sin(theta).astype(np.float32)
    sin[:, 0::2] *= -1.0
    return np.stack([np.cos(theta).astype(np.float32), sin])


def decay_masks():
    lg = np.log(1.0 - 2.0 ** (-5.0 - np.arange(XH, dtype=np.float64)))
    s = np.arange(P)[:, None]
    t = np.arange(P)[None, :]
    out = np.zeros((P, XH, 3, P), np.float64)
    for h in range(XH):
        out[:, h, 0] = np.where(t >= s, np.exp(lg[h] * np.maximum(t - s, 0)), 0.0)
        out[:, h, 1] = np.exp(lg[h] * (t + P - s))
        out[:, h, 2] = out[:, h, 0]
    return (out * HW ** -0.5).astype(np.float32).reshape(P, XH * 3 * P)


def weight_plan(w, layers):
    plan = []

    def product(name, src, rows, cols, paired=False):
        plan.append(dict(name=name, src=src, tiles=rows // 256, groups=cols // COLS, paired=paired))

    for i in range(layers):
        if i == 0:
            product("conv_in", w["conv_w_in"][0], D, 2 * D, True)
            product("k", w["xattn_wkv"][i, :, 0:D], D, D)
            product("conv_out", w["conv_w_out"][0], D, D)
        if i == 1:
            for m in (1, 0, 2):
                product("rkv", w["rwkv_w_rkv"][0, m], D, D)
            product("rwkv_out", w["rwkv_w_o"][0], D, D)
        if i == 2:
            product("sgu_in", w["sgu_w_in"][0], D, 2 * E2)
            plan[-1]["order"] = [4, 5, 6, 7, 0, 1, 2, 3]
            product("sgu_out", w["sgu_w_out"][0], E2, D)
        if i == 3:
            product("ret_in", w["ret_w_in"][0], D, 6 * D)
            product("ret_out", w["ret_w_out"][0], E2, D)
        if i:
            product("k", w["xattn_wkv"][i, :, 0:D], D, D)
        product("q", w["xattn_wq"][i], D, D)
        product("v", w["xattn_wkv"][i, :, D:2 * D], D, D)
        product("wo", w["xattn_wo"][i], D, D)
        product("gate_up", w["ffn_w_gate_up"][i], D, 2 * F, True)
        product("down", w["ffn_w_down"][i], F, D)
    tile = group = 0
    for p in plan:
        p["tile0"], p["group0"] = tile, group
        tile += p["tiles"] * p["groups"]
        group += p["groups"]
    return plan


def row_plan(w, layers):
    rows = []
    for i in range(layers):
        rows.append((f"mix{i}", w["mix_norm_g"][i:i + 1, :], True))
        if i in (0, 2):
            rows.append((f"mem{i}", w["mem_norm_g"][i:i + 1, :], True))
        if i == 0:
            b = w["conv_b_in"]
            rows += [("b_a", b[:, 0:D], False), ("b_gate", b[:, D:2 * D], False),
                     ("conv_g", w["conv_ln_g"], True), ("conv_b", w["conv_ln_b"], True)]
        if i == 1:
            rows += [(n, w["rwkv_" + n] if n != "r_k" else w["rwkv_r_k"].rearrange("a h n -> a (h n)"), True)
                     for n in ("k_k", "k_a", "r_k", "gn_g", "gn_b")]
        if i == 2:
            for name, src, j in SGU_ROWS:
                rows.append((f"{name}{j}", w[src][:, j * D:(j + 1) * D], name != "sgu_bias"))
        if i in (1, 3):
            rows.append((f"mem{i}", w["mem_norm_g"][i:i + 1, :], True))
        if i == 0:
            rows.append(("conv_bo", w["conv_b_out"], False))
        rows.append((f"xattn{i}", w["xattn_norm_g"][i:i + 1, :], True))
        rows.append((f"ffn{i}", w["ffn_norm_g"][i:i + 1, :], True))
    rows.append(("final", w["final_norm_g"].rearrange("(a n) -> a n", a=1), True))
    return rows


SGU_ROWS = [("sgu_bias", "sgu_b_in", 2), ("sgu_bias", "sgu_b_in", 3), ("sgu_bias", "sgu_b_in", 0), ("sgu_g", "sgu_ln_g", 0),
            ("sgu_bias", "sgu_b_in", 1), ("sgu_b", "sgu_ln_b", 0), ("sgu_g", "sgu_ln_g", 1), ("sgu_b", "sgu_ln_b", 1)]


def small_plan(layers):
    events = []
    for i in range(layers):
        if i == 1:
            events += [("rms", None), ("drop", "mix1"),
                       ("pow", "kk"), ("drop", "k_k"), ("drop", "k_a"), ("drop", "r_k"),
                       ("pow", "gn"), ("pow", "gn"), ("pow", "gn"), ("pow", "gn"), ("drop", "gn_g"), ("drop", "gn_b"), ("drop", "mem1")]
        else:
            events += [("drop", f"mix{i}")] + [("rms", None)] * (2 if i == 0 else 1)
        if i == 0:
            events += [("drop", "mem0"), ("drop", "b_a"), ("drop", "b_gate"), ("pow", "ln"), ("drop", "conv_g"),
                       ("drop", "conv_b")]
        if i == 2:
            events += [("drop", "mem2"), ("drop", "sgu_bias2"), ("drop", "sgu_bias3"), ("pow", "ln")]
            events += [("drop", f"{name}{j}") for name, _, j in SGU_ROWS[2:]]
        if i == 3:
            events += [("pow", "ret"), ("drop", "mem3")]
        events += [("drop", "conv_bo")] * (i == 0) + [("drop", f"xattn{i}"), ("rms", None), ("drop", f"ffn{i}"), ("rms", None)]
    return events + [("rms", None), ("drop", "final")]


def trunk_program(nc, w, out, layers):
    f32, f32r = mybir.dt.float32, mybir.dt.float32r
    ALU, ACT, AX = mybir.AluOpType, mybir.ActivationFunctionType, mybir.AxisListType
    plan = weight_plan(w, layers)
    rows = row_plan(w, layers)
    row_at = {name: n for n, (name, _, _) in enumerate(rows)}

    KB = 1024
    cursor = [(nc.sbuf_base + 63) // 64 * 64]

    def place(name, shape, dtype, at=None):
        size = 4 * int(np.prod(shape[1:]))
        if at is None:
            at = cursor[0]
            cursor[0] += (size + 63) // 64 * 64
        assert at + size <= nc.sbuf_usable_end, (name, at, size, nc.sbuf_usable_end)
        return nc.alloc_sbuf_tensor_at(name, shape, dtype, offset=at)

    raw = place("raw_weights", [P, RAW, 2, COLS], f32)
    w_high = place("weights_high", [P, SPLIT, 2, COLS], f32r)
    w_low = place("weights_low", [P, SPLIT, 2, COLS], f32r)
    x = place("x", [P, HALVES, D], f32)
    mem = place("mem", [P, HALVES, D], f32)
    row = place("rows", [P, 2, D], f32)
    masks = place("masks", [P, N_MASKS, P], f32)
    ones = place("ones", [1, P], f32)
    sums = place("square_sums", [P, HALVES, 2], f32)
    mean_sq = place("mean_square", [P, HALVES], f32)
    rstd = place("rstd", [P, HALVES], f32)
    rms_col = place("rms_col", [P, HALVES], f32)
    rms_row = place("rms_row", [1, T], f32)
    neg_half = place("neg_half", [P, NH], f32)
    stat = place("stat", [P, HALVES], f32)
    scratch_at = cursor[0]
    scratch = place("scratch", [P, COLS], f32)
    bn = place("bn", [P, HALVES, 4, 6], f32)
    mv = place("mean_var", [P, HALVES, 2], f32)
    den = place("softmax_den", [P, 3, HALVES * XH], f32)
    taps = place("taps", [P, KC, 32], f32)
    small = place("head_stats", [P, 6, NH], f32, cursor[0] - KB)
    pc = place("chunk_decay", [P, HALVES, NH // 2, 2], f32, cursor[0] - KB + 384)
    mix_cols = place("mix_columns", [P, KC, 6], f32, cursor[0] - KB + 640)
    XT0 = cursor[0]
    xT_high = place("xT_high", [P, KC, T], f32r)
    xT_low = place("xT_low", [P, KC, T], f32r)
    ARENA = cursor[0]
    memT_high = place("memT_high", [P, KC, T], f32r, ARENA)
    memT_low = place("memT_low", [P, KC, T], f32r, ARENA + 8 * KB)
    kT = place("kT", [P, KC, T], f32, ARENA + 16 * KB)
    v_tok = place("v_tok", [P, HALVES, D], f32, ARENA + 24 * KB)
    BIG = ARENA + 32 * KB
    hT_high = place("hT_high", [P, FC, T], f32r, BIG)
    hT_low = place("hT_low", [P, FC, T], f32r, BIG + 22 * KB)
    sgate = place("silu_gate", [P, HALVES, 2, 256], f32, ARENA + 24 * KB)
    htok = place("h_tok", [P, HALVES, 2, 256], f32, ARENA + 28 * KB)
    k_tok = place("k_tok", [P, 2, HALVES, COLS], f32, BIG + 36 * KB)
    xn = place("x_normed", [P, HALVES, D], f32, BIG + 36 * KB)
    xg = place("x_gained", [P, HALVES, D], f32, ARENA + 16 * KB)
    q_tok = place("q_tok", [P, HALVES, D], f32, BIG)
    qT = place("qT", [P, KC, T], f32, BIG + 8 * KB)
    prob = place("prob", [P, HALVES, XH, T], f32, BIG + 16 * KB)
    probT = place("probT", [P, XH, HALVES, T], f32, BIG + 24 * KB)
    yT_high = place("yT_high", [P, 2 * KC, T], f32r, XT0)

    psum = nc.alloc_psum_tensor("psum", [P, 8, COLS], f32)
    TR = 4

    def sem(name):
        return nc.alloc_semaphore(name)

    raw_loaded = [sem(f"raw_loaded{s}") for s in range(RAW)]
    w_high_ready = sem("w_high_ready")
    w_low_ready = sem("w_low_ready")
    tile_used = sem("tile_used")
    group_drained = sem("group_drained")
    cols_filled = sem("cols_filled")
    cols_high = sem("cols_high")
    cols_drained = sem("cols_drained")
    x_loaded = sem("x_loaded")
    const_loaded = sem("const_loaded")
    row_loaded = [sem(f"row_loaded{s}") for s in range(2)]
    row_used = sem("row_used")
    vec_step = sem("vec_step")
    squares_summed = sem("squares_summed")
    rstd_ready = sem("rstd_ready")
    stat_ready = sem("stat_ready")
    root_ready = sem("root_ready")
    pool_step = sem("pool_step")
    rms_copied = sem("rms_copied")
    tok_ready = sem("tok_ready")
    scores_filled = sem("scores_filled")
    scores_used = sem("scores_used")
    neg_max = sem("neg_max")
    exp_done = sem("exp_done")
    act_out = sem("act_out")
    vec_out = sem("vec_out")
    mem_scaled = sem("mem_scaled")
    result_ready = sem("result_ready")
    stored = sem("stored")
    mixer_in = sem("mixer_in")
    mix_loaded = sem("mix_loaded")
    mixer_free = sem("mixer_free")
    mixer_zero = sem("mixer_zero")
    tap_ready = sem("tap_ready")
    tap_used = sem("tap_used")
    conv_filled = sem("conv_filled")
    square_summed = sem("square_summed")
    lane_filled = [sem(f"lane_filled{j}") for j in range(2)]
    lane_used = [sem(f"lane_used{j}") for j in range(2)]
    y_part = sem("y_part")

    ident = masks[:, M_IDENT, :]

    z_tok = place("z_tok", [P, HALVES, D], f32, BIG)
    zT = place("zT", [P, KC, T + TAPS - 1], f32, BIG + 8 * KB)
    conv = place("conv", [P, KC, T], f32, BIG + 18 * KB)
    sig = place("sig", [P, 2, HALVES, 256], f32, BIG + 26 * KB)
    dw_tok = place("dw_tok", [32, D], f32, BIG + 30 * KB)
    tap_diag = place("tap_diagonals", [P, 4, P], f32, scratch_at)
    u_tok = place("u_tok", [P, HALVES, E2], f32, BIG)
    g_tok = place("g_tok", [P, HALVES, E2], f32, BIG + 16 * KB)
    gate_low = place("gate_low", [P, 2 * KC, T], f32r, BIG + 16 * KB)
    ws_in = place("ws_in", [P, 8, P], f32, ARENA + 24 * KB)
    wsT = place("wsT", [P, 8, P], f32, ARENA + 28 * KB)
    bs_in = place("bs_in", [8, P], f32, BIG + 32 * KB)
    bsT = place("bsT", [P, 8], f32, BIG + 33 * KB)
    sgu_low = place("sgu_low", [P, 2 * KC, T], f32r, BIG + 16 * KB)

    qk = [place(f"ret_{n}", [P, HALVES, D], f32, ARENA + 8 * KB * j) for j, n in enumerate("qk")]
    o_tok = place("o_tok", [P, HALVES, E2], f32, ARENA)
    rv = place("ret_v", [P, HALVES, E2], f32, ARENA + 16 * KB)
    ret_low = place("ret_low", [P, 2 * KC, T], f32r, ARENA + 16 * KB)
    rg = place("ret_gate", [P, HALVES, E2], f32, ARENA + 32 * KB)
    rotary = place("rotary_cs", [P, 2, HALVES, HW], f32, ARENA + 48 * KB)
    decay = place("decay", [P, XH, 3 * P], f32, ARENA + 52 * KB)
    sc = place("ret_scores", [P, XH, 3 * P], f32, ARENA + 58 * KB)
    rtmp = place("rot_tmp", [P, XH, HW // 2, 2], f32, ARENA + 64 * KB)
    qkT = [place(f"ret_{n}T", [P, KC, T], f32, XT0 + 8 * KB * j) for j, n in enumerate("qk")]
    hT = place("hT", [P, KC, T + 1], f32, ARENA)
    diff = place("shift_diff", [P, KC, T], f32, ARENA + 8 * KB + 256)
    xs = place("xs", [P, KC, T], f32, ARENA + 16 * KB + 256)
    W0 = ARENA + 24 * KB + 256
    rr, rk, rvv, lw, ra, rgate = [place("rwkv_" + n, [P, HALVES, D], f32, W0 + 8 * KB * j)
                                  for j, n in enumerate(["r", "k", "v", "lw", "a", "gate"])]
    xs_b = place("xs_b", [P, KC, T], f32, W0 + 16 * KB)
    mix_in = place("mix_in", [6, D], f32, W0 + 32 * KB)
    lora = [place(f"lora_hidden{j}", [P, T], f32, W0 + (48 + j) * KB) for j in range(3)]
    lora1 = [place("lora1_" + n, [P, KC, k], f32, XT0 + o) for n, k, o in (("w", 64, 0), ("a", 64, 2 * KB), ("g", 160, 4 * KB))]
    lora2 = [place("lora2_" + n, [k, D], f32, W0 + 4 * KB * j)
             for j, (n, k) in enumerate((("w", 65), ("a", 65), ("g", P), ("g_rest", 32)))]
    kk = place("kk", [P, HALVES, D], f32, ARENA)
    U0 = ARENA + 8 * KB + 256
    tmp = [place(f"tmp{j}", [P, D], f32, U0 + 4 * KB * j) for j in range(2)]
    exps = [place(f"exp{j}", [P, COLS], f32, U0 + 2 * KB * j) for j in range(3)]
    aT, bT, kkT = [place("chunk_" + n, [P, 4, P], f32, XT0 + 2 * KB * j) for j, n in enumerate(["aT", "bT", "kT"])]
    rTs = [place("chunk_rT0", [P, 4, P], f32, XT0 + 6 * KB), place("chunk_rT1", [P, 4, P], f32, W0 + 48 * KB)]
    fronts = [[aT, bT, kkT, rTs[u]] for u in range(2)]
    inv, invT = [place("chunk_" + n, [P, 8, P], f32, XT0 + (8 + 4 * j) * KB) for j, n in enumerate(["inv", "invT"])]
    lvl, abT, akT, rbT = [place("chunk_" + n, [P, 8, P], f32, U0 + 4 * KB * j) for j, n in enumerate(["level", "abT", "akT", "rbT"])]
    rkT = place("chunk_rkT", [P, 8, P], f32, U0)
    wT = place("chunk_wT", [P, 4, P], f32, W0 + 30 * KB)
    hh = place("chunk_h", [P, 8, HD], f32, W0 + 24 * KB)
    uu = place("chunk_u", [P, 8, HD], f32, W0 + 24 * KB)
    zz = place("chunk_z", [P, 8, HD], f32, W0 + 26 * KB)
    state = place("state", [P, NH // 2, HD], f32, W0 + 28 * KB)

    def bank(b):
        return psum[:, b, :]

    def source(p, g, kt):
        if p["paired"]:
            half = p["groups"] * 256
            v = p["src"].rearrange("(k p) n -> p k n", p=P)
            return [v[:, 2 * kt:2 * kt + 2, a * half + 256 * g:a * half + 256 * g + 256] for a in range(2)]
        return p["src"].rearrange("(k p) n -> p k n", p=P)[:, 2 * kt:2 * kt + 2, COLS * g:COLS * g + COLS]

    n_tiles = sum(p["tiles"] * p["groups"] for p in plan)

    with nc.Block() as block:

        @block.sync
        def _(sp):
            sp.dma_start(x[:, :, :], w["x"][0].rearrange("(h p) n -> p h n", p=P)).then_inc(x_loaded, 16)
            sp.dma_start(mem[:, :, :], w["mem"][0].rearrange("(h p) n -> p h n", p=P)).then_inc(x_loaded, 16)
            sp.dma_start(masks[:, :, :], w["masks"].rearrange("p (m n) -> p m n", n=P)).then_inc(const_loaded, 16)
            n = 0
            for p in plan:
                for g in range(p["groups"]):
                    for kt in range(p["tiles"]):
                        if n >= RAW:
                            sp.wait_ge(w_low_ready, n - RAW + 1)
                        if p["paired"]:
                            for a, src in enumerate(source(p, g, kt)):
                                sp.dma_start(raw[:, n % RAW, :, 256 * a:256 * a + 256], src).then_inc(raw_loaded[n % RAW], 16)
                        else:
                            sp.dma_start(raw[:, n % RAW, :, :], source(p, p.get("order", range(p["groups"]))[g], kt)).then_inc(raw_loaded[n % RAW], 32)
                        n += 1
            sp.wait_ge(result_ready, 1)
            sp.dma_start(out[0].rearrange("(h p) n -> p h n", p=P), xn[:, :, :]).then_inc(stored, 16)
            sp.wait_ge(stored, 16)

        @block.gpsimd
        def _(pool):
            pool.memset(ones[:, :], 1.0).then_inc(mixer_zero, 1)
            pool.memset(neg_half[:, :], -0.5).then_inc(pool_step, 1)
            at = dict(row=0, norm=0, stat=0, step=1)

            def link(ins):
                at["step"] += 1
                ins.then_inc(pool_step, 1)
                pool.wait_ge(pool_step, at["step"])

            def load_row():
                n = at["row"]
                at["row"] += 1
                if n >= len(rows):
                    return
                name, src, wide = rows[n]
                if n >= 2:
                    pool.wait_ge(row_used, n - 1)
                dst, v = (row[:, n % 2, :], src.to_broadcast([P, D])) if wide else (row[0:1, n % 2, :], src)
                pool.dma_start(dst, v).then_inc(row_loaded[n % 2], 16)
                if name == "mix0":
                    pool.memset(zT[:, :, 0:TAPS - 1], 0.0).then_inc(mixer_zero, 1)
                    pool.dma_start(dw_tok[0:TAPS, :], w["conv_dw"][0]).then_inc(mixer_in, 16)
                    pool.dma_start(dw_tok[TAPS:TAPS + 1, :], w["conv_dw_b"]).then_inc(mixer_in, 16)

            def load_mixer(i):
                pool.wait_ge(mixer_free, i)
                if i == 1:
                    pool.dma_start(mix_in[:, :], w["rwkv_mix"][0]).then_inc(mix_loaded, 16)
                    for j, n1 in enumerate(("rwkv_w1", "rwkv_a1", "rwkv_g1")):
                        pool.dma_start(lora1[j][:, :, :], w[n1][0].rearrange("(k p) n -> p k n", p=P)).then_inc(mixer_in, 16)
                    for j, n in enumerate("wa"):
                        pool.dma_start(lora2[j][0:64, :], w[f"rwkv_{n}2"][0]).then_inc(mixer_in, 16)
                        pool.dma_start(lora2[j][64:65, :], w[f"rwkv_{n}0"]).then_inc(mixer_in, 16)
                    pool.dma_start(lora2[2][:, :], w["rwkv_g2"][0, 0:P, :]).then_inc(mixer_in, 16)
                    pool.dma_start(lora2[3][:, :], w["rwkv_g2"][0, P:P + 32, :]).then_inc(mixer_in, 16)
                if i == 2:
                    pool.dma_start(ws_in[:, :, :], w["sgu_ws"][0].rearrange("g t s -> t g s")).then_inc(mixer_in, 16)
                    pool.dma_start(bs_in[:, :], w["sgu_bs"][0]).then_inc(mixer_in, 16)
                if i == 3:
                    pool.dma_start(rotary[:, 0, :, :], w["rotary"][0].rearrange("(h p) n -> p h n", p=P)).then_inc(mixer_in, 16)
                    pool.dma_start(rotary[:, 1, :, :], w["rotary"][1].rearrange("(h p) n -> p h n", p=P)).then_inc(mixer_in, 16)
                    pool.dma_start(decay[:, :, :], w["decay"].rearrange("p (h n) -> p h n", h=XH)).then_inc(mixer_in, 16)

            load_row()
            load_row()
            pool.wait_ge(pool_step, 1)
            roots = {"ln": (mv[:, :, 1], stat[:, :]), "kk": (small[:, 1:3, :], small[:, 2:4, :]),
                     "gn": (small[:, 0, 0:8], small[:, 3, 0:8]), "ret": (small[:, 1, 0:8], small[:, 2, 0:8])}
            for kind, name in small_plan(layers):
                if kind == "drop":
                    load_row()
                elif kind == "rms":
                    at["norm"] += 1
                    pool.wait_ge(squares_summed, 4 * at["norm"])
                    link(pool.tensor_tensor(mean_sq[:, :], sums[:, :, 0], sums[:, :, 1], ALU.add))
                    link(pool.tensor_scalar(mean_sq[:, :], mean_sq[:, :], 1.0 / D, 1e-6, ALU.mult, ALU.add))
                    link(pool.tensor_tensor(rstd[:, :], mean_sq[:, :], neg_half[:, 0:HALVES], ALU.pow))
                    pool.tensor_tensor(rms_col[:, :], mean_sq[:, :], rstd[:, :], ALU.mult).then_inc(rstd_ready, 1)
                    if at["norm"] in (2 + 3 * i for i in range(1, layers)):
                        load_mixer((at["norm"] - 2) // 3)
                else:
                    at["stat"] += 1
                    pool.wait_ge(stat_ready, at["stat"])
                    src, dst = roots[name]
                    for j in (range(HALVES - 1, -1, -1) if len(src.shape) == 3 else range(1)):
                        v, o = (src[:, j, :], dst[:, j, :]) if len(src.shape) == 3 else (src, dst)
                        link(pool.tensor_tensor(o, v, neg_half[:, 0:v.shape[-1]], ALU.pow))
                    pool.sem_inc(root_ready, 1)

        @block.scalar
        def _(act):
            at = dict(prod=0, split=0, col=0, high=0, score=0, sumsq=0, stat=0, exp=0, step=0, vec=0, neg=0, tile=0, lane=0, lane1=0)

            def split_to(n):
                while at["split"] < min(n, n_tiles):
                    t = at["split"]
                    act.wait_ge(raw_loaded[t % RAW], 32 * (t // RAW + 1))
                    if t >= SPLIT:
                        act.wait_ge(tile_used, t - SPLIT + 1)
                    act.activation(w_high[:, t % SPLIT, :, :], raw[:, t % RAW, :, :], ACT.Copy).then_inc(w_high_ready, 1)
                    at["split"] += 1

            def group_done(tiles):
                at["tile"] += tiles
                split_to(at["tile"] + LOOK)
                act.wait_ge(tile_used, at["tile"])

            def columns(high, chunks, c0=0):
                for c in range(0, chunks, 2):
                    act.wait_ge(cols_filled, at["col"] + 1)
                    act.activation(high[:, c0 + c:c0 + c + 2, :], bank(TR + at["col"] % 2), ACT.Copy).then_inc(cols_high, 1)
                    at["col"] += 1

            def skip_columns(banks):
                at["col"] += banks

            def squares(src, g):
                for h in range(HALVES):
                    if at["sumsq"]:
                        act.wait_ge(squares_summed, at["sumsq"])
                    act.activation(scratch[:, :], src[:, h, g * COLS:(g + 1) * COLS], ACT.Square,
                                   accum_out=sums[:, h, g:g + 1]).then_inc(squares_summed, 1)
                    at["sumsq"] += 1

            def scale_ready():
                act.wait_ge(rstd_ready, at["sumsq"] // 4)

            def residual(groups, tiles, deferred=True):
                for g in range(groups):
                    group_done(tiles)
                    at["prod"] += 1
                    if deferred and g == 0:
                        act.wait_ge(group_drained, at["prod"])
                        squares(x, g)
                        split_to(at["tile"] + 2 * LOOK)
                    if deferred:
                        columns(xT_high, KC // 2, g * KC // 2)
                    if not (deferred and g == 0):
                        act.wait_ge(group_drained, at["prod"])
                        squares(x, g)

            def product_groups(groups, tiles, evac=None):
                for g in range(groups):
                    group_done(tiles)
                    if evac:
                        evac(g, at["prod"] % 2)
                    at["prod"] += 1

            def gelu_evac(g, par):
                dst = g_tok if g < 4 else u_tok
                for h in range(HALVES):
                    act.activation(dst[:, h, (g % 4) * COLS:(g % 4 + 1) * COLS], bank(2 * par + h), ACT.Gelu,
                                   scale=rstd[:, h:h + 1]).then_inc(act_out, 1)

            def sigmoid_evac(g, par):
                for h in range(HALVES):
                    if g >= 2:
                        act.wait_ge(group_drained, at["prod"] - 1)
                    act.activation(sig[:, g % 2, h, :], psum[:, 2 * par + h, 256:512], ACT.Sigmoid, scale=rstd[:, h:h + 1]).then_inc(act_out, 1)

            def silu_evac(g, par):
                for h in range(HALVES):
                    if g >= 2:
                        act.wait_ge(group_drained, at["prod"] - 1)
                    act.activation(sgate[:, g % 2, h, :], psum[:, 2 * par + h, 0:256], ACT.Silu, scale=rstd[:, h:h + 1]).then_inc(act_out, 1)

            def conv_mixer():
                skip_columns(1)
                scale_ready()
                group_done(4)
                sigmoid_evac(0, at["prod"] % 2)
                at["prod"] += 1
                split_to(at["tile"] + 2 * LOOK)
                columns(memT_high, KC)
                skip_columns(2)
                for g in range(1, 4):
                    group_done(4)
                    sigmoid_evac(g, at["prod"] % 2)
                    at["prod"] += 1
                split_to(at["tile"] + SPLIT)
                act.wait_ge(cols_drained, 4 + 4 + 2)
                n = 0
                for c in range(CONV_DVE, KC):
                    for t in range(TAPS):
                        if n >= 4:
                            act.wait_ge(tap_used, n - 3)
                        act.activation(tap_diag[:, n % 4, :], ident, ACT.Copy, scale=taps[:, c, t:t + 1]).then_inc(tap_ready, 1)
                        n += 1
                skip_columns(4)
                product_groups(1, 4)
                skip_columns(4)
                product_groups(1, 4)
                at["vec"] += 1
                act.wait_ge(vec_out, at["vec"])
                act.activation(z_tok[:, :, :], z_tok[:, :, :], ACT.Silu).then_inc(act_out, 1)
                columns(xT_high, KC)
                skip_columns(4)
                return 2, 4

            def sgu_mixer():
                skip_columns(1)
                scale_ready()
                for g in range(8):
                    group_done(4)
                    gelu_evac(g, at["prod"] % 2)
                    at["prod"] += 1
                    if g == 0:
                        split_to(at["tile"] + 2 * LOOK)
                        columns(memT_high, KC)
                        skip_columns(3)
                at["score"] += 8
                columns(yT_high, 2 * KC)
                return 2, 8

            def ret_mixer():
                scale_ready()
                product_groups(4, 4)
                for g in range(8):
                    group_done(4)
                    par = at["prod"] % 2
                    dst, fn = (rv, ACT.Copy) if g < 4 else (rg, ACT.Silu)
                    for h in range(HALVES):
                        act.activation(dst[:, h, (g % 4) * COLS:(g % 4 + 1) * COLS], bank(2 * par + h), fn, scale=rstd[:, h:h + 1]).then_inc(act_out, 1)
                    at["prod"] += 1
                skip_columns(8)
                at["score"] += XH
                for n in range(HALVES * XH):
                    act.wait_ge(scores_filled, at["score"] + 1)
                    if n:
                        act.wait_ge(square_summed, n)
                    act.activation(rtmp[:, 0:2, :, :].rearrange("p a n e -> p (a n e)"), bank(6 + at["score"] % 2), ACT.Square,
                                   accum_out=small[:, 0, n:n + 1]).then_inc(square_summed, 1)
                    at["score"] += 1
                columns(yT_high, 2 * KC)
                return 2, 8

            def lane_take():
                n = at["lane"]
                act.wait_ge(lane_filled[0], n + 1)
                at["lane"] += 1
                return n % 4

            def lane_copy(dst, view, fn=ACT.Copy):
                b = lane_take()
                act.activation(dst, view(psum[:, b, :]), fn).then_inc(lane_used[0], 1)

            def rwkv_mixer():
                skip_columns(4 + 1)
                for j, fn in enumerate((ACT.Tanh, ACT.Copy, ACT.Sigmoid)):
                    lane_copy(lora[j][0:(P if j == 2 else 64), :], lambda v: v[0:(P if j == 2 else 64), 0:T], fn)
                    if j == 2:
                        lane_copy(lora[0][0:32, :], lambda v: v[0:32, 0:T], fn)
                    for h in range(HALVES):
                        for n in range(2):
                            dst = (lw, ra, rgate)[j][:, h, COLS * n:COLS * n + COLS]
                            lane_copy(dst, lambda v: v, ACT.Copy if j == 2 else ACT.Sigmoid)
                def mixed_high(m):
                    at["vec"] += 1
                    act.wait_ge(vec_out, at["vec"])
                    for c in range(4):
                        if m:
                            act.wait_ge(tile_used, at["tile"] + c + 1)
                        act.activation(xT_high[:, 2 * c:2 * c + 2, :], (xs_b, xs, xs_b)[m][:, 2 * c:2 * c + 2, :], ACT.Copy).then_inc(act_out, 1)
                        if m:
                            split_to(at["tile"] + LOOK + c + 1)

                mixed_high(0)
                for m in range(2):
                    product_groups(1, 4)
                    mixed_high(m + 1)
                    product_groups(1, 4)
                split_to(at["tile"] + SPLIT)
                product_groups(2, 4)
                for h in range(HALVES):
                    for n in range(2):
                        act.wait_ge(lane_filled[1], at["lane1"] + 1)
                        b = 4 + at["lane1"] % 4
                        at["lane1"] += 1
                        at["vec"] += 1
                        act.wait_ge(vec_out, at["vec"])
                        act.activation(exps[0][:, :], bank(b), ACT.Exp).then_inc(act_out, 1)
                        act.activation(exps[1][:, :], bank(b), ACT.Exp, scale=-1.0).then_inc(act_out, 1)
                        act.wait_ge(lane_used[1], at["lane1"])
                        act.activation(exps[2][:, :], exps[2][:, :], ACT.Exp).then_inc(act_out, 1)
                lane_copy(pc[:, :, :, :], lambda v: v[:, 0:32].rearrange("p (h n c) -> p h n c", h=HALVES, c=2), ACT.Exp)
                pairs = lambda v: v.rearrange("p (h t) -> p h t", h=4)
                heads8 = lambda v: v.rearrange("p (h t) -> p h t", h=8)
                for h in range(HALVES):
                    for hg in range(2):
                        unit = 2 * h + hg
                        if unit == 0:
                            for dst in fronts[0]:
                                lane_copy(dst[:, :, :], pairs)
                        for level in range(1, LEVELS):
                            if level == 4:
                                lane_copy(hh[:, :, :], heads8)
                            for sb in range(2):
                                lane_copy(invT[:, sb:8:2, :], pairs)
                        lane_copy(wT[:, :, :], pairs)
                        if unit < 3:
                            for dst in fronts[(unit + 1) % 2]:
                                lane_copy(dst[:, :, :], pairs)
                        lane_copy(zz[:, :, :], heads8)
                        lane_copy(rr[:, h, 512 * hg:512 * hg + 512], lambda v: v)
                columns(xT_high, KC)
                return 2, 4

            act.wait_ge(x_loaded, 32)
            squares(mem, 0)
            squares(mem, 1)
            split_to(1)
            columns(xT_high, KC)
            split_to(LOOK)
            act.wait_ge(mem_scaled, 1)
            squares(x, 0)
            squares(x, 1)
            for i in range(layers):
                groups, tiles = [conv_mixer, rwkv_mixer, sgu_mixer, ret_mixer][i]()
                if i in (1, 3):
                    columns(memT_high, KC)
                residual(groups, tiles)
                if i:
                    product_groups(2, 4)
                    skip_columns(4)
                product_groups(2, 4)
                skip_columns(4)
                product_groups(1, 4)
                for h in range(HALVES):
                    for hp in range(XH // 2):
                        at["neg"] += 1
                        act.wait_ge(neg_max, at["neg"])
                        for e in range(2):
                            hd = 2 * hp + e
                            j = h * XH + hd
                            act.activation(prob[:, h, hd, :], psum[:, 6 + at["score"] % 2, e * T:(e + 1) * T], ACT.Exp,
                                           bias=den[:, 0, j:j + 1], scale=float(HW) ** -0.5,
                                           accum_out=den[:, 1, j:j + 1]).then_inc(exp_done, 1)
                        at["score"] += 1
                product_groups(1, 4)
                skip_columns(4)
                for c in range(XH):
                    act.wait_ge(scores_filled, at["score"] + 1)
                    act.activation(xT_high[:, 2 * c:2 * c + 2, :], bank(6 + at["score"] % 2), ACT.Copy).then_inc(cols_high, 1)
                    at["score"] += 1
                residual(2, 4)
                scale_ready()
                for g in range(11):
                    group_done(4)
                    silu_evac(g, at["prod"] % 2)
                    at["prod"] += 1
                    if g:
                        columns(hT_high, 2, 2 * (g - 1))
                columns(hT_high, 2, 20)
                residual(2, 11, i + 1 < layers and i != 0)

        @block.vector
        def _(dve):
            at = dict(prod=0, split=0, col=0, high=0, score=0, sumsq=0, stat=0, exp=0, step=0, act=0, tile=0, lane=0)

            def link(ins):
                at["step"] += 1
                ins.then_inc(vec_step, 1)
                dve.wait_ge(vec_step, at["step"])

            def split_to(n):
                while at["split"] < min(n, n_tiles):
                    t = at["split"]
                    dve.wait_ge(w_high_ready, t + 1)
                    dve.tensor_tensor(w_low[:, t % SPLIT, :, :], raw[:, t % RAW, :, :],
                                      w_high[:, t % SPLIT, :, :].bitcast(f32), ALU.subtract).then_inc(w_low_ready, 1)
                    at["split"] += 1

            def group_done(tiles):
                at["tile"] += tiles
                split_to(at["tile"] + LOOK)
                dve.wait_ge(tile_used, at["tile"])

            def columns(high, low, chunks, c0=0):
                for c in range(0, chunks, 2):
                    at["high"] += 1
                    dve.wait_ge(cols_high, at["high"])
                    dve.tensor_tensor(low[:, c0 + c:c0 + c + 2, :], psum[:, TR + at["col"] % 2, :].rearrange("p (c t) -> p c t", c=2),
                                      high[:, c0 + c:c0 + c + 2, :].bitcast(f32), ALU.subtract).then_inc(cols_drained, 1)
                    at["col"] += 1

            def plain_columns(dst_of, banks):
                for b in range(banks):
                    dve.wait_ge(cols_filled, at["col"] + 1)
                    dst, src = dst_of(b, TR + at["col"] % 2)
                    dve.tensor_copy(dst, src).then_inc(cols_drained, 1)
                    at["col"] += 1

            def pair_of(dst):
                return lambda b, bk: (dst[:, 2 * b:2 * b + 2, :], psum[:, bk, :].rearrange("p (c t) -> p c t", c=2))

            def use_row(name):
                n = row_at[name]
                dve.wait_ge(row_loaded[n % 2], 16 * (n // 2 + 1))
                return row[:, n % 2, :]

            def drop_row(ins):
                ins.then_inc(row_used, 1)

            def scale_ready():
                at["norm"] = at.get("norm", 0) + 1
                dve.wait_ge(rstd_ready, at["norm"])

            def tok_done(ins):
                at["tok"] = at.get("tok", 0) + 1
                ins.then_inc(tok_ready, 1)

            def tok_signal():
                at["tok"] = at.get("tok", 0) + 1
                dve.sem_inc(tok_ready, 1)

            def gain(dst, src, name, g0, g1):
                r = use_row(name)
                c = slice(g0 * COLS, g1 * COLS)
                for h in range(HALVES):
                    tok_done(dve.tensor_tensor(dst[:, h, c], src[:, h, c], r[:, c], ALU.mult))
                if g1 == 2:
                    dve.wait_ge(tok_ready, at["tok"])
                    dve.sem_inc(row_used, 1)

            def normed(name):
                scale_ready()
                r = use_row(name)
                for h in range(HALVES):
                    tok_done(dve.scalar_tensor_tensor(xn[:, h, :], x[:, h, :], rstd[:, h:h + 1], r, ALU.mult, ALU.mult))
                dve.wait_ge(tok_ready, at["tok"])
                dve.sem_inc(row_used, 1)

            def rms_rows():
                dve.wait_ge(cols_filled, at["col"] + 1)
                dve.tensor_copy(rms_row[:, :], psum[0:1, TR + at["col"] % 2, 0:T]).then_inc(cols_drained, 1)
                at["col"] += 1

            def drained(ins):
                ins.then_inc(group_drained, 1)
                at["prod"] += 1

            def residual(groups, tiles, buf, name=None, bias_row=False):
                for g in range(groups):
                    group_done(tiles)
                    par = at["prod"] % 2
                    for h in range(HALVES):
                        cols = x[:, h, g * COLS:(g + 1) * COLS]
                        ins = dve.tensor_tensor(cols, cols, bank(2 * par + h), ALU.add)
                        drained(ins) if h else link(ins)
                    dve.wait_ge(group_drained, at["prod"])
                    if bias_row and g:
                        dve.sem_inc(row_used, 1)
                    if name:
                        gain(buf, x, name, g, g + 1)
                        if g == 0:
                            split_to(at["tile"] + 2 * LOOK)
                        columns(xT_high, xT_low, KC // 2, g * KC // 2)

            def scaled(dst, groups, tiles):
                for g in range(groups):
                    group_done(tiles)
                    par = at["prod"] % 2
                    for h in range(HALVES):
                        ins = dve.tensor_scalar(dst[:, h, g * COLS:(g + 1) * COLS], bank(2 * par + h), rstd[:, h:h + 1], None, ALU.mult)
                        drained(ins) if h else link(ins)

            def copies(dst, groups, tiles, g0=0):
                for g in range(groups):
                    group_done(tiles)
                    par = at["prod"] % 2
                    for h in range(HALVES):
                        ins = dve.tensor_copy(dst[:, h, (g + g0) * COLS:(g + g0 + 1) * COLS], bank(2 * par + h))
                        drained(ins) if h else link(ins)

            def gated(g, mul_cols, gate_of, dst_of):
                par = at["prod"] % 2
                for h in range(HALVES):
                    at["act"] += 1
                    dve.wait_ge(act_out, at["act"])
                    ins = dve.scalar_tensor_tensor(dst_of(h), psum[:, 2 * par + h, mul_cols:mul_cols + 256], rstd[:, h:h + 1],
                                                   gate_of(h), ALU.mult, ALU.mult)
                    drained(ins) if h else link(ins)
                dve.wait_ge(group_drained, at["prod"])

            def layer_norm(buf, width, gains, biases):
                for h in range(HALVES):
                    for s in range(width // 512):
                        link(dve.bn_stats(bn[:, h, s, :], buf[:, h, 512 * s:512 * s + 512]))
                    link(dve.bn_aggr(mv[:, h, :], bn[:, h, 0:width // 512, :].rearrange("p s c -> p (s c)")))
                dve.tensor_scalar(mv[:, :, 1], mv[:, :, 1], 1e-5, None, ALU.add).then_inc(stat_ready, 1)
                at["stat"] += 1
                dve.wait_ge(root_ready, at["stat"])
                for h in range(HALVES):
                    link(dve.tensor_scalar(buf[:, h, :], buf[:, h, :], mv[:, h, 0:1], stat[:, h:h + 1], ALU.subtract, ALU.mult))
                for names, op in ((gains, ALU.mult), (biases, ALU.add)):
                    for j, name in enumerate(names):
                        r = use_row(name)
                        for h in range(HALVES):
                            v = buf[:, h, j * D:(j + 1) * D]
                            link(dve.tensor_tensor(v, v, r, op))
                        dve.sem_inc(row_used, 1)

            def key_group(g):
                par = at["prod"] % 2
                for h in range(HALVES):
                    ins = dve.tensor_copy(k_tok[:, g, h, :], bank(2 * par + h))
                    drained(ins) if h else link(ins)

            def conv_mixer():
                gain(xn, mem, "mem0", 0, 2)
                scale_ready()
                rms_rows()
                group_done(4)
                gated(0, 0, lambda h: sig[:, 0, h, :], lambda h: z_tok[:, h, 0:256])
                split_to(at["tile"] + 2 * LOOK)
                columns(memT_high, memT_low, KC)
                plain_columns(lambda b, bk: (taps[:, 4 * b:4 * b + 4, :], psum[:, bk, 0:128].rearrange("p (c t) -> p c t", c=4)), 2)
                for g in range(1, 4):
                    group_done(4)
                    gated(g, 0, lambda h: sig[:, g % 2, h, :], lambda h: z_tok[:, h, 256 * g:256 * g + 256])
                dve.sem_inc(row_used, 2)
                tok_signal()
                plain_columns(lambda b, bk: (zT[:, 2 * b:2 * b + 2, TAPS - 1:TAPS - 1 + T],
                                             psum[:, bk, :].rearrange("p (c t) -> p c t", c=2)), 4)
                dve.wait_ge(cols_drained, at["col"])
                dve.wait_ge(mixer_zero, 2)
                split_to(at["tile"] + SPLIT)
                base = at["step"]
                for t in range(TAPS):
                    for c in range(CONV_DVE):
                        src = zT[:, c, t:t + T]
                        if t:
                            dve.wait_ge(vec_step, base + CONV_DVE * (t - 1) + c + 1)
                            ins = dve.scalar_tensor_tensor(conv[:, c, :], src, taps[:, c, t:t + 1], conv[:, c, :], ALU.mult, ALU.add)
                        else:
                            ins = dve.tensor_scalar(conv[:, c, :], src, taps[:, c, 0:1], taps[:, c, TAPS:TAPS + 1], ALU.mult, ALU.add)
                        ins.then_inc(vec_step, 1)
                        at["step"] += 1
                dve.wait_ge(conv_filled, 1)
                for c in range(CONV_DVE, KC):
                    j = c - CONV_DVE
                    link(dve.tensor_scalar(conv[:, c, :], psum[:, 6 + j // 2, T * (j % 2):T * (j % 2) + T], taps[:, c, TAPS:TAPS + 1], None, ALU.add))
                tok_signal()
                group_done(4)
                key_group(0)
                plain_columns(lambda b, bk: (z_tok[:, b // 2, (b % 2) * 512:(b % 2) * 512 + 512], psum[:, bk, :]), 4)
                dve.wait_ge(cols_drained, at["col"])
                layer_norm(z_tok, D, ["conv_g"], ["conv_b"])
                dve.sem_inc(vec_out, 1)
                at["act"] += 1
                group_done(4)
                key_group(1)
                columns(xT_high, xT_low, KC)
                plain_columns(pair_of(kT), 4)
                return 2, 4

            def sgu_mixer():
                def group_evacuated(g):
                    group_done(4)
                    at["act"] += HALVES
                    dve.wait_ge(act_out, at["act"])
                    dve.sem_inc(group_drained, 1)
                    at["prod"] += 1
                    if g % 2:
                        dve.sem_inc(row_used, 1)
                    if g < 4:
                        for h in range(HALVES):
                            link(dve.bn_stats(bn[:, h, g, :], g_tok[:, h, COLS * g:COLS * g + COLS]))

                def affine(name, j, op):
                    r = use_row(name)
                    for h in range(HALVES):
                        v = g_tok[:, h, j * D:(j + 1) * D]
                        link(dve.tensor_tensor(v, v, r, op))

                scale_ready()
                rms_rows()
                group_evacuated(0)
                gain(xn, mem, "mem2", 0, 2)
                split_to(at["tile"] + 2 * LOOK)
                columns(memT_high, memT_low, KC)
                plain_columns(lambda b, bk: (wsT[:, 4 * b:4 * b + 4, :], psum[:, bk, :].rearrange("p (c t) -> p c t", c=4)) if b < 2
                              else (bsT[:, :], psum[:, bk, 0:8]), 3)
                dve.wait_ge(cols_drained, at["col"])
                for g in range(8):
                    link(dve.tensor_tensor(wsT[:, g, :], wsT[:, g, :], masks[:, M_TRI_ALL, :], ALU.mult))
                for g in range(1, 4):
                    group_evacuated(g)
                for h in range(HALVES):
                    link(dve.bn_aggr(mv[:, h, :], bn[:, h, :, :].rearrange("p s c -> p (s c)")))
                dve.tensor_scalar(mv[:, :, 1], mv[:, :, 1], 1e-5, None, ALU.add).then_inc(stat_ready, 1)
                at["stat"] += 1
                dve.wait_ge(root_ready, at["stat"])
                for h in range(HALVES):
                    link(dve.tensor_scalar(g_tok[:, h, :], g_tok[:, h, :], mv[:, h, 0:1], stat[:, h:h + 1], ALU.subtract, ALU.mult))
                group_evacuated(4)
                affine("sgu_g0", 0, ALU.mult)
                group_evacuated(5)
                dve.sem_inc(row_used, 1)
                affine("sgu_b0", 0, ALU.add)
                group_evacuated(6)
                group_evacuated(7)
                dve.sem_inc(row_used, 1)
                for name, op in (("sgu_g1", ALU.mult), ("sgu_b1", ALU.add)):
                    affine(name, 1, op)
                    dve.sem_inc(row_used, 1)
                tok_signal()
                for h in range(HALVES):
                    for gp in range(4):
                        dve.wait_ge(scores_filled, at["score"] + 1)
                        for e in range(2):
                            g = 2 * gp + e
                            u = u_tok[:, h, 256 * g:256 * g + 256]
                            ins = dve.scalar_tensor_tensor(u, psum[:, 6 + at["score"] % 2, 256 * e:256 * e + 256], bsT[:, g:g + 1], u,
                                                           ALU.add, ALU.mult)
                            ins.then_inc(scores_used, 1) if e else link(ins)
                        at["score"] += 1
                columns(yT_high, sgu_low, 2 * KC)
                return 2, 8

            def ret_mixer():
                scale_ready()
                for j in range(2):
                    scaled(qk[j], 2, 4)
                dve.wait_ge(group_drained, at["prod"])
                for g in range(8):
                    group_done(4)
                    at["act"] += HALVES
                    dve.wait_ge(act_out, at["act"])
                    dve.sem_inc(group_drained, 1)
                    at["prod"] += 1
                    if g == 0:
                        dve.wait_ge(mixer_in, 16 * MIXER_LOADS[3])
                    if g < 4:
                        v = qk[g // 2][:, g % 2, :].rearrange("p (a n e) -> p a n e", a=XH, e=2)
                        cos = rotary[:, 0, g % 2, :].unsqueeze(1).to_broadcast([P, XH, HW])
                        sin = rotary[:, 1, g % 2, :].rearrange("p (n e) -> p n e", e=2)
                        for e in range(2):
                            link(dve.tensor_tensor(rtmp[:, :, :, e], v[:, :, :, 1 - e],
                                                   sin[:, :, e].unsqueeze(1).to_broadcast([P, XH, HW // 2]), ALU.mult))
                        flat = qk[g // 2][:, g % 2, :].rearrange("p (a n) -> p a n", a=XH)
                        link(dve.tensor_tensor(flat, flat, cos, ALU.mult))
                        link(dve.tensor_tensor(flat, flat, rtmp[:, :, :, :].rearrange("p a n e -> p a (n e)"), ALU.add))
                tok_signal()
                for j in range(2):
                    plain_columns(pair_of(qkT[j]), 4)
                for hd in range(XH):
                    dve.wait_ge(scores_filled, at["score"] + 1)
                    dve.tensor_tensor(sc[:, hd, :], psum[:, 6 + at["score"] % 2, 0:3 * P], decay[:, hd, :], ALU.mult).then_inc(scores_used, 1)
                    at["score"] += 1
                for h in range(HALVES):
                    for hd in range(XH):
                        dve.wait_ge(square_summed, XH * h + hd + 1)
                        dve.tensor_tensor(o_tok[:, h, 512 * hd:512 * hd + 512], bank(6 + at["score"] % 2),
                                          rg[:, h, 512 * hd:512 * hd + 512], ALU.mult).then_inc(scores_used, 1)
                        at["score"] += 1
                dve.wait_ge(scores_used, at["score"])
                dve.tensor_scalar(small[:, 1, 0:8], small[:, 0, 0:8], 1.0 / 512, 1e-6, ALU.mult, ALU.add).then_inc(stat_ready, 1)
                at["stat"] += 1
                dve.wait_ge(root_ready, at["stat"])
                for n in range(HALVES * XH):
                    v = o_tok[:, n // XH, 512 * (n % XH):512 * (n % XH) + 512]
                    link(dve.tensor_scalar(v, v, small[:, 2, n:n + 1], None, ALU.mult))
                tok_signal()
                columns(yT_high, ret_low, 2 * KC)
                return 2, 8

            def lane_take():
                n = at["lane"]
                dve.wait_ge(lane_filled[1], n + 1)
                at["lane"] += 1
                return 4 + n % 4

            def over_heads(m):
                return masks[:, m, :].unsqueeze(1).to_broadcast([P, 4, P])

            def per_head(v):
                return v.unsqueeze(2).to_broadcast([P, NH, HD])

            def by_head(v):
                return v.rearrange("p (h n) -> p h n", h=NH)

            def mixed(m, dst):
                for c in range(KC):
                    last = dve.scalar_tensor_tensor(dst[:, c, :], diff[:, c, :], mix_cols[:, c, m:m + 1], hT[:, c, 1:T + 1], ALU.mult, ALU.add)
                link(last)

            def rwkv_mixer():
                link(dve.memset(hT[:, :, 0:1], 0.0))
                plain_columns(lambda b, bk: (hT[:, 2 * b:2 * b + 2, 1:T + 1], psum[:, bk, :].rearrange("p (c t) -> p c t", c=2)), 4)
                plain_columns(lambda b, bk: (mix_cols[:, :, :], psum[:, bk, 0:48].rearrange("p (c t) -> p c t", c=KC)), 1)
                dve.wait_ge(cols_drained, at["col"])
                link(dve.tensor_tensor(diff[:, :, :], hT[:, :, 0:T], hT[:, :, 1:T + 1], ALU.subtract))
                for j in range(2):
                    link(dve.memset(lora[j][64:65, :], 1.0))
                for j, m in enumerate((1, 4, 5)):
                    if j == 2:
                        dve.wait_ge(lane_used[0], 1)
                    mixed(m, (xs, xs_b, xs)[j])
                    tok_signal()
                for m, (src, buf, free) in enumerate(((2, xs_b, 6), (0, xs, 12))):
                    dve.wait_ge(lane_used[0], free)
                    mixed(src, buf)
                    dve.sem_inc(vec_out, 1)

                def mixed_low(m):
                    for c in range(4):
                        cs = slice(2 * c, 2 * c + 2)
                        at["act"] += 1
                        dve.wait_ge(act_out, at["act"])
                        tok_done(dve.tensor_tensor(xT_low[:, cs, :], (xs_b, xs, xs_b)[m][:, cs, :], xT_high[:, cs, :].bitcast(f32), ALU.subtract))
                        if m:
                            split_to(at["tile"] + LOOK + c + 1)
                    dve.wait_ge(tok_ready, at["tok"])

                mixed_low(0)
                mixed(3, xs_b)
                dve.sem_inc(vec_out, 1)
                for h in range(HALVES):
                    link(dve.tensor_scalar(lw[:, h, :], lw[:, h, :], -float(np.exp(-0.5)), None, ALU.mult))
                tok_signal()
                copies(rk, 1, 4)
                mixed_low(1)
                copies(rk, 1, 4, 1)
                dve.wait_ge(group_drained, at["prod"])
                r = use_row("k_k")
                for h in range(HALVES):
                    link(dve.tensor_tensor(kk[:, h, :], rk[:, h, :], r, ALU.mult))
                    link(dve.tensor_tensor(tmp[h][:, :], kk[:, h, :], kk[:, h, :], ALU.mult))
                    link(dve.tensor_reduce(small[:, 1 + h, :], by_head(tmp[h][:, :]), AX.X, ALU.add))
                dve.tensor_scalar(small[:, 1:3, :], small[:, 1:3, :], 1e-24, None, ALU.max).then_inc(stat_ready, 1)
                copies(rr, 1, 4)
                mixed_low(2)
                copies(rr, 1, 4, 1)
                split_to(at["tile"] + SPLIT)
                at["stat"] += 1
                dve.wait_ge(root_ready, at["stat"])
                for h in range(HALVES):
                    link(dve.tensor_tensor(by_head(kk[:, h, :]), by_head(kk[:, h, :]), per_head(small[:, 2 + h, :]), ALU.mult))
                dve.sem_inc(row_used, 1)
                r = use_row("k_a")
                for h in range(HALVES):
                    link(dve.scalar_tensor_tensor(tmp[0][:, :], ra[:, h, :], -1.0, r, ALU.add, ALU.mult))
                    link(dve.scalar_tensor_tensor(rk[:, h, :], tmp[0][:, :], 1.0, rk[:, h, :], ALU.add, ALU.mult))
                dve.sem_inc(row_used, 1)
                dve.wait_ge(group_drained, at["prod"])
                r = use_row("r_k")
                for h in range(HALVES):
                    link(dve.tensor_tensor(tmp[0][:, :], rr[:, h, :], rk[:, h, :], ALU.mult))
                    link(dve.tensor_tensor(tmp[0][:, :], tmp[0][:, :], r, ALU.mult))
                    link(dve.tensor_reduce(small[:, 4 + h, :], by_head(tmp[0][:, :]), AX.X, ALU.add))
                    link(dve.tensor_tensor(ra[:, h, :], ra[:, h, :], kk[:, h, :], ALU.mult))
                dve.sem_inc(row_used, 1)
                dve.sem_inc(vec_out, 1)
                copies(rvv, 2, 4)
                for h in range(HALVES):
                    for n in range(2):
                        b = lane_take()
                        cols = slice(COLS * n, COLS * n + COLS)
                        at["act"] += 2
                        dve.wait_ge(act_out, at["act"])
                        dve.tensor_tensor(exps[2][:, :], bank(b), lw[:, h, cols], ALU.subtract).then_inc(lane_used[1], 1)
                        link(dve.tensor_tensor(rr[:, h, cols], rr[:, h, cols], exps[0][:, :], ALU.mult))
                        link(dve.tensor_tensor(rk[:, h, cols], rk[:, h, cols], exps[1][:, :], ALU.mult))
                        link(dve.tensor_tensor(ra[:, h, cols], ra[:, h, cols], exps[1][:, :], ALU.mult))
                        at["act"] += 1
                        dve.wait_ge(act_out, at["act"])
                        link(dve.scalar_tensor_tensor(kk[:, h, cols], kk[:, h, cols], -1.0, exps[2][:, :], ALU.mult, ALU.mult))
                        if 2 * h + n < 3:
                            dve.sem_inc(vec_out, 1)
                dve.wait_ge(lane_used[0], 17)
                link(dve.memset(state[:, :, :], 0.0))
                tok_signal()
                heads = lambda b: psum[:, b, :].rearrange("p (h t) -> p h t", h=4)
                chunks = lambda b: psum[:, b, 0:4 * HD].rearrange("p (h t) -> p h t", h=4)

                def masked(dst, sb, m):
                    b = lane_take()
                    dve.tensor_tensor(dst[:, sb:8:2, :], heads(b), over_heads(m), ALU.mult).then_inc(lane_used[1], 1)

                def ab_masked():
                    for sb in range(2):
                        masked(abT, sb, M_STRICT)
                        masked(inv, sb, M_LEVEL)

                def start_inverse():
                    dve.wait_ge(lane_used[1], at["ab"])
                    for sb in range(2):
                        hs = slice(sb, 8, 2)
                        link(dve.tensor_tensor(inv[:, hs, :], inv[:, hs, :], over_heads(M_IDENT), ALU.add))
                        link(dve.tensor_tensor(invT[:, hs, :], abT[:, hs, :], over_heads(M_PAIR_T), ALU.mult))
                        link(dve.tensor_tensor(invT[:, hs, :], invT[:, hs, :], over_heads(M_IDENT), ALU.add))
                        tok_signal()

                def group_norm(unit, step):
                    h, c0 = unit // 2, 512 * (unit % 2)
                    cs = slice(c0, c0 + 512)
                    n8 = slice(c0 // HD, c0 // HD + 8)
                    eight = lambda v: v.rearrange("p (h n) -> p h n", h=8)
                    per8 = lambda v: v.unsqueeze(2).to_broadcast([P, 8, HD])
                    y, t = rr[:, h, cs], scratch[:, :]
                    if step == 0:
                        dve.wait_ge(lane_used[0], 17 + 4 + UNIT_BANKS * (unit + 1) - (4 if unit == 3 else 0))
                        link(dve.tensor_reduce(small[:, 2, 0:8], eight(y), AX.X, ALU.add))
                        link(dve.tensor_scalar(small[:, 2, 0:8], small[:, 2, 0:8], 1.0 / HD, None, ALU.mult))
                        link(dve.tensor_tensor(eight(y), eight(y), per8(small[:, 2, 0:8]), ALU.subtract))
                    if step == 1:
                        link(dve.tensor_tensor(t, y, y, ALU.mult))
                        link(dve.tensor_reduce(small[:, 0, 0:8], eight(t), AX.X, ALU.add))
                        dve.tensor_scalar(small[:, 0, 0:8], small[:, 0, 0:8], 1.0 / HD, HD * 1e-5, ALU.mult, ALU.add).then_inc(stat_ready, 1)
                        at["stat"] += 1
                        link(dve.tensor_tensor(eight(t), eight(rvv[:, h, cs]), per8(small[:, 4 + h, n8]), ALU.mult))
                    if step == 2:
                        dve.wait_ge(root_ready, at["stat"])
                        link(dve.tensor_tensor(eight(y), eight(y), per8(small[:, 3, 0:8]), ALU.mult))
                        link(dve.tensor_tensor(y, y, use_row("gn_g")[:, cs], ALU.mult))
                        if unit == 3:
                            dve.sem_inc(row_used, 1)
                    if step == 3:
                        link(dve.tensor_tensor(y, y, use_row("gn_b")[:, cs], ALU.add))
                        link(dve.tensor_tensor(y, y, t, ALU.add))
                    if step == 4:
                        link(dve.tensor_tensor(y, y, rgate[:, h, cs], ALU.mult))

                ab_masked()
                at["ab"] = at["lane"]
                start_inverse()
                for h in range(HALVES):
                    for hg in range(2):
                        unit = 2 * h + hg
                        for level in range(1, LEVELS):
                            for sb in range(2):
                                masked(lvl, sb, M_LEVEL + level)
                            if level < 3:
                                for sb in range(2):
                                    masked((akT, rbT)[level - 1], sb, (M_STRICT, M_INCL)[level - 1])
                            for sb in range(2):
                                b = lane_take()
                                d = inv[:, sb:8:2, :]
                                dve.tensor_tensor(d, heads(b), d, ALU.add).then_inc(lane_used[1], 1)
                            if unit:
                                group_norm(unit - 1, level - 1)
                        for sb in range(2):
                            masked(rkT, sb, M_INCL)
                        z_at = 17 + 4 + UNIT_BANKS * (unit + 1) - 1 - (4 if unit == 3 else 0)
                        dve.wait_ge(lane_used[0], z_at)
                        for c in range(2):
                            rs = slice(CH * c, CH * c + CH)
                            for sb in range(2):
                                b = lane_take()
                                dve.tensor_tensor(uu[rs, sb:8:2, :], chunks(b)[rs, :, :], zz[rs, sb:8:2, :], ALU.add).then_inc(lane_used[1], 1)
                            if c and unit < 3:
                                start_inverse()
                            b = lane_take()
                            st = state[:, 4 * hg:4 * hg + 4, :]
                            link(dve.tensor_tensor(st, chunks(b), st, ALU.add))
                            dve.tensor_tensor(st, st, pc[:, h, 4 * hg:4 * hg + 4, c:c + 1].to_broadcast([P, 4, HD]), ALU.mult).then_inc(lane_used[1], 1)
                            if c == 0 and unit < 3:
                                ab_masked()
                                at["ab"] = at["lane"]
                tok_signal()
                group_norm(3, 0)
                group_norm(3, 1)
                columns(xT_high, xT_low, KC // 2)
                for step in range(2, 5):
                    group_norm(3, step)
                dve.sem_inc(row_used, 1)
                tok_signal()
                columns(xT_high, xT_low, KC // 2, KC // 2)
                return 2, 4

            dve.wait_ge(x_loaded, 32)
            gain(xg, x, "mix0", 0, 2)
            split_to(1)
            columns(xT_high, xT_low, KC)
            split_to(LOOK)
            scale_ready()
            for h in range(HALVES):
                link(dve.tensor_scalar(mem[:, h, :], mem[:, h, :], rstd[:, h:h + 1], None, ALU.mult))
            dve.sem_inc(mem_scaled, 1)
            for i in range(layers):
                if i == 1:
                    normed("mix1")
                groups, tiles = [conv_mixer, rwkv_mixer, sgu_mixer, ret_mixer][i]()
                if i in (1, 3):
                    gain(xn, mem, f"mem{i}", 0, 2)
                    columns(memT_high, memT_low, KC)
                if i == 0:
                    use_row("conv_bo")
                residual(groups, tiles, xn, f"xattn{i}", i == 0)
                if i:
                    for g in range(2):
                        group_done(4)
                        key_group(g)
                    plain_columns(pair_of(kT), 4)
                scale_ready()
                scaled(q_tok, 2, 4)
                plain_columns(pair_of(qT), 4)
                copies(v_tok, 1, 4)
                for h in range(HALVES):
                    for hp in range(XH // 2):
                        dve.wait_ge(scores_filled, at["score"] + 1)
                        j = h * XH + 2 * hp
                        link(dve.tensor_reduce(den[:, 2, j:j + 2], psum[:, 6 + at["score"] % 2, :].rearrange("p (e t) -> p e t", e=2), AX.X, ALU.max))
                        dve.tensor_scalar(den[:, 0, j:j + 2], den[:, 2, j:j + 2], -float(HW) ** -0.5, None, ALU.mult).then_inc(neg_max, 1)
                        at["score"] += 1
                        at["exp"] += 2
                        dve.wait_ge(exp_done, at["exp"])
                        dve.sem_inc(scores_used, 1)
                        link(dve.reciprocal(den[:, 2, j:j + 2], den[:, 1, j:j + 2]))
                        for e in range(2):
                            v = prob[:, h, 2 * hp + e, :]
                            tok_done(dve.tensor_scalar(v, v, den[:, 2, j + e:j + e + 1], None, ALU.mult))
                copies(v_tok, 1, 4, 1)
                plain_columns(lambda b, bk: (probT[:, b, :, :], psum[:, bk, :].rearrange("p (c t) -> p c t", c=2)), 4)
                for c in range(XH):
                    at["high"] += 1
                    dve.wait_ge(cols_high, at["high"])
                    dve.tensor_tensor(xT_low[:, 2 * c:2 * c + 2, :], psum[:, 6 + at["score"] % 2, :].rearrange("p (c t) -> p c t", c=2),
                                      xT_high[:, 2 * c:2 * c + 2, :].bitcast(f32), ALU.subtract).then_inc(scores_used, 1)
                    at["score"] += 1
                residual(2, 4, xg, f"ffn{i}")
                scale_ready()
                for g in range(11):
                    group_done(4)
                    gated(g, 256, lambda h: sgate[:, g % 2, h, :], lambda h: htok[:, g % 2, h, :])
                    if g:
                        columns(hT_high, hT_low, 2, 2 * (g - 1))
                columns(hT_high, hT_low, 2, 20)
                defer = i + 1 < layers and i != 0
                residual(2, 11, xg, f"mix{i + 1}" if defer else None)
                dve.sem_inc(mixer_free, 1)
            normed("final")
            dve.sem_inc(result_ready, 1)

        @block.tensor
        def _(pe):
            at = dict(plan=0, prod=0, tile=0, col=0, score=0, tok=0)

            def product(name, high, low, groups, bias=None, ready=None, after=None, tok=None):
                p = plan[at["plan"]]
                if groups[-1] == p["groups"] - 1:
                    at["plan"] += 1
                assert p["name"] == name, (p["name"], name)
                for g in groups:
                    par = at["prod"] % 2
                    if at["prod"] >= 2:
                        pe.wait_ge(group_drained, at["prod"] - 1)
                    for kt in range(p["tiles"]):
                        t = at["tile"]
                        if g == groups[0] and ready:
                            pe.wait_ge(cols_drained, ready[kt])
                        if g == groups[0] and tok:
                            pe.wait_ge(tok_ready, tok[kt])
                        pe.wait_ge(w_low_ready, t + 1)
                        for k in range(2):
                            for h in range(HALVES):
                                c = 2 * kt + k
                                last = c == 2 * p["tiles"] - 1
                                xh, xl = high[:, c, h * P:(h + 1) * P], low[:, c, h * P:(h + 1) * P]
                                wh, wl = w_high[:, t % SPLIT, k, :], w_low[:, t % SPLIT, k, :]
                                o = bank(2 * par + h)
                                if last and bias:
                                    for lhs, rhs, c0, c1 in bias(g, h):
                                        pe.matmul(psum[:, 2 * par + h, c0:c1], lhs, rhs, start=False, stop=False, skip_group_check=True)
                                skip = bool(bias)
                                pe.matmul(o, xh, wh, start=c == 0, stop=False, skip_group_check=skip)
                                pe.matmul(o, xh, wl, start=False, stop=False, skip_group_check=skip)
                                mm = pe.matmul(o, xl, wh, start=False, stop=last, skip_group_check=skip)
                        mm.then_inc(tile_used, 1)
                        at["tile"] += 1
                        if after and (g, kt) in after:
                            after[g, kt]()
                    at["prod"] += 1
                if name == "k":
                    at["k_done"] = at["prod"]

            def transposes(src, banks, tok=0):
                at["tok"] += tok
                if at["tok"]:
                    pe.wait_ge(tok_ready, at["tok"])
                for b in range(banks):
                    n = at["col"]
                    if n >= 2:
                        pe.wait_ge(cols_drained, n - 1)
                    for off, v in src(b):
                        rows_, cols_ = v.shape
                        mm = pe.transpose(psum[0:cols_, TR + n % 2, off:off + rows_], v, ident[0:rows_, 0:rows_])
                    mm.then_inc(cols_filled, 1)
                    at["col"] += 1

            def two_chunks(buf, c0=0):
                return lambda b: [(256 * e + P * h, buf[:, h, (c0 + 2 * b + e) * P:(c0 + 2 * b + e + 1) * P])
                                  for e in range(2) for h in range(HALVES)]

            def row_ready(name):
                n = row_at[name]
                pe.wait_ge(row_loaded[n % 2], 16 * (n // 2 + 1))

            def brow(name, lo, n):
                return row[0:1, row_at[name] % 2, lo:lo + n]

            def columns_of(buf, banks=4):
                ready = [at["col"] + 1 + b for b in range(banks)]
                transposes(two_chunks(buf), banks, HALVES)
                return ready

            def residual_product(name, high, low, buf, bias=None, ready=None, after=None):
                state_ = {}

                def part(g):
                    def run():
                        state_[g] = [at["col"] + 1, at["col"] + 2]
                        transposes(two_chunks(buf, 4 * g), 2, HALVES)
                    return run

                tile = 6 if plan[at["plan"]]["tiles"] == 8 else 2
                product(name, high, low, range(2), bias, ready, {**(after or {}), (1, tile): part(0)})
                later = [at["col"] + 1, at["col"] + 2]
                return state_[0] + later, {(0, 1): part(1)}

            def root_rows():
                pe.wait_ge(rstd_ready, at["norm"])
                n = at["col"]
                pe.wait_ge(cols_drained, n - 1)
                for h in range(HALVES):
                    mm = pe.transpose(psum[0:1, TR + n % 2, P * h:P * h + P], rms_col[:, h:h + 1], ident)
                mm.then_inc(cols_filled, 1)
                at["col"] += 1
                at["rms_row"] = at["col"]

            def conv_mixer(ready, after):
                mem_at = []

                def scales():
                    row_ready("b_a")
                    row_ready("b_gate")
                    at["norm"] = 2
                    root_rows()
                    pe.wait_ge(cols_drained, at["rms_row"])

                def parameters():
                    memory_columns()
                    mem_at.append(at["col"])
                    pe.wait_ge(mixer_in, 32)
                    transposes(lambda b: [(32 * e, dw_tok[:, (4 * b + e) * P:(4 * b + e + 1) * P]) for e in range(4)], 2)

                rms = lambda h: rms_row[0:1, h * P:(h + 1) * P]
                product("conv_in", xT_high, xT_low, range(4),
                        lambda g, h: [(rms(h), brow("b_a", 256 * g, 256), 0, 256), (rms(h), brow("b_gate", 256 * g, 256), 256, 512)],
                        ready, {(0, 2): scales, (1, 2): parameters})
                mem_ready = [mem_at[0]] * 4
                transposes(two_chunks(z_tok), 4, 1)
                pe.wait_ge(cols_drained, at["col"])
                pe.wait_ge(mixer_zero, 2)
                n = 0
                for c in range(CONV_DVE, KC):
                    j = c - CONV_DVE
                    for t in range(TAPS):
                        pe.wait_ge(tap_ready, n + 1)
                        mm = pe.matmul(psum[:, 6 + j // 2, T * (j % 2):T * (j % 2) + T], tap_diag[:, n % 4, :], zT[:, c, t:t + T],
                                       start=(t == 0), stop=(t == TAPS - 1))
                        mm.then_inc(tap_used, 1)
                        n += 1
                pe.wait_ge(tap_used, n)
                pe.sem_inc(conv_filled, 1)
                product("k", memT_high, memT_low, [0], ready=mem_ready)
                transposes(lambda b: [(P * e, conv[:, 4 * (b % 2) + e, (b // 2) * P:(b // 2 + 1) * P]) for e in range(4)], 4, 1)
                product("k", memT_high, memT_low, [1])
                pe.wait_ge(act_out, 9)
                ready = [at["col"] + 1 + b for b in range(4)]
                transposes(two_chunks(z_tok), 4)
                row_ready("conv_bo")
                return residual_product("conv_out", xT_high, xT_low, xn,
                                        lambda g, h: [(ones[0:1, :], brow("conv_bo", COLS * g, COLS), 0, COLS)], ready,
                                        {(0, 3): key_columns})

            def memory_columns():
                transposes(two_chunks(xn), 4, HALVES)

            def key_columns():
                pe.wait_ge(group_drained, at["k_done"])
                transposes(lambda b: [(256 * e + P * h, k_tok[:, b // 2, h, (2 * (b % 2) + e) * P:(2 * (b % 2) + e + 1) * P])
                                      for e in range(2) for h in range(HALVES)], 4)

            def sgu_mixer(ready, after):
                def scales():
                    at["norm"] = 8
                    root_rows()
                    pe.wait_ge(cols_drained, at["rms_row"])

                def parameters():
                    memory_columns()
                    pe.wait_ge(mixer_in, 16 * MIXER_LOADS[2])
                    transposes(lambda b: [(P * e, ws_in[:, 4 * b + e, :]) for e in range(4)] if b < 2 else [(0, bs_in[:, :])], 3)

                after = {**after, (0, 2): scales, (1, 2): parameters}
                def bias(g, h):
                    part = (g // 2 + 2) % 4
                    row_ready(f"sgu_bias{part}")
                    return [(rms_row[0:1, h * P:(h + 1) * P], brow(f"sgu_bias{part}", COLS * (g % 2), COLS), 0, COLS)]

                product("sgu_in", xT_high, xT_low, range(8), bias, ready, after)
                at["tok"] += 1
                pe.wait_ge(tok_ready, at["tok"])
                for h in range(HALVES):
                    for gp in range(4):
                        n = at["score"]
                        pe.wait_ge(scores_used, n - 1)
                        for e in range(2):
                            g = 2 * gp + e
                            mm = pe.matmul(psum[:, 6 + n % 2, 256 * e:256 * e + 256], wsT[:, g, :], g_tok[:, h, 256 * g:256 * g + 256],
                                           start=True, stop=True)
                        mm.then_inc(scores_filled, 1)
                        at["score"] += 1
                pe.wait_ge(scores_used, at["score"])
                ready = [at["col"] + 1 + b for b in range(8)]
                transposes(two_chunks(u_tok), 8)
                return residual_product("sgu_out", yT_high, sgu_low, xn, None, ready)

            def ret_mixer(ready, after):
                product("ret_in", xT_high, xT_low, range(12), None, ready, after)
                for j in range(2):
                    transposes(two_chunks(qk[j]), 4, 1 - j)
                pe.wait_ge(cols_drained, at["col"])
                for hd in range(XH):
                    n = at["score"]
                    pe.wait_ge(scores_used, n - 1)
                    for s_, t0, c0 in ((0, 0, 0), (1, P, 2 * P)):
                        for c in range(2):
                            mm = pe.matmul(psum[:, 6 + n % 2, c0:c0 + T - t0], qkT[1][:, 2 * hd + c, s_ * P:(s_ + 1) * P],
                                           qkT[0][:, 2 * hd + c, t0:T], start=(c == 0), stop=(c == 1))
                    mm.then_inc(scores_filled, 1)
                    at["score"] += 1
                decayed = at["score"]
                for h in range(HALVES):
                    for hd in range(XH):
                        n = at["score"]
                        pe.wait_ge(scores_used, n - 1 if h or hd > 1 else decayed)
                        v = [rv[:, s_, 512 * hd:512 * hd + 512] for s_ in range(2)]
                        if h == 0:
                            mm = pe.matmul(bank(6 + n % 2), sc[:, hd, 0:P], v[0], start=True, stop=True)
                        else:
                            pe.matmul(bank(6 + n % 2), sc[:, hd, P:2 * P], v[0], start=True, stop=False)
                            mm = pe.matmul(bank(6 + n % 2), sc[:, hd, 2 * P:3 * P], v[1], start=False, stop=True)
                        mm.then_inc(scores_filled, 1)
                        at["score"] += 1
                ready = [at["col"] + 1 + b for b in range(8)]
                transposes(two_chunks(o_tok), 8, 1)
                return residual_product("ret_out", yT_high, ret_low, xn, None, ready, {(0, 1): memory_columns})

            lanes = [0, 0]

            def lane_bank(j):
                n = lanes[j]
                if n >= 4:
                    pe.wait_ge(lane_used[j], n - 3)
                return 4 * j + n % 4

            def lane_done(j, mm):
                mm.then_inc(lane_filled[j], 1)
                lanes[j] += 1
                return lanes[j]

            def lane_ready(j, n):
                pe.wait_ge(lane_used[j], n)

            def rwkv_mixer(ready, after):
                transposes(two_chunks(xn), 4, HALVES)
                pe.wait_ge(mix_loaded, 16)
                transposes(lambda b: [(6 * e, mix_in[:, e * P:(e + 1) * P]) for e in range(KC)], 1)
                pe.wait_ge(group_drained, at["prod"])
                pe.wait_ge(cols_drained, at["col"])
                pe.wait_ge(scores_used, at["score"])
                pe.wait_ge(mixer_in, 16 * MIXER_LOADS[1])
                for j, (m, width) in enumerate(((1, 64), (4, 64), (5, P))):
                    at["tok"] += 1
                    pe.wait_ge(tok_ready, at["tok"])
                    src = (xs, xs_b, xs)[j]
                    hid = [(lora[j], 0, width)] + ([(lora[0], P, 32)] if j == 2 else [])
                    for buf, o, k in hid:
                        b = lane_bank(0)
                        for c in range(KC):
                            mm = pe.matmul(psum[0:k, b, 0:T], lora1[j][:, c, o:o + k], src[:, c, :], start=(c == 0), stop=(c == KC - 1))
                        ready = lane_done(0, mm)
                    lane_ready(0, ready)
                    for h in range(HALVES):
                        for n in range(2):
                            b = lane_bank(0)
                            cols = slice(COLS * n, COLS * n + COLS)
                            if j < 2:
                                mm = pe.matmul(bank(b), lora[j][0:65, h * P:(h + 1) * P], lora2[j][:, cols], start=True, stop=True)
                            else:
                                pe.matmul(bank(b), lora[2][:, h * P:(h + 1) * P], lora2[2][:, cols], start=True, stop=False)
                                mm = pe.matmul(bank(b), lora[0][0:32, h * P:(h + 1) * P], lora2[3][:, cols], start=False, stop=True)
                            lane_done(0, mm)
                lane_ready(0, lanes[0])

                def input_ready():
                    at["tok"] += 4
                    return [at["tok"] - 3 + c for c in range(4)]

                product("rkv", xT_high, xT_low, range(2), tok=input_ready())
                at["tok"] += 1
                lw_at = at["tok"]
                product("rkv", xT_high, xT_low, range(2), tok=input_ready())
                pe.wait_ge(tok_ready, lw_at)
                for h in range(HALVES):
                    for n in range(2):
                        b = lane_bank(1)
                        mm = pe.matmul(bank(b), masks[:, M_CUM, :], lw[:, h, COLS * n:COLS * n + COLS], start=True, stop=True)
                        lane_done(1, mm)
                product("rkv", xT_high, xT_low, range(2), tok=input_ready())
                pe.wait_ge(group_drained, at["prod"])
                b = lane_bank(0)
                for h in range(HALVES):
                    for n in range(NH // 2):
                        o = (h * NH // 2 + n) * 2
                        mm = pe.matmul(psum[:, b, o:o + 2], lw[:, h, P * n:P * n + P], masks[:, M_CHUNK, 0:2], start=True, stop=True)
                lane_done(0, mm)
                for _ in range(WARM):
                    pe.matmul(bank(1), ident, masks[:, 0:COLS // P, :].rearrange("p m c -> p (m c)"), start=True, stop=True)
                at["tok"] += 1
                pe.wait_ge(tok_ready, at["tok"])
                own = [slice(CH * c, CH * c + CH) for c in range(2)]

                def of_head(buf, n):
                    return buf[HD * (n % 2):HD * (n % 2) + HD, n // 2, :]

                def front(unit):
                    for src in (kk, ra, rk, rr):
                        b = lane_bank(0)
                        for e in range(4):
                            c0 = 512 * (unit % 2) + P * e
                            mm = pe.transpose(psum[:, b, P * e:P * e + P], src[:, unit // 2, c0:c0 + P], ident)
                        at["front"] = lane_done(0, mm)

                def score(sb, l, r):
                    b = lane_bank(1)
                    for e in range(4):
                        n = 2 * e + sb
                        mm = pe.matmul(psum[:, b, P * e:P * e + P], of_head(l, n), of_head(r, n), start=True, stop=True)
                    return lane_done(1, mm)

                def start_inverse(unit):
                    aT, bT = fronts[unit % 2][0:2]
                    lane_ready(0, at["front"])
                    for sb in range(2):
                        score(sb, bT, aT)
                        score(sb, aT, bT)

                def by_token(b, l, r, start=True, stop=True, skip=False):
                    for n in range(8):
                        mm = pe.matmul(psum[:, b, HD * n:HD * n + HD], l[:, n, :], r(n), start=start and (n == 0 or not skip), stop=stop,
                                       skip_group_check=skip)
                    return mm

                def y_after():
                    if at["y"]:
                        pe.wait_ge(y_part, at["y"])

                def y_done(mm):
                    mm.then_inc(y_part, 1)
                    at["y"] += 1

                at["y"] = 0
                front(0)
                start_inverse(0)
                for h in range(HALVES):
                    for hg in range(2):
                        unit = 2 * h + hg
                        aT, bT, kkT, rT = fronts[unit % 2]

                        def head(buf, n, rs=slice(0, P)):
                            return buf[rs, h, 512 * hg + HD * n:512 * hg + HD * n + HD]

                        def pairwise(sb, l, r):
                            b = lane_bank(1)
                            for e in range(4):
                                n = 2 * e + sb
                                mm = pe.matmul(psum[:, b, P * e:P * e + P], l[:, n, :], r[:, n, :], start=True, stop=True)
                            return lane_done(1, mm)

                        def turn(sb):
                            lane_ready(1, inv_at[sb])
                            b = lane_bank(0)
                            for e in range(4):
                                mm = pe.transpose(psum[:, b, P * e:P * e + P], inv[:, 2 * e + sb, :], ident)
                            turn_at[sb] = lane_done(0, mm)

                        at["tok"] += 2
                        pe.wait_ge(tok_ready, at["tok"])
                        inv_at, turn_at = [lanes[1]] * 2, [0, 0]
                        for level in range(1, LEVELS):
                            q_at = []
                            for sb in range(2):
                                lane_ready(1, inv_at[sb])
                                q_at.append(pairwise(sb, abT, inv))
                                if level > 1:
                                    turn(sb)
                            if level < 3:
                                for sb in range(2):
                                    s_at = score(sb, *((kkT, aT), (bT, rT))[level - 1])
                                if level == 1:
                                    ak_at = s_at
                            if level == 4:
                                lane_ready(1, ak_at)
                                h_at = lane_done(0, by_token(lane_bank(0), akT, lambda n: head(rvv, n)))
                            for sb in range(2):
                                lane_ready(1, q_at[sb])
                                if turn_at[sb]:
                                    lane_ready(0, turn_at[sb])
                                inv_at[sb] = pairwise(sb, invT, lvl)
                        for sb in range(2):
                            turn(sb)
                            score(sb, kkT, rT)
                        lane_ready(0, turn_at[1])
                        b = lane_bank(0)
                        for n in range(8):
                            o = HD * (n % 2)
                            mm = pe.matmul(psum[o:o + HD, b, P * (n // 2):P * (n // 2) + P], head(kk, n), invT[:, n, :], start=True, stop=True)
                        w_at = lane_done(0, mm)
                        if unit < 3:
                            front(unit + 1)
                        lane_ready(0, h_at)
                        lane_done(0, by_token(lane_bank(0), invT, lambda n: hh[:, n, :]))
                        lane_ready(0, w_at)
                        lane_ready(1, lanes[1])
                        yb = lane_bank(0)
                        y_after()
                        y_done(by_token(yb, rkT, lambda n: head(rvv, n), stop=False, skip=True))
                        for c in range(2):
                            rs = own[c]
                            for sb in range(2):
                                heads_ = [(n, state[HD * sb:HD * sb + HD, 4 * hg + n // 2, :]) for n in range(sb, 8, 2)]
                                b = lane_bank(1)
                                for n, st in heads_:
                                    mm = pe.matmul(psum[rs, b, HD * (n // 2):HD * (n // 2) + HD], of_head(wT, n)[:, rs], st, start=True, stop=True)
                                u_at = lane_done(1, mm)
                                y_after()
                                for n, st in heads_:
                                    mm = pe.matmul(psum[rs, yb, HD * n:HD * n + HD], of_head(rT, n)[:, rs], st, start=False, stop=False,
                                                   skip_group_check=True)
                                y_done(mm)
                            b = lane_bank(1)
                            for n in range(8):
                                o = HD * (n % 2)
                                pe.matmul(psum[o:o + HD, b, HD * (n // 2):HD * (n // 2) + HD], head(rk, n, rs), head(rvv, n, rs),
                                          start=(n < 2), stop=False, skip_group_check=True)
                            lane_ready(1, u_at)
                            for n in range(8):
                                o = HD * (n % 2)
                                mm = pe.matmul(psum[o:o + HD, b, HD * (n // 2):HD * (n // 2) + HD], head(ra, n, rs), uu[rs, n, :],
                                               start=False, stop=(n >= 6), skip_group_check=True)
                            s_at = lane_done(1, mm)
                            if c == 0:
                                if unit < 3:
                                    start_inverse(unit + 1)
                                lane_ready(1, s_at)
                        y_after()
                        lane_done(0, by_token(yb, rbT, lambda n: uu[:, n, :], start=False, skip=True))
                lane_ready(1, lanes[1])
                ready = [at["col"] + 1 + b for b in range(4)]
                transposes(two_chunks(rr), 2, 1)
                transposes(two_chunks(rr, 4), 2, 1)
                return residual_product("rwkv_out", xT_high, xT_low, xn, None, ready, {(0, 1): memory_columns})

            pe.wait_ge(const_loaded, 16)
            pe.wait_ge(mixer_zero, 1)
            ready, after = columns_of(xg), {}
            for i in range(layers):
                mixer = [conv_mixer, rwkv_mixer, sgu_mixer, ret_mixer][i]
                ready, after = mixer(ready, after)
                if i:
                    product("k", memT_high, memT_low, range(2), after=after)
                    key_columns()
                    after = {}
                product("q", xT_high, xT_low, range(2), None, ready, after)
                pe.wait_ge(group_drained, at["prod"])
                transposes(two_chunks(q_tok), 4)
                product("v", memT_high, memT_low, [0])
                pe.wait_ge(cols_drained, at["col"])
                for h in range(HALVES):
                    for hp in range(XH // 2):
                        n = at["score"]
                        if n >= 2:
                            pe.wait_ge(scores_used, n - 1)
                        for e in range(2):
                            hd = 2 * hp + e
                            for c in range(2):
                                mm = pe.matmul(psum[:, 6 + n % 2, e * T:(e + 1) * T], qT[:, 2 * hd + c, h * P:(h + 1) * P],
                                               kT[:, 2 * hd + c, :], start=(c == 0), stop=(c == 1))
                        mm.then_inc(scores_filled, 1)
                        at["score"] += 1
                product("v", memT_high, memT_low, [1])
                transposes(lambda b: [(256 * m + P * h, prob[:, h, b, m * P:(m + 1) * P]) for m in range(2) for h in range(HALVES)],
                           4, HALVES * XH)
                pe.wait_ge(group_drained, at["prod"])
                prob_at = at["col"] - 3
                ready = []
                for hd in range(XH):
                    n = at["score"]
                    pe.wait_ge(cols_drained, prob_at + hd)
                    pe.wait_ge(scores_used, n - 1)
                    for e in range(2):
                        c = 2 * hd + e
                        for m in range(2):
                            mm = pe.matmul(psum[:, 6 + n % 2, e * T:(e + 1) * T], v_tok[:, m, c * P:(c + 1) * P],
                                           probT[:, hd, m, :], start=(m == 0), stop=(m == 1))
                    mm.then_inc(scores_filled, 1)
                    at["score"] += 1
                pe.wait_ge(scores_used, at["score"])
                ready, after = residual_product("wo", xT_high, xT_low, xg)
                for g in range(11):
                    product("gate_up", xT_high, xT_low, [g], None, ready if g == 0 else None, after if g == 0 else None)
                    if g:
                        pe.wait_ge(group_drained, at["prod"] - 1)
                        transposes(lambda b: [(256 * e + P * h, htok[:, (g - 1) % 2, h, e * P:(e + 1) * P])
                                              for e in range(2) for h in range(HALVES)], 1)
                pe.wait_ge(group_drained, at["prod"])
                transposes(lambda b: [(256 * e + P * h, htok[:, 0, h, e * P:(e + 1) * P])
                                      for e in range(2) for h in range(HALVES)], 1)
                ready = [at["col"]] * 11
                ready[0:10] = [at["col"] - 1] * 10
                if i + 1 < layers and i != 0:
                    ready, after = residual_product("down", hT_high, hT_low, xg, None, ready)
                else:
                    product("down", hT_high, hT_low, range(2), None, ready)


def kernel(**inputs):
    import concourse.bacc as _bacc
    from concourse import mybir as _mybir
    from concourse.bass_utils import run_bass_kernel_spmd as _run

    arrays = {f"in_{name}": np.ascontiguousarray(a) for name, a in inputs.items()}
    arrays["in_masks"] = constant_masks()
    arrays["in_rotary"] = rotary_tables()
    arrays["in_decay"] = decay_masks()
    nc = _bacc.Bacc("TRN2", target_bir_lowering=False, num_devices=1)
    w = {name[3:]: nc.dram_tensor(name, a.shape, _mybir.dt.from_np(a.dtype), kind="ExternalInput").ap()
         for name, a in arrays.items()}
    out = nc.dram_tensor("out", (1, T, D), _mybir.dt.float32, kind="ExternalOutput").ap()
    trunk_program(nc, w, out, 4)
    return _run(nc, [arrays], core_ids=[0]).results[0]["out"]
```
